# Optimizing a Trainium2 kernel written in Bass

```python
import jax, jax.numpy as jnp
from jax import lax
import numpy as np

D_MODEL = 1024
BATCH = 1
SEQ = 256
DEPTH = 2

CHUNK = 64
MIX_WIDTH = D_MODEL
N_MIXERS = 4
GROUP_WIDTH = MIX_WIDTH // N_MIXERS
POOL_WINDOWS = (2, 4, 8, 16)
POOL_GROUP = GROUP_WIDTH // len(POOL_WINDOWS)
SGU_HEADS = 4
SGU_BLOCK = 128
SGU_HEAD_DIM = GROUP_WIDTH // SGU_HEADS
LRU_BLOCKS = 4
LRU_BLOCK_DIM = GROUP_WIDTH // LRU_BLOCKS
CONV_WIDTH = 4
LRU_C = 8.0
HGRN_HEADS = 4
HGRN_HEAD_DIM = GROUP_WIDTH // HGRN_HEADS
N_IN_SLICES = 9
IN_WIDTH = N_IN_SLICES * GROUP_WIDTH
D_FF = 7 * D_MODEL // 2
N_EXPERTS = 8
TOP_K = 2
N_DENSE = (DEPTH + 1) // 2
N_MOE = DEPTH // 2
EPS = 1e-6
MIN_FORGET = 1e-30

kernel_name = 'hybrid_stream_block'

def rms_norm(x, g):
    xf = x.astype(jnp.float32)
    y = xf * lax.rsqrt(jnp.mean(xf * xf, axis=-1, keepdims=True) + EPS)
    return (y * g.astype(jnp.float32)).astype(x.dtype)

def modulate(h, shift, scale):
    return h * (1.0 + scale[:, None, :]) + shift[:, None, :]

def swiglu(h, w1, w3, w2):
    return (jax.nn.silu(h @ w1) * (h @ w3)) @ w2

def pool_mixer(x, w, scale):
    bsz, slen, _ = x.shape
    xf = x.astype(jnp.float32)
    cs = jnp.pad(jnp.cumsum(xf, axis=1), ((0, 0), (1, 0), (0, 0)))
    pos = jnp.arange(1, slen + 1, dtype=jnp.float32)[None, :, None]
    means = []
    for gi, win in enumerate(POOL_WINDOWS):
        csg = cs[..., gi * POOL_GROUP:(gi + 1) * POOL_GROUP]
        lo = jnp.pad(csg, ((0, 0), (win - 1, 0), (0, 0)))[:, :slen]
        means.append((csg[:, 1:] - lo) / jnp.minimum(pos, float(win)))
    d = (jnp.concatenate(means, axis=-1) - xf).reshape(bsz, slen, len(POOL_WINDOWS), POOL_GROUP)
    y = jnp.einsum('bsgi,gij->bsgj', d, w.astype(jnp.float32)).reshape(bsz, slen, GROUP_WIDTH)
    return (y * scale.astype(jnp.float32)).astype(x.dtype)

def sgu_mixer(u, v, ws, bias):
    bsz, slen, _ = u.shape
    u = jax.nn.gelu(u)
    vf = jax.nn.gelu(v).astype(jnp.float32)
    mu = jnp.mean(vf, axis=-1, keepdims=True)
    var = jnp.mean(jnp.square(vf - mu), axis=-1, keepdims=True)
    vn = ((vf - mu) * lax.rsqrt(var + EPS)).astype(u.dtype)
    vb = vn.reshape(bsz, slen // SGU_BLOCK, SGU_BLOCK, SGU_HEADS, SGU_HEAD_DIM)
    tri = jnp.tril(jnp.ones((SGU_BLOCK, SGU_BLOCK), dtype=ws.dtype))
    z = jnp.einsum('hts,bnshd->bnthd', ws * tri, vb) + bias.T[None, None, :, :, None]
    return u * z.reshape(bsz, slen, GROUP_WIDTH)

def _linear_combine(left, right):
    a1, b1 = left
    a2, b2 = right
    return a1 * a2, a2 * b1 + b2

def lru_mixer(xb, gate, conv_w, conv_b, wa, ba, wx, bx, lam):
    bsz, slen, _ = xb.shape
    xp = jnp.pad(xb, ((0, 0), (CONV_WIDTH - 1, 0), (0, 0)))
    xc = conv_b + sum(conv_w[k] * xp[:, k:k + slen] for k in range(CONV_WIDTH))
    xh = xc.reshape(bsz, slen, LRU_BLOCKS, LRU_BLOCK_DIM)
    r = jax.nn.sigmoid(jnp.einsum('bshi,hij->bshj', xh, wa).reshape(bsz, slen, GROUP_WIDTH) + ba)
    i = jax.nn.sigmoid(jnp.einsum('bshi,hij->bshj', xh, wx).reshape(bsz, slen, GROUP_WIDTH) + bx)
    log_a = LRU_C * r.astype(jnp.float32) * jax.nn.log_sigmoid(lam.astype(jnp.float32))
    a = jnp.exp(log_a)
    b = jnp.sqrt(jnp.maximum(-jnp.expm1(2.0 * log_a), 0.0)) * (i * xc).astype(jnp.float32)
    _, h = lax.associative_scan(_linear_combine, (a, b), axis=1)
    return jax.nn.gelu(gate) * h.astype(xb.dtype)

def hgrn_mixer(q, fz, inp, g, lb, norm_g):
    bsz, slen, _ = q.shape
    n_chunks = slen // CHUNK
    lb = lb.astype(jnp.float32)
    z = fz.astype(jnp.float32)
    qf = jax.nn.silu(q.astype(jnp.float32))
    sig = jax.nn.sigmoid(z)
    f = lb + (1.0 - lb) * sig
    log_f = jnp.log(jnp.maximum(f, MIN_FORGET))
    k = (1.0 - lb) * (1.0 - sig)
    v = inp.astype(jnp.float32)

    def to_chunks(t):
        return t.reshape(bsz, n_chunks, CHUNK, HGRN_HEADS, HGRN_HEAD_DIM).transpose(1, 0, 3, 2, 4)

    causal = jnp.tril(jnp.ones((CHUNK, CHUNK), dtype=bool))[:, :, None]
    causal_f = causal.astype(jnp.float32)

    def step(state, xs):
        qc, kc, vc, gc = xs
        b = jnp.cumsum(gc, axis=2)
        o_inter = jnp.einsum('bhtk,bhkv->bhtv', qc * jnp.exp(b), state)
        diff = b[:, :, :, None, :] - b[:, :, None, :, :]
        decay = jnp.exp(jnp.where(causal, diff, 0.0)) * causal_f
        scores = jnp.einsum('bhtk,bhtsk,bhsk->bhts', qc, decay, kc)
        o = o_inter + jnp.einsum('bhts,bhsv->bhtv', scores, vc)
        b_last = b[:, :, -1:, :]
        state = (jnp.exp(b_last[:, :, 0, :])[..., None] * state
                 + jnp.einsum('bhsk,bhsv->bhkv', kc * jnp.exp(b_last - b), vc))
        return state, o

    s0 = jnp.zeros((bsz, HGRN_HEADS, HGRN_HEAD_DIM, HGRN_HEAD_DIM), jnp.float32)
    _, o = lax.scan(step, s0, (to_chunks(qf), to_chunks(k), to_chunks(v), to_chunks(log_f)))
    o = o.transpose(1, 0, 3, 2, 4).reshape(bsz, slen, HGRN_HEADS, HGRN_HEAD_DIM)
    o = o * lax.rsqrt(jnp.mean(o * o, axis=-1, keepdims=True) + EPS)
    o = o * norm_g.astype(jnp.float32).reshape(HGRN_HEADS, HGRN_HEAD_DIM)
    return (o.reshape(bsz, slen, GROUP_WIDTH) * jax.nn.silu(g.astype(jnp.float32))).astype(q.dtype)

def moe_ffn(h, router_w, router_b, w1, w3, w2):
    logits = h.astype(jnp.float32) @ router_w.astype(jnp.float32) + router_b.astype(jnp.float32)
    top_v, top_i = lax.top_k(logits, TOP_K)
    top_w = jax.nn.softmax(top_v, axis=-1)
    combine = jnp.sum(jax.nn.one_hot(top_i, N_EXPERTS, dtype=jnp.float32) * top_w[..., None], axis=-2)
    combine = combine.astype(h.dtype)
    y = jnp.zeros_like(h)
    for e in range(N_EXPERTS):
        y = y + combine[..., e:e + 1] * swiglu(h, w1[e], w3[e], w2[e])
    return y

def setup_inputs(seed: int = 0) -> dict:
    key = jax.random.key(seed)
    ks = jax.random.split(key, 40)
    counter = [0]

    def nxt():
        k = ks[counter[0]]
        counter[0] += 1
        return k

    def nrm(shape, scale):
        return scale * jax.random.normal(nxt(), shape, jnp.float32)

    def gain(shape):
        return 1.0 + nrm(shape, 0.02)

    G = GROUP_WIDTH
    gate_pattern = jnp.repeat(jnp.array([0.0, 0.0, 1.0, 0.0, 0.0, 1.0], jnp.float32), D_MODEL)
    a0 = jax.random.uniform(nxt(), (DEPTH, G), jnp.float32, 0.9, 0.999)
    p = a0 ** (1.0 / LRU_C)
    lam = jnp.log(p) - jnp.log1p(-p)
    return {
        'x': nrm((BATCH, SEQ, D_MODEL), 1.0),
        'c': nrm((BATCH, D_MODEL), 1.0),
        'w_mod': nrm((DEPTH, D_MODEL, 6 * D_MODEL), 0.2 * D_MODEL ** -0.5),
        'b_mod': gate_pattern + nrm((DEPTH, 6 * D_MODEL), 0.02),
        'norm_mix': gain((DEPTH, D_MODEL)),
        'norm_ffn': gain((DEPTH, D_MODEL)),
        'norm_final': gain((D_MODEL,)),
        'w_in': nrm((DEPTH, D_MODEL, IN_WIDTH), D_MODEL ** -0.5),
        'w_out': nrm((DEPTH, MIX_WIDTH, D_MODEL), MIX_WIDTH ** -0.5),
        'pool_w': nrm((DEPTH, len(POOL_WINDOWS), POOL_GROUP, POOL_GROUP), POOL_GROUP ** -0.5),
        'pool_scale': 1.0 + nrm((DEPTH, G), 0.05),
        'pool_out_norm': gain((DEPTH, G)),
        'sgu_ws': nrm((DEPTH, SGU_HEADS, SGU_BLOCK, SGU_BLOCK), 0.5 * SGU_BLOCK ** -0.5),
        'sgu_b': 1.0 + nrm((DEPTH, SGU_HEADS, SGU_BLOCK), 0.02),
        'sgu_out_norm': gain((DEPTH, G)),
        'conv_w': nrm((DEPTH, CONV_WIDTH, G), CONV_WIDTH ** -0.5),
        'conv_b': nrm((DEPTH, G), 0.02),
        'lru_wa': nrm((DEPTH, LRU_BLOCKS, LRU_BLOCK_DIM, LRU_BLOCK_DIM), LRU_BLOCK_DIM ** -0.5),
        'lru_ba': nrm((DEPTH, G), 0.02),
        'lru_wx': nrm((DEPTH, LRU_BLOCKS, LRU_BLOCK_DIM, LRU_BLOCK_DIM), LRU_BLOCK_DIM ** -0.5),
        'lru_bx': nrm((DEPTH, G), 0.02),
        'lru_lambda': lam,
        'lru_out_norm': gain((DEPTH, G)),
        'hgrn_gamma': nrm((DEPTH, G), 0.5),
        'hgrn_out_norm': gain((DEPTH, G)),
        'ffn_w1': nrm((N_DENSE, D_MODEL, D_FF), D_MODEL ** -0.5),
        'ffn_w3': nrm((N_DENSE, D_MODEL, D_FF), D_MODEL ** -0.5),
        'ffn_w2': nrm((N_DENSE, D_FF, D_MODEL), D_FF ** -0.5),
        'router_w': nrm((N_MOE, D_MODEL, N_EXPERTS), D_MODEL ** -0.5),
        'router_b': nrm((N_MOE, N_EXPERTS), 0.01),
        'moe_w1': nrm((N_MOE, N_EXPERTS, D_MODEL, D_FF), D_MODEL ** -0.5),
        'moe_w3': nrm((N_MOE, N_EXPERTS, D_MODEL, D_FF), D_MODEL ** -0.5),
        'moe_w2': nrm((N_MOE, N_EXPERTS, D_FF, D_MODEL), D_FF ** -0.5),
    }

def reference(x, c, w_mod, b_mod, norm_mix, norm_ffn, norm_final, w_in, w_out,
              pool_w, pool_scale, pool_out_norm, sgu_ws, sgu_b, sgu_out_norm,
              conv_w, conv_b, lru_wa, lru_ba, lru_wx, lru_bx, lru_lambda, lru_out_norm,
              hgrn_gamma, hgrn_out_norm, ffn_w1, ffn_w3, ffn_w2,
              router_w, router_b, moe_w1, moe_w3, moe_w2):
    p_layers = jax.nn.softmax(hgrn_gamma.astype(jnp.float32), axis=0)
    lower_bounds = jnp.cumsum(p_layers, axis=0) - p_layers[0:1]
    c_act = jax.nn.silu(c)
    for l in range(DEPTH):
        mod = c_act @ w_mod[l] + b_mod[l]
        sh1, sc1, g1, sh2, sc2, g2 = jnp.split(mod, 6, axis=-1)
        h = modulate(rms_norm(x, norm_mix[l]), sh1, sc1)
        proj = h @ w_in[l]
        pa, pu, pv, px, pg, dq, dfz, di, dg = jnp.split(proj, N_IN_SLICES, axis=-1)
        ya = rms_norm(pool_mixer(pa, pool_w[l], pool_scale[l]), pool_out_norm[l])
        yb = rms_norm(sgu_mixer(pu, pv, sgu_ws[l], sgu_b[l]), sgu_out_norm[l])
        yc = rms_norm(lru_mixer(px, pg, conv_w[l], conv_b[l], lru_wa[l], lru_ba[l],
                                lru_wx[l], lru_bx[l], lru_lambda[l]), lru_out_norm[l])
        yd = hgrn_mixer(dq, dfz, di, dg, lower_bounds[l], hgrn_out_norm[l])
        y = jnp.concatenate([ya, yb, yc, yd], axis=-1) @ w_out[l]
        x = x + g1[:, None, :] * y
        h = modulate(rms_norm(x, norm_ffn[l]), sh2, sc2)
        if l % 2 == 0:
            f = swiglu(h, ffn_w1[l // 2], ffn_w3[l // 2], ffn_w2[l // 2])
        else:
            f = moe_ffn(h, router_w[l // 2], router_b[l // 2], moe_w1[l // 2], moe_w3[l // 2], moe_w2[l // 2])
        x = x + g2[:, None, :] * f
    return rms_norm(x, norm_final)


_drawn_inputs = setup_inputs


def setup_inputs(seed=0):
    import zlib

    import numpy as np

    out = dict(_drawn_inputs(seed))
    spreads = {}
    factors = {'norm_final': 23.158,
     'pool_out_norm': 23.123,
     'sgu_b': 37.796,
     'sgu_out_norm': 21.561,
     'lru_ba': 42.479,
     'lru_bx': 24.996,
     'lru_out_norm': 20.044,
     'hgrn_gamma': 3.915,
     'hgrn_out_norm': 38.296,
     'router_b': 25.599,
     'norm_ffn': 8.0,
     'pool_scale': 3.036}
    for name, (base, spread) in spreads.items():
        noise = np.random.default_rng([zlib.crc32(name.encode()), seed]).standard_normal(out[name].shape)
        drawn = base * np.exp(spread * noise) if base else spread * noise
        out[name] = __import__('jax').numpy.asarray(drawn.astype(out[name].dtype))
    for name, factor in factors.items():
        out[name] = (out[name] * factor).astype(out[name].dtype)
    return out
```

```python
from contextlib import ExitStack

import concourse.bass as bass
from concourse import mybir

P = 128
D = 1024
KB = D // P
T = 256
TT = T // P
DEPTH = 2
G = 256
CB = G // P
HD = 64
NH = G // HD
WINDOWS = (2, 4, 8, 16)
CONV = 4
LRU_C = 8.0
DFF = 7 * D // 2
W = 512
NJ = DFF // W
HB = W // P
NE = 8
SLOTS = P
EPS = 1e-6
MIN_FORGET = 1e-30
C = 16
NC = T // C
CT_ = P // C
RING = 6
EDGE = P + 16
LN_FLOOR = 2.0 ** -60

F32 = mybir.dt.float32
I32 = mybir.dt.int32
ALU = mybir.AluOpType
ACT = mybir.ActivationFunctionType
X = mybir.AxisListType.X

ROWS = {}
_at = 0
for _name, _n in (("norm_mix", KB), ("norm_ffn", KB), ("pool_scale", CB), ("pool_out", CB), ("sgu_out", CB),
                  ("conv_w", CONV * CB), ("conv_b", CB), ("lru_ba", CB), ("lru_bx", CB), ("lambda", CB),
                  ("lru_out", CB), ("hgrn_out", CB), ("gamma", DEPTH * CB), ("c", KB),
                  ("b_sh1", KB), ("b_sc1", KB), ("b_sh2", KB), ("b_sc2", KB)):
    ROWS[_name] = (_at, _n)
    _at += _n
NROWS = _at

COLS = {n: i * G for i, n in enumerate(("pa", "pu", "pv", "px", "pg", "dq", "dfz", "di", "dg"))}
GROUPS = ("dfz", "di", "dq", "px", "pg", "pv", "dg", "pu", "pa")
WIN_ORDER = (3, 2, 1, 4, 0)
MOD_PARTS = ("sh1", "sc1", "sh2", "sc2", "g1", "g2")
MOD_COL = {"sh1": 0, "sc1": 1, "g1": 2, "sh2": 3, "sc2": 4, "g2": 5}
FFN_ORDER = ([("w1", 0), ("w3", 0)]
             + [x for j in range(1, NJ) for x in (("w1", j), ("w3", j), ("w2", j - 1))] + [("w2", NJ - 1)])
NCH = len(FFN_ORDER)
PAIR = 2
assert PAIR * NCH % RING == 0 and NE % PAIR == 0


class Steps:

    def __init__(self, sem, names):
        self.sem, self.names = sem, names
        self.count = 0
        self.index = {n: i + 1 for i, n in enumerate(names)}

    def at(self, name, rep=0):
        return rep * len(self.names) + self.index[name]

    def said(self, name):
        assert self.names[self.count % len(self.names)] == name, (self.names[self.count % len(self.names)], name)
        self.count += 1



N_ROW_LOADS = 25
N_CONSTS = 81
CHAIN = CB * (NC - 1)

STEPS = {
    "pre_v":
        ("params neg abs min gm gd0 gd1 gs gr p0 p1 c1 lb0 lb1 lbo lbn ls lk0 lk1").split(),
    "pre_a":
        ("c gexp lexp lln").split(),
    "pre_t":
        ("rows").split(),
    "mod_v":
        ("c0k0 c0k1 c0k2 c0k3 c0k4 c0k5 c0k6 c0k7 c1k0 c1k1 c1k2 c1k3 c1k4 c1k5 c1k6 c1k7").split(),
    "mod_t":
        ("sum").split(),
    "mod_e":
        ("add fin").split(),
    "gate_t":
        ("sum").split(),
    "gate_v":
        ("g0 g1").split(),
    "norm_v":
        ("rc xn0 xn1 h2 h3 h6 h7").split(),
    "norm_a":
        ("sq0 sq1 rt h0 h1 h4 h5").split(),
    "norm_t":
        ("t0 t1 t2 t3").split(),
    "mix_v":
        ("wst f0 f1 k0 k1 fa fb kc lf b0 b1 bk kd v vx0 vx1 vx2 vx3 vx4 vx5 vx6 vx7 cv00 cv01 cv02 xc0 "
         "cv10 cv11 cv12 xc1 qt a2 m m0 ix bb hs0 hs1 yc_raw sf0 sf1 mu vc0 vc1 rvr vn0 vn1 yb_raw rec_d "
         "od yd0 yd1 rec_c yc0 yc1 rec_b yb0 yb1 rec_a ya0 ya1").split(),
    "mix_a":
        ("sig lna lnb lnk eb ea kh q kt xp gate_c gv0 gv1 r0 r1 i0 i1 a0 a1 th0 th1 sm gate_d sqc sv0 sv1 "
         "rv gu pa sqd rtd rtc pd sqb rtb ps0 ps1 sqa rta").split(),
    "mix_t":
        ("ws dfz di dq kt px u0 u1 u2 u3 u4 u5 u6 u7 pg pv wa wx sc0 dg pu pa sc1 o z ssd ssc aband ssb "
         "apool ssa wout0 wout1 wout2 wout3").split(),
    "tri_d":
        ("d").split(),
    "tri_e":
        ("e").split(),
    "tri_q":
        ("q").split(),
    "chain_v":
        ("s").split(),
    "res_v":
        ("r0 r1 r2 r3 r4 r5 r6 r7").split(),
    "ffn_v":
        ("a0 a1").split(),
    "ffn_a":
        ("s0 s1").split(),
    "ffn_t":
        ("h1_0 h3_0 h1_1 h3_1").split(),
    "ffn_w":
        ("w").split(),
    "route_v":
        ("lg max0 eq0 cand0 first0 pick0 lg2 max1 eq1 cand1 first1 pick1 sel diff one w1 w2 sw1 sw2 wt pos "
         "most most_i idle").split(),
    "route_a":
        ("exp").split(),
    "route_t":
        ("logits pos").split(),
    "slot_v":
        ("pos d0_0 d0_1 wd0_0 wd0_1 d1_0 d1_1 wd1_0 wd1_1 d2_0 d2_1 wd2_0 wd2_1 d3_0 d3_1 wd3_0 wd3_1 d4_0 "
         "d4_1 wd4_0 wd4_1 d5_0 d5_1 wd5_0 wd5_1 d6_0 d6_1 wd6_0 wd6_1 d7_0 d7_1 wd7_0 wd7_1").split(),
    "slot_a":
        ("sp0 sp1 sp2 sp3 sp4 sp5 sp6 sp7").split(),
    "slot_t":
        ("g0 g1 tr0 tr1 tr2 tr3 tr4 tr5 tr6 tr7").split(),
    "moe_v":
        ("spread m0 m1 m2 m3 m4 m5 m6 y1").split(),
    "moe_a":
        ("s0 s1 at0 s2 at1 s3 at2 s4 at3 s5 at4 s6 at5 at6 y0").split(),
    "moe_t":
        ("h1_0 h3_0 h1_1 t0 h3_1 w_0 h1_2 t1 h3_2 w_1 h1_3 t2 h3_3 w_2 h1_4 t3 h3_4 w_3 h1_5 t4 h3_5 w_4 "
         "h1_6 t5 h3_6 w_5 t6 ga w_6 gb c0 c1 c2 c3").split(),
    "fill_v":
        ("x4 x5 x6 x7").split(),
    "fill_a":
        ("x0 x1 x2 x3").split(),
    "sum_v":
        ("a0 a1 a2 a3").split(),
    "end_v":
        ("rc out0 out1").split(),
    "end_a":
        ("sq0 sq1 rt").split(),
}


def hybrid_stream_block(nc, a, out):
    ctx = ExitStack()
    with ctx:
        def sb(name, shape, dt=F32):
            return ctx.enter_context(nc.sbuf_tensor(name, shape, dt))

        def sem(name):
            return ctx.enter_context(nc.semaphore(name))

        ring = sb("ring", [P, RING, KB * W])
        x = sb("x", [P, TT, D])
        xn = sb("xn", [P, TT, D])
        y_t = xn[:, :, :].rearrange("p t (b c) -> p (t b) c", c=T)
        h_t = sb("h_t", [P, KB, T])
        mod_acc = sb("mod_acc", [P, 2, D])
        mod_tmp = sb("mod_tmp", [P, KB])
        mod_col = sb("mod_col", [P, DEPTH * 4, KB])
        gate_row = sb("gate_row", [P, D])
        consts = sb("consts", [P, 7, P])
        ident, ones, head_ones, triu, lower, before, iota_f = (consts[:, i, :] for i in range(7))
        band_a = sb("band_a", [P, NH, EDGE])
        band_b = sb("band_b", [P, NH, P])
        scan_keep = sb("scan_keep", [P, T])
        chunk_of = sb("chunk_of", [P, CT_])
        head_sel = sb("head_sel", [P, 2])
        row_sel = sb("row_sel", [NH, CB, P])
        eps_col = sb("eps_col", [P, 1])
        params = sb("params", [P, DEPTH, NROWS])
        c_act = sb("c_act", [P, KB])
        lru_k = sb("lru_k", [P, DEPTH, 2, CB])
        floor_col = sb("floor_col", [P, DEPTH, 3, CB])
        small = sb("small", [P, 16, 8])
        blocks = sb("blocks", [P, 3, CB, P])
        ws_t = sb("ws_t", [P, NH, P])
        sgu_bias = sb("sgu_bias", [NH, P])
        x_pad = sb("x_pad", [P, CB, CONV - 1 + T])
        norm_s = sb("norm_s", [P, 4, TT])
        low = ExitStack()
        tmp = low.enter_context(nc.sbuf_tensor("tmp", [P, 14, G * CB], F32))
        v_wide = low.enter_context(nc.sbuf_tensor("v_wide", [P, 2, W], F32))
        tri = low.enter_context(nc.sbuf_tensor("tri", [P, C, NC, C], F32))
        state = low.enter_context(nc.sbuf_tensor("state", [P, CB, NC, HD], F32))
        s_full = v_wide[:, :, :].rearrange("p t (h n) -> p t h n", h=NH)
        prow = tmp[0:NROWS, 0, 0:DEPTH * P].rearrange("p (l n) -> p l n", l=DEPTH)
        low.close()
        moe_mem = ExitStack()

        def mb(name, shape, dt=F32):
            return moe_mem.enter_context(nc.sbuf_tensor(name, shape, dt))

        dispatch = mb("dispatch", [P, TT, NE + 1, SLOTS])
        spread = mb("spread", [P, NE, T])
        spread_e = mb("spread_e", [P, T])
        x_slots = mb("x_slots", [P, 2, KB, SLOTS])
        moe_sum = mb("moe_sum", [P, TT, D])
        act_s = mb("act_s", [P, 2, W])
        act_m = mb("act_m", [P, 2, W])
        act_t = mb("act_t", [P, 2, W])
        y_slots = mb("y_slots", [P, D])
        route = mb("route", [P, 14, TT, NE])
        route_c = mb("route_c", [P, 6, TT, 1])
        picked = mb("picked", [P, TT, SLOTS])
        router = mb("router", [P, KB, NE])
        router_bias = mb("router_bias", [1, NE])
        most = mb("most", [P, 4])
        most_i = mb("most_i", [P, 1], I32)
        moe_mem.close()
        bank = [ctx.enter_context(nc.psum_tensor(f"bank{i}", [P, W], F32)) for i in range(8)]

        landed = [sem(f"landed_{i}") for i in range(RING)]
        s_x = sem("x_loaded")
        s_rows = sem("rows_loaded")
        s_blk = sem("blocks_loaded")
        s_ws = sem("ws_loaded")
        s_gate = sem("gate_bias_loaded")
        s_router = sem("router_loaded")
        s_const = sem("constants_made")
        s_out = sem("out_stored")

        def steps(name):
            return Steps(sem(name), STEPS[name])

        pre_v, pre_a, pre_t = steps("pre_v"), steps("pre_a"), steps("pre_t")
        mod_v, mod_t, mod_e = steps("mod_v"), steps("mod_t"), steps("mod_e")
        gate_t, gate_v = steps("gate_t"), steps("gate_v")
        norm_v, norm_a, norm_t = steps("norm_v"), steps("norm_a"), steps("norm_t")
        mix_v, mix_a, mix_t = steps("mix_v"), steps("mix_a"), steps("mix_t")
        tri_d, tri_e, tri_q = steps("tri_d"), steps("tri_e"), steps("tri_q")
        chain_v = steps("chain_v")
        res_v = steps("res_v")
        ffn_v, ffn_a, ffn_t, ffn_w = steps("ffn_v"), steps("ffn_a"), steps("ffn_t"), steps("ffn_w")
        route_v, route_a, route_t = steps("route_v"), steps("route_a"), steps("route_t")
        slot_v, slot_a, slot_t = steps("slot_v"), steps("slot_a"), steps("slot_t")
        moe_v, moe_a, moe_t = steps("moe_v"), steps("moe_a"), steps("moe_t")
        fill_v, fill_a, sum_v = steps("fill_v"), steps("fill_a"), steps("sum_v")
        end_v, end_a = steps("end_v"), steps("end_a")

        def done(eng, ins, s, name, rep=0):
            s.said(name)
            eng.wait_ge(s.sem, s.at(name, rep))

        def mark(ins, s, name):
            s.said(name)

        def par(name, l, i=0, n=1):
            r = ROWS[name][0] + i
            return params[:, l, r:r + n]

        def mod_src(l, part, half):
            col = MOD_COL[part] * D + half * W
            return a["w_mod"][l].rearrange("(k p) n -> p k n", p=P)[:, :, col:col + W]

        def win_src(l, c):
            return a["w_in"][l].rearrange("(k p) n -> p k n", p=P)[:, :, c * W:min((c + 1) * W, 9 * G)]

        def wout_src(l, half):
            return a["w_out"][l].rearrange("(k p) n -> p k n", p=P)[:, :, half * W:(half + 1) * W]

        def ffn_src(kind, j):
            if kind == "w2":
                return a["ffn_w2"][0].rearrange("(b p) n -> p b n", p=P)[:, j * W // P:(j + 1) * W // P, :]
            return a[f"ffn_{kind}"][0].rearrange("(k p) n -> p k n", p=P)[:, :, j * W:(j + 1) * W]

        chunks = []

        def mod_chunks(l, part):
            for half in range(2):
                chunks.append((("mod", l, part, half), mod_src(l, part, half),
                               (mod_v, f"c{half}k{KB - 1}", 6 * l + MOD_PARTS.index(part))))

        def win_chunks(l):
            last = {3: "di", 2: "pg", 1: "pv", 4: "dg", 0: "pa"}
            for c in WIN_ORDER:
                chunks.append((("win", l, c), win_src(l, c), (mix_t, last[c], l)))

        def wout_chunks(l):
            for half in range(2):
                chunks.append((("wout", l, half), wout_src(l, half), (mix_t, "wout3", l)))

        mod_chunks(0, "sh1")
        mod_chunks(0, "sc1")
        win_chunks(0)
        mod_chunks(0, "sh2")
        mod_chunks(0, "sc2")
        wout_chunks(0)
        mod_chunks(0, "g1")
        mod_chunks(0, "g2")
        freed = {"w1": (ffn_t, "h1_1"), "w3": (ffn_t, "h3_1"), "w2": (ffn_w, "w")}
        mods = list(MOD_PARTS)
        for kind, j in FFN_ORDER:
            chunks.append((("ffn", kind, j), ffn_src(kind, j), (*freed[kind], j)))
            if kind == "w3" and mods:
                mod_chunks(1, mods.pop(0))
        win_chunks(1)
        wout_chunks(1)
        NPRE = len(chunks)
        number = {key: n for n, (key, _, _) in enumerate(chunks)}

        def slot(n):
            return ring[:, n % RING, :]

        def wide(key):
            cols = 9 * G - 4 * W if key[0] == "win" and key[2] == 4 else W
            return slot(number[key])[:, 0:KB * cols].rearrange("p (k n) -> p k n", n=cols)

        def arrived(eng, key):
            n = number[key]
            eng.wait_ge(landed[n % RING], 16 * (n // RING + 1))

        def moe_slot(u, i):
            return slot(NPRE + u * NCH + i)

        def moe_arrived(eng, q, g, u, i):
            n = NPRE + u * NCH + i
            turns = PAIR * NCH // RING
            eng.wait_ge(landed[n % RING], ((n // RING + 1) + turns * (q * (NE // PAIR) + g)) * 16)

        def expert(q, g, u):
            return q * NE + g * PAIR + u

        block = ctx.enter_context(nc.Block())

        @block.sync
        def _(eng):
            for n, (key, src, _) in enumerate(chunks):
                if n >= RING:
                    s, name, rep = chunks[n - RING][2]
                    eng.wait_ge(s.sem, s.at(name, rep))
                if key[0] == "ffn" and key[1] == "w2":
                    dst = slot(n).rearrange("p (b n) -> p b n", n=D)
                else:
                    dst = wide(key)
                eng.dma_start(dst, src).then_inc(landed[n % RING], 16)

            moe_freed = {"w1": "h1_", "w3": "h3_", "w2": "w_"}

            def load_expert(q, g, u, i, g_src):
                n = u * NCH + i - RING
                if n >= 0:
                    kind, j = FFN_ORDER[n % NCH]
                    eng.wait_ge(moe_t.sem, moe_t.at(f"{moe_freed[kind]}{j}", expert(q, g, n // NCH)))
                elif q == 0 and g_src is None:
                    s, name, rep = chunks[NPRE + n][2]
                    eng.wait_ge(s.sem, s.at(name, rep))
                else:
                    kind, j = FFN_ORDER[NCH + n]
                    eng.wait_ge(moe_t.sem, moe_t.at(f"{moe_freed[kind]}{j}", expert(q, g - 1, PAIR - 1)))
                kind, j = FFN_ORDER[i]
                w = a[f"moe_{kind}"][0]
                e = 0 if g_src is None else g_src * PAIR
                we = w[bass.ds(e + u, 1)] if g_src is not None else w[u:u + 1]
                if kind == "w2":
                    src = we.rearrange("e (b p) n -> (e p) b n", p=P)[:, j * W // P:(j + 1) * W // P, :]
                    dst = moe_slot(u, i).rearrange("p (b n) -> p b n", n=D)
                else:
                    src = we.rearrange("e (k p) n -> (e p) k n", p=P)[:, :, j * W:(j + 1) * W]
                    dst = moe_slot(u, i).rearrange("p (k n) -> p k n", n=W)
                eng.dma_start(dst, src).then_inc(landed[(NPRE + u * NCH + i) % RING], 16)

            def load_pass(q):
                for i in range(RING):
                    load_expert(q, 0, 0, i, None)
                with eng.Fori(0, NE // PAIR - 1) as g:
                    for c in range(RING, PAIR * NCH):
                        load_expert(q, g, c // NCH, c % NCH, g)
                    for i in range(RING):
                        load_expert(q, g + 1, 0, i, g + 1)
                last = NE // PAIR - 1
                for c in range(RING, PAIR * NCH):
                    load_expert(q, last, c // NCH, c % NCH, last)

            load_pass(0)
            eng.wait_ge(route_v.sem, route_v.at("most_i"))
            with eng.If(eng.value_load(most_i[0:1, 0:1], min_val=0, max_val=T) > SLOTS):
                load_pass(1)
            for tt in range(TT):
                eng.wait_ge(end_v.sem, end_v.at(f"out{tt}"))
                eng.dma_start(out[0, tt * P:(tt + 1) * P, :], xn[:, tt, :]).then_inc(s_out, 16)
            eng.wait_ge(s_out, 16 * TT)

        @block.gpsimd
        def _(eng):
            eng.dma_start(x[:, :, :], a["x"][0].rearrange("(t p) d -> p t d", p=P)).then_inc(s_x, 16)
            per_l = (("norm_mix", a["norm_mix"]), ("norm_ffn", a["norm_ffn"]), ("pool_scale", a["pool_scale"]),
                     ("pool_out", a["pool_out_norm"]), ("sgu_out", a["sgu_out_norm"]), ("conv_b", a["conv_b"]),
                     ("lru_ba", a["lru_ba"]), ("lru_bx", a["lru_bx"]), ("lambda", a["lru_lambda"]),
                     ("lru_out", a["lru_out_norm"]), ("hgrn_out", a["hgrn_out_norm"]))
            n = 0
            for name, src in per_l:
                r, k = ROWS[name]
                eng.dma_start(prow[r:r + k, :, :], src.rearrange("l (r p) -> r l p", p=P)).then_inc(s_rows, 16)
                n += 1
            for l in range(DEPTH):
                r, k = ROWS["conv_w"]
                eng.dma_start(prow[r:r + k, l, :], a["conv_w"][l].rearrange("k (r p) -> (k r) p", p=P))\
                   .then_inc(s_rows, 16)
                r, k = ROWS["gamma"]
                eng.dma_start(prow[r:r + k, l, :], a["hgrn_gamma"].rearrange("l (r p) -> (l r) p", p=P))\
                   .then_inc(s_rows, 16)
                r, k = ROWS["c"]
                eng.dma_start(prow[r:r + k, l, :], a["c"].rearrange("o (r p) -> (o r) p", p=P)).then_inc(s_rows, 16)
                for part in ("sh1", "sc1", "sh2", "sc2"):
                    r, k = ROWS["b_" + part]
                    col = MOD_COL[part] * D
                    eng.dma_start(prow[r:r + k, l, :], a["b_mod"][l, col:col + D].rearrange("(r p) -> r p", p=P))\
                       .then_inc(s_rows, 16)
                    n += 1
                n += 3
            assert n == N_ROW_LOADS

            consts_made = 0

            def made(ins):
                nonlocal consts_made
                consts_made += 1
                ins.then_inc(s_const, 1)
                eng.wait_ge(s_const, consts_made)

            made(eng.memset(consts[:, :, :], 1.0))
            made(eng.affine_select(out=ident, in_=ident, compare_op=ALU.is_equal, fill=0.0, base=0,
                                   pattern=[[-1, P]], channel_multiplier=1))
            made(eng.affine_select(out=triu, in_=triu, compare_op=ALU.is_ge, fill=0.0, base=0,
                                   pattern=[[1, P]], channel_multiplier=-1))
            made(eng.affine_select(out=before, in_=before, compare_op=ALU.is_ge, fill=0.0, base=-1,
                                   pattern=[[1, P]], channel_multiplier=-1))
            made(eng.affine_select(out=head_ones[:, 0:HD], in_=head_ones[:, 0:HD], compare_op=ALU.is_ge, fill=0.0,
                                   base=HD - 1, pattern=[[0, HD]], channel_multiplier=-1))
            made(eng.affine_select(out=head_ones[:, HD:P], in_=head_ones[:, HD:P], compare_op=ALU.is_ge, fill=0.0,
                                   base=-HD, pattern=[[0, HD]], channel_multiplier=1))
            made(eng.iota(iota_f, [[1, P]], base=0, channel_multiplier=0, allow_small_or_imprecise_dtypes=True))
            made(eng.tensor_copy(head_sel[:, 0:1], head_ones[:, 0:1]))
            made(eng.tensor_copy(head_sel[:, 1:2], head_ones[:, HD:HD + 1]))
            made(eng.memset(eps_col[:, :], EPS))
            made(eng.memset(scan_keep[:, :], 1.0))
            made(eng.memset(scan_keep[:, 0:T:C], 0.0))
            made(eng.memset(chunk_of[:, :], 1.0))
            made(eng.affine_select(out=chunk_of[:, :], in_=chunk_of[:, :], compare_op=ALU.is_ge, fill=0.0, base=0,
                                   pattern=[[-C, CT_]], channel_multiplier=1))
            made(eng.affine_select(out=chunk_of[:, :], in_=chunk_of[:, :], compare_op=ALU.is_ge, fill=0.0,
                                   base=C - 1, pattern=[[C, CT_]], channel_multiplier=-1))
            made(eng.memset(row_sel[:, :, :], 1.0))
            made(eng.affine_select(out=row_sel[:, :, :], in_=row_sel[:, :, :], compare_op=ALU.is_ge, fill=0.0,
                                   base=HD - 1, pattern=[[-P, CB], [-1, P]], channel_multiplier=HD))
            made(eng.affine_select(out=row_sel[:, :, :], in_=row_sel[:, :, :], compare_op=ALU.is_ge, fill=0.0,
                                   base=0, pattern=[[P, CB], [1, P]], channel_multiplier=-HD))
            made(eng.memset(x_pad[:, :, :], 0.0))
            made(eng.memset(blocks[:, :, :, :], 0.0))
            made(eng.memset(tri[:, :, :, :], 0.0))
            made(eng.memset(state[:, :, 0, :], 0.0))
            pos = band_b[:, 0, 0:1]
            made(eng.memset(band_a[:, :, :], 1.0))
            for g, win in enumerate(WINDOWS):
                made(eng.memset(band_a[:, g, :], 1.0 / win))
                for t in range(win - 1):
                    made(eng.memset(band_a[:, g, t:t + 1], 1.0 / (t + 1)))
                made(eng.memset(band_b[:, g, :], 1.0 / win))
                for m, n in ((band_a[:, g, :], EDGE), (band_b[:, g, :], P)):
                    made(eng.affine_select(out=m, in_=m, compare_op=ALU.is_ge, fill=0.0, base=0,
                                           pattern=[[1, n]], channel_multiplier=-1))
                    made(eng.affine_select(out=m, in_=m, compare_op=ALU.is_ge, fill=0.0, base=win - 1,
                                           pattern=[[-1, n]], channel_multiplier=1))
                    made(eng.tensor_tensor(m[:, 0:P], m[:, 0:P], ident, ALU.subtract))
            assert consts_made == N_CONSTS

            for l in range(DEPTH):
                if l:
                    eng.wait_ge(mix_t.sem, mix_t.at("apool", l - 1))
                for k, w in enumerate((a["pool_w"], a["lru_wa"], a["lru_wx"])):
                    for q in range(2):
                        eng.dma_start(blocks[q * HD:(q + 1) * HD, k, :, q * HD:(q + 1) * HD],
                                      w[l].rearrange("(b q) i j -> q i b j", q=2)[q]).then_inc(s_blk, 16)
                if l:
                    eng.wait_ge(res_v.sem, res_v.at("r7", 2 * l - 1))
                    eng.wait_ge(mix_v.sem, mix_v.at("yd1", l - 1))
                else:
                    eng.wait_ge(pre_t.sem, pre_t.at("rows"))
                eng.dma_start(tmp[:, 13, :].rearrange("p (h s) -> p h s", h=NH),
                              a["sgu_ws"][l].rearrange("h t s -> t h s")).then_inc(s_ws, 16)
                eng.dma_start(sgu_bias[:, :], a["sgu_b"][l]).then_inc(s_ws, 16)
                eng.dma_start(gate_row[:, :], a["b_mod"][l:l + 1, 2 * D:3 * D].to_broadcast([P, D]))\
                   .then_inc(s_gate, 16)
                eng.wait_ge(res_v.sem, res_v.at("r7", 2 * l))
                eng.dma_start(gate_row[:, :], a["b_mod"][l:l + 1, 5 * D:6 * D].to_broadcast([P, D]))\
                   .then_inc(s_gate, 16)
            eng.dma_start(router[:, :, :], a["router_w"][0].rearrange("(k p) e -> p k e", p=P)).then_inc(s_router, 16)
            eng.dma_start(router_bias[:, :], a["router_b"][0:1, :]).then_inc(s_router, 16)
            eng.wait_ge(res_v.sem, res_v.at("r7", 2 * DEPTH - 1))
            eng.dma_start(gate_row[:, :], a["norm_final"].rearrange("(o d) -> o d", o=1).to_broadcast([P, D]))\
               .then_inc(s_gate, 16)

        @block.tensor
        def _(eng):
            mm = nc.tensor.matmul

            def row_sum_columns(l, part):
                n = MOD_PARTS.index(part)
                eng.wait_ge(mod_v.sem, mod_v.at(f"c1k{KB - 1}", 6 * l + n))
                b = bank[6] if l == 0 and n >= 2 else bank[0]
                if 4 * l + n > 0:
                    eng.wait_ge(mod_e.sem, mod_e.at("fin", 4 * l + n - 1))
                if l == 1:
                    eng.wait_ge(ffn_a.sem, ffn_a.at("s0", n + 1))
                for k in range(KB):
                    ins = mm(b[:, k:k + 1], mod_acc[:, n % 2, k * P:(k + 1) * P], ones[:, 0:1], start=True, stop=True)
                mark(ins.then_inc(mod_t.sem, 1), mod_t, "sum")

            def row_sum_wide(l, which, b):
                n = 4 + which
                eng.wait_ge(mod_v.sem, mod_v.at(f"c1k{KB - 1}", 6 * l + n))
                for half in range(2):
                    ins = mm(b[half][:, :], ones, mod_acc[:, n % 2, half * W:(half + 1) * W], start=True, stop=True)
                mark(ins.then_inc(gate_t.sem, 1), gate_t, "sum")

            def turn_xn(q):
                eng.wait_ge(norm_v.sem, norm_v.at("xn1", q))
                for b in range(4):
                    for i in range(2):
                        for tt in range(TT):
                            ins = nc.tensor.transpose(bank[4 + b][:, i * T + tt * P:i * T + (tt + 1) * P],
                                                      xn[:, tt, (2 * b + i) * P:(2 * b + i + 1) * P], ident)
                    mark(ins.then_inc(norm_t.sem, 1), norm_t, f"t{b}")

            def mixers(l):
                eng.wait_ge(s_ws, 32 * (l + 1))
                for h in range(NH):
                    ins = nc.tensor.transpose(bank[3][:, h * P:(h + 1) * P], tmp[:, 13, h * P:(h + 1) * P], ident)
                mark(ins.then_inc(mix_t.sem, 1), mix_t, "ws")

                free = {"px": (mix_a, "sig"), "pg": (mix_v, "v"), "pv": (mix_a, "q"), "dg": (mix_a, "xp"),
                        "pu": (mix_a, "gate_c"), "pa": (mix_a, "gv1")}

                def project(name):
                    b = bank[GROUPS.index(name) % 3]
                    c, off = COLS[name] // W, COLS[name] % W
                    arrived(eng, ("win", l, c))
                    if name in free:
                        s, reader = free[name]
                        eng.wait_ge(s.sem, s.at(reader, l))
                    w = wide(("win", l, c))
                    for i in range(2):
                        for k in range(KB):
                            if name in ("di", "pv", "pa"):
                                ins = mm(b[:, i * G:(i + 1) * G], h_t[:, k, i * P:(i + 1) * P], w[:, k, off:off + G],
                                         start=k == 0, stop=k == KB - 1)
                            else:
                                ins = mm(b[:, i * T:(i + 1) * T], w[:, k, off + i * P:off + (i + 1) * P], h_t[:, k, :],
                                         start=k == 0, stop=k == KB - 1)
                    mark(ins.then_inc(mix_t.sem, 1), mix_t, name)

                def channel_sum(b, src, name):
                    for i in range(CB):
                        ins = mm(b[:, 0:T], ones, src[:, i * T:(i + 1) * T], start=i == 0, stop=i == CB - 1)
                    mark(ins.then_inc(mix_t.sem, 1), mix_t, name)

                eng.wait_ge(norm_a.sem, norm_a.at("h5", 2 * l))
                eng.wait_ge(norm_v.sem, norm_v.at("h7", 2 * l))
                project("dfz")
                project("di")
                project("dq")
                eng.wait_ge(mix_a.sem, mix_a.at("kh", l))
                for tt in range(TT):
                    for i in range(CB):
                        ins = nc.tensor.transpose(bank[4][:, tt * G + i * P:tt * G + (i + 1) * P],
                                                  tmp[:, 4, i * T + tt * P:i * T + (tt + 1) * P], ident)
                mark(ins.then_inc(mix_t.sem, 1), mix_t, "kt")
                project("px")
                eng.wait_ge(mix_a.sem, mix_a.at("kt", l))
                for n, (i, tt, q) in enumerate((i, tt, q) for i in range(CB) for tt in range(TT) for q in range(2)):
                    h = 2 * i + q
                    eng.wait_ge(mix_v.sem, mix_v.at(f"vx{n}", l))
                    b = bank[6 + tt] if i == 0 else bank[4 + tt]
                    ins = mm(b[q * HD:(q + 1) * HD, :], tmp[:, 5, tt * G + h * HD:tt * G + (h + 1) * HD],
                             v_wide[:, n % 2, :], start=True, stop=True)
                    mark(ins.then_inc(mix_t.sem, 1), mix_t, f"u{n}")
                project("pg")
                project("pv")
                eng.wait_ge(mix_v.sem, mix_v.at("xc1", l))
                eng.wait_ge(s_blk, 96 * (l + 1))
                eng.wait_ge(chain_v.sem, chain_v.at("s", l * CHAIN + CHAIN - 1))
                for k, name in ((1, "wa"), (2, "wx")):
                    for i in range(CB):
                        ins = mm(bank[3 + k][:, i * T:(i + 1) * T], blocks[:, k, i, :], tmp[:, 7, i * T:(i + 1) * T],
                                 start=True, stop=True)
                    mark(ins.then_inc(mix_t.sem, 1), mix_t, name)
                def scores(i):
                    for r in range(C):
                        eng.wait_ge(tri_q.sem, tri_q.at("q", (l * CB + i) * C + r))
                        for tt in range(TT):
                            c0 = (tt * CB + i) * 2 * C
                            ins = mm(bank[6][:, c0 + r:c0 + 2 * C:C],
                                     tri[:, r, tt * CT_:(tt + 1) * CT_, :].rearrange("p i s -> p (i s)"),
                                     head_sel[:, :], start=True, stop=True)
                    mark(ins.then_inc(mix_t.sem, 1), mix_t, f"sc{i}")

                scores(0)
                project("dg")
                project("pu")
                project("pa")
                scores(1)
                eng.wait_ge(mix_v.sem, mix_v.at("wst", l))
                for tt in range(TT):
                    eng.wait_ge(mix_v.sem, mix_v.at(f"sf{tt}", l))
                    for h in range(NH):
                        q, i = h % 2, h // 2
                        mm(bank[3][q * HD:(q + 1) * HD, i * T + tt * P:i * T + (tt + 1) * P],
                           tmp[:, 6, tt * G + h * HD:tt * G + (h + 1) * HD], s_full[:, tt, h, :],
                           start=tt == 0 and i == 0, stop=False, skip_group_check=True)
                eng.wait_ge(mix_v.sem, mix_v.at("qt", l))
                for h in range(NH):
                    q, i = h % 2, h // 2
                    for c in range(1, NC):
                        ins = mm(bank[3][q * HD:(q + 1) * HD, i * T + c * C:i * T + (c + 1) * C],
                                 state[q * HD:(q + 1) * HD, i, c, :],
                                 tmp[q * HD:(q + 1) * HD, 3, i * T + c * C:i * T + (c + 1) * C],
                                 start=False, stop=h >= 2 and c == NC - 1, skip_group_check=True)
                mark(ins.then_inc(mix_t.sem, 1), mix_t, "o")
                eng.wait_ge(mix_v.sem, mix_v.at("vn1", l))
                eng.wait_ge(mix_v.sem, mix_v.at("wst", l))
                eng.wait_ge(mix_a.sem, mix_a.at("r1", l))
                for tt in range(TT):
                    for i in range(CB):
                        mm(bank[4][:, i * T + tt * P:i * T + (tt + 1) * P], row_sel[:, i, :], sgu_bias[:, :],
                           start=tt == 0 and i == 0, stop=False, skip_group_check=True)
                for tt in range(TT):
                    for h in range(NH):
                        q, i = h % 2, h // 2
                        ins = mm(bank[4][q * HD:(q + 1) * HD, i * T + tt * P:i * T + (tt + 1) * P],
                                 tmp[:, 4, tt * G + h * HD:tt * G + (h + 1) * HD], ws_t[:, h, :],
                                 start=False, stop=True, skip_group_check=True)
                mark(ins.then_inc(mix_t.sem, 1), mix_t, "z")
                eng.wait_ge(mix_a.sem, mix_a.at("sqd", l))
                eng.wait_ge(chain_v.sem, chain_v.at("s", l * CHAIN + CHAIN - 1))
                mark(mm(bank[7][:, :], head_ones, tmp[:, 2, :], start=True, stop=True).then_inc(mix_t.sem, 1),
                     mix_t, "ssd")
                eng.wait_ge(mix_a.sem, mix_a.at("sqc", l))
                eng.wait_ge(mix_a.sem, mix_a.at("i1", l))
                channel_sum(bank[5], tmp[:, 8, :], "ssc")
                eng.wait_ge(mix_a.sem, mix_a.at("pa", l))
                eng.wait_ge(mix_v.sem, mix_v.at("sf1", l))
                for g in range(NH):
                    q, i = g % 2, g // 2
                    mm(bank[6][q * HD:(q + 1) * HD, i * T:i * T + EDGE], tmp[:, 11, g * HD:(g + 1) * HD],
                       band_a[:, g, :], start=i == 0, stop=False, skip_group_check=True)
                    ins = mm(bank[6][q * HD:(q + 1) * HD, i * T + P:(i + 1) * T],
                             tmp[:, 11, G + g * HD:G + (g + 1) * HD], band_b[:, g, :],
                             start=False, stop=True, skip_group_check=True)
                mark(ins.then_inc(mix_t.sem, 1), mix_t, "aband")
                eng.wait_ge(mix_a.sem, mix_a.at("sqb", l))
                eng.wait_ge(mix_a.sem, mix_a.at("rtd", l))
                channel_sum(bank[7], tmp[:, 4, :], "ssb")
                eng.wait_ge(mix_a.sem, mix_a.at("pd", l))
                eng.wait_ge(mix_v.sem, mix_v.at("yb_raw", l))
                for i in range(CB):
                    ins = mm(bank[4][:, i * T:(i + 1) * T], blocks[:, 0, i, :], tmp[:, 6, i * T:(i + 1) * T],
                             start=True, stop=True)
                mark(ins.then_inc(mix_t.sem, 1), mix_t, "apool")
                eng.wait_ge(mix_a.sem, mix_a.at("sqa", l))
                eng.wait_ge(mix_a.sem, mix_a.at("rtc", l))
                channel_sum(bank[5], tmp[:, 1, :], "ssa")
                for half in range(2):
                    arrived(eng, ("wout", l, half))
                for name in ("gate_d", "gu", "pa"):
                    eng.wait_ge(mix_a.sem, mix_a.at(name, l))
                eng.wait_ge(mix_v.sem, mix_v.at("od", l))
                for n, (name, g) in enumerate((("yc1", 2), ("yd1", 3), ("yb1", 1), ("ya1", 0))):
                    eng.wait_ge(mix_v.sem, mix_v.at(name, l))
                    for tt in range(TT):
                        for half in range(2):
                            for i in range(2 * g, 2 * g + 2):
                                ins = mm(bank[2 * tt + half][:, :], y_t[:, i, tt * P:(tt + 1) * P],
                                         wide(("wout", l, half))[:, i, :], start=n == 0 and i == 2 * g,
                                         stop=n == 3 and i == 2 * g + 1)
                            if n == 3:
                                mark(ins.then_inc(mix_t.sem, 1), mix_t, f"wout{2 * tt + half}")
                if l == 0:
                    row_sum_columns(0, "sh2")
                    row_sum_columns(0, "sc2")
                eng.wait_ge(mix_v.sem, mix_v.at("ya1", l))
                row_sum_wide(l, 0, (bank[5], bank[7]))

            def ffn():
                for j in range(NJ + 1):
                    if j < NJ:
                        for i in range(2):
                            for name, b, (s, ev) in (("w1", bank[i], (ffn_a, f"s{i}")),
                                                     ("w3", bank[2 + i], (ffn_v, f"a{i}"))):
                                arrived(eng, ("ffn", name, j))
                                if j:
                                    eng.wait_ge(s.sem, s.at(ev, j - 1))
                                if name == "w1" and i == 0 and 2 <= j:
                                    if j - 2 < 4:
                                        eng.wait_ge(mod_e.sem, mod_e.at("fin", 4 + j - 2))
                                w = wide(("ffn", name, j))
                                for hb in range(2):
                                    for k in range(KB):
                                        c = (2 * i + hb) * P
                                        ins = mm(b[:, hb * T:(hb + 1) * T], w[:, k, c:c + P], h_t[:, k, :],
                                                 start=k == 0, stop=k == KB - 1)
                                mark(ins.then_inc(ffn_t.sem, 1), ffn_t, f"h{name[1]}_{i}")
                        if 1 <= j <= 4:
                            row_sum_columns(1, MOD_PARTS[j - 1])
                    if j:
                        jj = j - 1
                        arrived(eng, ("ffn", "w2", jj))
                        eng.wait_ge(ffn_v.sem, ffn_v.at("a1", jj))
                        w = slot(number[("ffn", "w2", jj)]).rearrange("p (b n) -> p b n", n=D)
                        at = tmp[:, 2 + 2 * (jj % 2):4 + 2 * (jj % 2), :].rearrange("p a (b t) -> p (a b) t", t=T)
                        for tt in range(TT):
                            for half in range(2):
                                for hb in range(W // P):
                                    ins = mm(bank[4 + 2 * tt + half][:, :], at[:, hb, tt * P:(tt + 1) * P],
                                             w[:, hb, half * W:(half + 1) * W], start=jj == 0 and hb == 0,
                                             stop=jj == NJ - 1 and hb == W // P - 1)
                        mark(ins.then_inc(ffn_w.sem, 1), ffn_w, "w")

            def routing():
                eng.wait_ge(s_router, 32)
                for tt in range(TT):
                    for k in range(KB):
                        mm(bank[2][:, tt * NE:(tt + 1) * NE], h_t[:, k, tt * P:(tt + 1) * P], router[:, k, :],
                           start=k == 0, stop=False)
                    ins = mm(bank[2][:, tt * NE:(tt + 1) * NE], ones[0:1, :], router_bias[:, :], start=False, stop=True)
                mark(ins.then_inc(route_t.sem, 1), route_t, "logits")
                eng.wait_ge(route_v.sem, route_v.at("sel", 0))
                mm(bank[2][:, 64:64 + NE], before, route[:, 8, 0, :], start=True, stop=True)
                mm(bank[2][:, 64 + NE:64 + 2 * NE], ones, route[:, 8, 0, :], start=True, stop=False)
                mm(bank[2][:, 64 + NE:64 + 2 * NE], before, route[:, 8, 1, :], start=False, stop=True)
                mm(bank[2][:, 64 + 2 * NE:64 + 3 * NE], ones, route[:, 8, 0, :], start=True, stop=False)
                ins = mm(bank[2][:, 64 + 2 * NE:64 + 3 * NE], ones, route[:, 8, 1, :], start=False, stop=True)
                mark(ins.then_inc(route_t.sem, 1), route_t, "pos")

            def gather(b, e, first, name, s):
                for k in range(4):
                    for tt in range(TT):
                        ins = mm(b[:, k * P:(k + 1) * P], xn[:, tt, (first + k) * P:(first + k + 1) * P],
                                 dispatch[:, tt, e, :] if isinstance(e, int)
                                 else dispatch[:, tt, bass.ds(e, 1), :].rearrange("p o n -> p (o n)"),
                                 start=tt == 0, stop=tt == TT - 1)
                mark(ins.then_inc(s.sem, 1), s, name)

            def experts(q):
                eng.wait_ge(slot_v.sem, slot_v.at("d0_1", q))
                eng.wait_ge(gate_v.sem, gate_v.at("g1", 2 * DEPTH - 1))
                gather(bank[4], 0, 0, "g0", slot_t)
                gather(bank[5], 0, 4, "g1", slot_t)
                for e in range(NE):
                    eng.wait_ge(slot_v.sem, slot_v.at(f"wd{e}_1", q))
                    if e >= 2:
                        eng.wait_ge(slot_a.sem, slot_a.at(f"sp{e - 2}", q))
                    for tt in range(TT):
                        ins = nc.tensor.transpose(bank[e % 2][:, tt * P:(tt + 1) * P], act_m_pick(e, tt), ident)
                    mark(ins.then_inc(slot_t.sem, 1), slot_t, f"tr{e}")
                eng.wait_ge(slot_a.sem, slot_a.at(f"sp{NE - 1}", q))
                with eng.Fori(0, NE // PAIR) as g:
                    for u in range(PAIR):
                        one_expert(q, g, u)

            def act_m_pick(e, tt):
                return act_t[:, e % 2, tt * P:(tt + 1) * P]

            def one_expert(q, g, u):
                r = expert(q, g, u)
                xs = x_slots[:, u % 2, :, :]
                fill = q * (NE + 1) + g * PAIR + u

                def up(j, name, b):
                    i = FFN_ORDER.index((name, j))
                    moe_arrived(eng, q, g, u, i)
                    w = moe_slot(u, i).rearrange("p (k n) -> p k n", n=W)
                    for k in range(KB):
                        ins = mm(b[:, :], xs[:, k, :], w[:, k, :], start=k == 0, stop=k == KB - 1)
                    mark(ins.then_inc(moe_t.sem, 1), moe_t, f"h{name[1]}_{j}")

                def turn(j):
                    eng.wait_ge(moe_v.sem, moe_v.at(f"m{j}", r))
                    if j == 0:
                        eng.wait_ge(sum_v.sem, sum_v.at("a2", r))
                    for hb in range(W // P):
                        ins = nc.tensor.transpose(bank[6][:, hb * P:(hb + 1) * P],
                                                  act_m[:, j % 2, hb * P:(hb + 1) * P], ident)
                    mark(ins.then_inc(moe_t.sem, 1), moe_t, f"t{j}")

                def down(j):
                    i = FFN_ORDER.index(("w2", j))
                    moe_arrived(eng, q, g, u, i)
                    eng.wait_ge(moe_a.sem, moe_a.at(f"at{j}", r))
                    w = moe_slot(u, i).rearrange("p (b n) -> p b n", n=D)
                    for half in range(2):
                        for hb in range(W // P):
                            ins = mm(bank[4 + half][:, :], act_t[:, j % 2, hb * P:(hb + 1) * P],
                                     w[:, hb, half * W:(half + 1) * W], start=j == 0 and hb == 0,
                                     stop=j == NJ - 1 and hb == W // P - 1)
                    mark(ins.then_inc(moe_t.sem, 1), moe_t, f"w_{j}")

                for j in range(NJ):
                    if j == 0:
                        eng.wait_ge(fill_a.sem, fill_a.at("x3", fill))
                        eng.wait_ge(fill_v.sem, fill_v.at("x7", fill))
                    if j == 1:
                        eng.wait_ge(sum_v.sem, sum_v.at("a1", r))
                    if j >= 2:
                        eng.wait_ge(moe_a.sem, moe_a.at(f"s{j - 2}", r))
                    up(j, "w1", bank[j % 2])
                    if j:
                        turn(j - 1)
                    if j >= 2:
                        eng.wait_ge(moe_v.sem, moe_v.at(f"m{j - 2}", r))
                    up(j, "w3", bank[2 + j % 2])
                    if j:
                        down(j - 1)
                turn(NJ - 1)
                eng.wait_ge(sum_v.sem, sum_v.at("a3", r))
                gather(bank[7], g * PAIR + u + 1, 0, "ga", moe_t)
                down(NJ - 1)
                eng.wait_ge(fill_a.sem, fill_a.at("x3", fill + 1))
                gather(bank[7], g * PAIR + u + 1, 4, "gb", moe_t)
                eng.wait_ge(moe_v.sem, moe_v.at("spread", r))
                eng.wait_ge(moe_a.sem, moe_a.at("y0", r))
                eng.wait_ge(moe_v.sem, moe_v.at("y1", r))
                for n, b in enumerate((1, 3, 6, 7)):
                    tt, half = n // 2, n % 2
                    if b == 7:
                        eng.wait_ge(fill_v.sem, fill_v.at("x7", fill + 1))
                    mark(mm(bank[b][:, :], spread_e[:, tt * P:(tt + 1) * P], y_slots[:, half * W:(half + 1) * W],
                            start=True, stop=True).then_inc(moe_t.sem, 1), moe_t, f"c{n}")

            eng.wait_ge(s_const, N_CONSTS)
            eng.wait_ge(s_rows, 16 * N_ROW_LOADS)
            for l in range(DEPTH):
                ins = nc.tensor.transpose(bank[7][:, l * P:l * P + NROWS], prow[:, l, :], ident[0:NROWS, 0:NROWS])
            mark(ins.then_inc(pre_t.sem, 1), pre_t, "rows")
            row_sum_columns(0, "sh1")
            row_sum_columns(0, "sc1")
            for l in range(DEPTH):
                turn_xn(2 * l)
                mixers(l)
                turn_xn(2 * l + 1)
                if l == 0:
                    row_sum_wide(l, 1, (bank[0], bank[1]))
                    eng.wait_ge(gate_v.sem, gate_v.at("g1", 2 * l + 1))
                    eng.wait_ge(norm_a.sem, norm_a.at("h5", 2 * l + 1))
                    eng.wait_ge(norm_v.sem, norm_v.at("h7", 2 * l + 1))
                    ffn()
            row_sum_wide(1, 1, (bank[0], bank[1]))
            eng.wait_ge(norm_a.sem, norm_a.at("h5", 3))
            eng.wait_ge(norm_v.sem, norm_v.at("h7", 3))
            routing()
            experts(0)
            eng.wait_ge(route_v.sem, route_v.at("most_i"))
            with eng.If(eng.value_load(most_i[0:1, 0:1], min_val=0, max_val=T) > SLOTS):
                experts(1)

        def rows2(ap):
            return ap.rearrange("p (b t) -> p b t", b=CB)

        @block.vector
        def _(eng):
            tt_, ts_, stt = nc.vector.tensor_tensor, nc.vector.tensor_scalar, nc.vector.scalar_tensor_tensor

            def mod_part(l, part):
                n = MOD_PARTS.index(part)
                rep = 6 * l + n
                if n >= 2:
                    eng.wait_ge(mod_t.sem, mod_t.at("sum", 4 * l + n - 2))
                elif l:
                    eng.wait_ge(gate_t.sem, gate_t.at("sum", 2 * (l - 1) + n))
                for half in range(2):
                    key = ("mod", l, part, half)
                    arrived(eng, key)
                    dst = mod_acc[:, n % 2, half * W:(half + 1) * W]
                    for k in range(KB):
                        if k == 0:
                            ins = ts_(dst, wide(key)[:, 0, :], c_act[:, 0:1], None, ALU.mult)
                        else:
                            ins = stt(out=dst, in0=wide(key)[:, k, :], scalar=c_act[:, k:k + 1], in1=dst,
                                      op0=ALU.mult, op1=ALU.add)
                        done(eng, ins.then_inc(mod_v.sem, 1), mod_v, f"c{half}k{k}", rep)

            def mod_columns(l, part):
                n = MOD_PARTS.index(part)
                rep = 4 * l + n
                eng.wait_ge(mod_t.sem, mod_t.at("sum", rep))
                b = bank[6] if l == 0 and n >= 2 else bank[0]
                bias = par("b_" + part, l, 0, KB)
                gain = par("norm_mix" if n < 2 else "norm_ffn", l, 0, KB)
                if part.startswith("sh"):
                    done(eng, tt_(mod_tmp[:, :], b[:, 0:KB], bias, ALU.add).then_inc(mod_e.sem, 1), mod_e, "add", rep)
                    done(eng, nc.vector.tensor_copy(mod_col[:, rep, :], mod_tmp[:, :]).then_inc(mod_e.sem, 1),
                         mod_e, "fin", rep)
                else:
                    done(eng, stt(out=mod_tmp[:, :], in0=b[:, 0:KB], scalar=1.0, in1=bias, op0=ALU.add, op1=ALU.add).then_inc(mod_e.sem, 1),
                         mod_e, "add", rep)
                    done(eng, tt_(mod_col[:, rep, :], mod_tmp[:, :], gain, ALU.mult).then_inc(mod_e.sem, 1),
                         mod_e, "fin", rep)

            def gate(l, which, b):
                rep = 2 * l + which
                eng.wait_ge(s_gate, 16 * (rep + 1))
                eng.wait_ge(gate_t.sem, gate_t.at("sum", rep))
                for half in range(2):
                    g = gate_row[:, half * W:(half + 1) * W]
                    done(eng, tt_(g, b[half][:, :], g, ALU.add).then_inc(gate_v.sem, 1), gate_v, f"g{half}", rep)

            def norm(q):
                eng.wait_ge(norm_a.sem, norm_a.at("rt", q))
                done(eng, nc.vector.reciprocal(norm_s[:, 2, :], norm_s[:, 1, :]).then_inc(norm_v.sem, 1),
                     norm_v, "rc", q)
                for tt in range(TT):
                    done(eng, ts_(xn[:, tt, :], x[:, tt, :], norm_s[:, 2, tt:tt + 1], None, ALU.mult).then_inc(norm_v.sem, 1),
                         norm_v, f"xn{tt}", q)
                for b in (1, 3):
                    eng.wait_ge(norm_t.sem, norm_t.at(f"t{b}", q))
                    for i in range(2):
                        k = 2 * b + i
                        done(eng, ts_(h_t[:, k, :], bank[4 + b][:, i * T:(i + 1) * T],
                                      mod_col[:, 2 * q + 1, k:k + 1], mod_col[:, 2 * q, k:k + 1], ALU.mult, ALU.add).then_inc(norm_v.sem, 1),
                             norm_v, f"h{k}", q)

            def residual(rep, src, waits):
                t = h_t[:, 0:2, :].rearrange("p k t -> p (k t)")
                for n in range(4):
                    tt, half = n // 2, n % 2
                    for s, name, last in waits[n]:
                        eng.wait_ge(s.sem, s.at(name, last))
                    c = slice(half * W, (half + 1) * W)
                    done(eng, tt_(t, src[n], gate_row[:, c], ALU.mult).then_inc(res_v.sem, 1),
                         res_v, f"r{2 * n}", rep)
                    done(eng, tt_(x[:, tt, c], x[:, tt, c], t, ALU.add).then_inc(res_v.sem, 1),
                         res_v, f"r{2 * n + 1}", rep)

            def mixers(l):
                def v(ins, name):
                    done(eng, ins, mix_v, name, l)

                def t(i):
                    return tmp[:, i, :]

                eng.wait_ge(mix_t.sem, mix_t.at("ws", l))
                v(tt_(ws_t[:, :, :], bank[3][:, :].rearrange("p (h n) -> p h n", h=NH),
                      triu.unsqueeze(1).to_broadcast([P, NH, P]), ALU.mult).then_inc(mix_v.sem, 1), "wst")
                eng.wait_ge(mix_a.sem, mix_a.at("sig", l))
                for i in range(CB):
                    c = slice(i * T, (i + 1) * T)
                    v(ts_(t(1)[:, c], t(0)[:, c], floor_col[:, l, 1, i:i + 1], floor_col[:, l, 0, i:i + 1],
                          ALU.mult, ALU.add).then_inc(mix_v.sem, 1), f"f{i}")
                for i in range(CB):
                    c = slice(i * T, (i + 1) * T)
                    v(ts_(t(2)[:, c], t(0)[:, c], floor_col[:, l, 2, i:i + 1], floor_col[:, l, 1, i:i + 1],
                          ALU.mult, ALU.add).then_inc(mix_v.sem, 1), f"k{i}")
                v(ts_(t(3), t(1), LN_FLOOR, None, ALU.max).then_inc(mix_v.sem, 1), "fa")
                v(ts_(t(4), t(1), MIN_FORGET, LN_FLOOR, ALU.max, ALU.min).then_inc(mix_v.sem, 1), "fb")
                v(ts_(t(2), t(2), LN_FLOOR, None, ALU.max).then_inc(mix_v.sem, 1), "kc")
                eng.wait_ge(mix_a.sem, mix_a.at("lnb", l))
                v(tt_(t(3), t(3), t(4), ALU.add).then_inc(mix_v.sem, 1), "lf")
                for i in range(CB):
                    c = slice(i * T, (i + 1) * T)
                    v(nc.vector.tensor_tensor_scan(t(1)[:, c], scan_keep[:, :], t(3)[:, c], 0.0, ALU.mult, ALU.add).then_inc(mix_v.sem, 1),
                      f"b{i}")
                eng.wait_ge(mix_a.sem, mix_a.at("lnk", l))
                v(tt_(t(2), t(1), t(2), ALU.subtract).then_inc(mix_v.sem, 1), "bk")
                b4 = t(1).rearrange("p (n s) -> p n s", s=C)
                bk4 = t(2).rearrange("p (n s) -> p n s", s=C)
                v(tt_(t(4).rearrange("p (n s) -> p n s", s=C), b4[:, :, C - 1:C].to_broadcast([P, CB * NC, C]), bk4,
                      ALU.subtract).then_inc(mix_v.sem, 1), "kd")

                def differences(i):
                    for r in range(C):
                        rep = (l * CB + i) * C + r
                        if i or l:
                            if i:
                                eng.wait_ge(mix_t.sem, mix_t.at(f"sc{i - 1}", l))
                            else:
                                eng.wait_ge(mix_t.sem, mix_t.at(f"sc{CB - 1}", l - 1))
                        n = slice(i * NC, (i + 1) * NC)
                        done(eng, tt_(tri[:, r, :, 0:r + 1], b4[:, n, r:r + 1].to_broadcast([P, NC, r + 1]),
                                      bk4[:, n, 0:r + 1], ALU.subtract).then_inc(tri_d.sem, 1), tri_d, "d", rep)

                def times_q(i):
                    q4 = t(0).rearrange("p (n s) -> p n s", s=C)
                    for r in range(C):
                        rep = (l * CB + i) * C + r
                        eng.wait_ge(tri_e.sem, tri_e.at("e", rep))
                        n = slice(i * NC, (i + 1) * NC)
                        done(eng, tt_(tri[:, r, :, 0:r + 1], tri[:, r, :, 0:r + 1],
                                      q4[:, n, r:r + 1].to_broadcast([P, NC, r + 1]), ALU.mult).then_inc(tri_q.sem, 1),
                             tri_q, "q", rep)

                def values_by_chunk(n):
                    i, tt, q = n // (2 * TT), n // 2 % TT, n % 2
                    h = 2 * i + q
                    if n >= 2:
                        eng.wait_ge(mix_t.sem, mix_t.at(f"u{n - 2}", l))
                    src = t(6)[:, tt * G + h * HD:tt * G + (h + 1) * HD]
                    v(tt_(v_wide[:, n % 2, :].rearrange("p (j c) -> p j c", j=CT_),
                          src.unsqueeze(1).to_broadcast([P, CT_, HD]),
                          chunk_of[:, :].unsqueeze(2).to_broadcast([P, CT_, HD]), ALU.mult).then_inc(mix_v.sem, 1),
                      f"vx{n}")

                eng.wait_ge(mix_t.sem, mix_t.at("di", l))
                v(nc.vector.tensor_copy(t(6), bank[1][:, :]).then_inc(mix_v.sem, 1), "v")
                differences(0)
                values_by_chunk(0)
                values_by_chunk(1)
                eng.wait_ge(mix_a.sem, mix_a.at("q", l))
                times_q(0)
                for n in range(2, 8):
                    values_by_chunk(n)
                eng.wait_ge(mix_a.sem, mix_a.at("xp", l))
                for i in range(CB):
                    c = slice(i * T, (i + 1) * T)
                    v(ts_(t(7)[:, c], x_pad[:, i, 0:T], par("conv_w", l, i), par("conv_b", l, i), ALU.mult, ALU.add).then_inc(mix_v.sem, 1),
                      f"cv{i}0")
                    for k in range(1, CONV):
                        v(stt(out=t(7)[:, c], in0=x_pad[:, i, k:k + T], scalar=par("conv_w", l, k * CB + i),
                              in1=t(7)[:, c], op0=ALU.mult, op1=ALU.add).then_inc(mix_v.sem, 1),
                          f"cv{i}{k}" if k < CONV - 1 else f"xc{i}")
                eng.wait_ge(mix_a.sem, mix_a.at("ea", l))
                eng.wait_ge(mix_t.sem, mix_t.at("u7", l))
                if l:
                    eng.wait_ge(mix_t.sem, mix_t.at("o", l - 1))
                ea = small[:, 8:12, :].rearrange("p a b -> p (a b)")
                for c in range(NC - 1):
                    for i in range(CB):
                        u = bank[(6 if i == 0 else 4) + c // CT_][:, (c % CT_) * HD:(c % CT_ + 1) * HD]
                        done(eng, stt(out=state[:, i, c + 1, :], in0=state[:, i, c, :],
                                      scalar=ea[:, i * NC + c:i * NC + c + 1], in1=u, op0=ALU.mult, op1=ALU.add).then_inc(chain_v.sem, 1),
                             chain_v, "s", l * CHAIN + c * CB + i)
                v(tt_(t(3), t(3), t(0), ALU.mult).then_inc(mix_v.sem, 1), "qt")
                differences(1)
                times_q(1)
                eng.wait_ge(mix_a.sem, mix_a.at("a1", l))
                v(tt_(t(11), t(10), t(10), ALU.mult).then_inc(mix_v.sem, 1), "a2")
                eng.wait_ge(mix_a.sem, mix_a.at("th1", l))
                v(stt(out=t(11), in0=t(11), scalar=1.0, in1=t(8), op0=ALU.add, op1=ALU.mult).then_inc(mix_v.sem, 1),
                  "m")
                v(ts_(t(11), t(11), 0.0, None, ALU.max).then_inc(mix_v.sem, 1), "m0")
                v(tt_(t(9), t(9), t(7), ALU.mult).then_inc(mix_v.sem, 1), "ix")
                eng.wait_ge(mix_a.sem, mix_a.at("sm", l))
                v(tt_(t(9), t(11), t(9), ALU.mult).then_inc(mix_v.sem, 1), "bb")
                for i in range(CB):
                    c = slice(i * T, (i + 1) * T)
                    v(nc.vector.tensor_tensor_scan(t(8)[:, c], t(10)[:, c], t(9)[:, c], 0.0, ALU.mult, ALU.add).then_inc(mix_v.sem, 1),
                      f"hs{i}")
                v(tt_(t(12), t(12), t(8), ALU.mult).then_inc(mix_v.sem, 1), "yc_raw")
                eng.wait_ge(mix_t.sem, mix_t.at("u7", l))
                eng.wait_ge(mix_t.sem, mix_t.at("sc1", l))
                for tt in range(TT):
                    sc = bank[6][:, tt * NH * C:(tt + 1) * NH * C].rearrange("p (h r) -> p h r", r=C)
                    v(tt_(s_full[:, tt, :, :].rearrange("p h (j r) -> p h j r", r=C),
                          sc.unsqueeze(2).to_broadcast([P, NH, CT_, C]),
                          chunk_of[:, :].unsqueeze(1).unsqueeze(3).to_broadcast([P, NH, CT_, C]), ALU.mult).then_inc(mix_v.sem, 1),
                      f"sf{tt}")
                eng.wait_ge(mix_a.sem, mix_a.at("gv1", l))
                v(ts_(small[:, 1, 0:2], small[:, 0, 0:2], -1.0 / G, None, ALU.mult).then_inc(mix_v.sem, 1), "mu")
                for tt in range(TT):
                    c = slice(tt * G, (tt + 1) * G)
                    v(ts_(t(4)[:, c], t(4)[:, c], small[:, 1, tt:tt + 1], None, ALU.add).then_inc(mix_v.sem, 1),
                      f"vc{tt}")
                eng.wait_ge(mix_a.sem, mix_a.at("rv", l))
                v(nc.vector.reciprocal(small[:, 4, 0:2], small[:, 3, 0:2]).then_inc(mix_v.sem, 1), "rvr")
                for tt in range(TT):
                    c = slice(tt * G, (tt + 1) * G)
                    v(ts_(t(4)[:, c], t(4)[:, c], small[:, 4, tt:tt + 1], None, ALU.mult).then_inc(mix_v.sem, 1),
                      f"vn{tt}")
                eng.wait_ge(mix_t.sem, mix_t.at("z", l))
                eng.wait_ge(mix_a.sem, mix_a.at("gu", l))
                v(tt_(t(7), t(7), bank[4][:, :], ALU.mult).then_inc(mix_v.sem, 1), "yb_raw")
                eng.wait_ge(mix_a.sem, mix_a.at("rtd", l))
                v(nc.vector.reciprocal(t(5), t(5)).then_inc(mix_v.sem, 1), "rec_d")
                v(tt_(t(2), bank[3][:, :], t(5), ALU.mult).then_inc(mix_v.sem, 1), "od")
                for i in range(CB):
                    c = slice(i * T, (i + 1) * T)
                    v(stt(out=y_t[:, 6 + i, :], in0=t(2)[:, c], scalar=par("hgrn_out", l, i), in1=t(13)[:, c],
                          op0=ALU.mult, op1=ALU.mult).then_inc(mix_v.sem, 1), f"yd{i}")
                for n, (name, at, rt, src, par_name) in enumerate((("c", 4, 9, 12, "lru_out"), ("b", 2, 10, 7, "sgu_out"),
                                                              ("a", 0, 2, 3, "pool_out"))):
                    eng.wait_ge(mix_a.sem, mix_a.at(f"rt{name}", l))
                    r = t(rt)[:, 0:T]
                    v(nc.vector.reciprocal(r, r).then_inc(mix_v.sem, 1), f"rec_{name}")
                    for i in range(CB):
                        c = slice(i * T, (i + 1) * T)
                        v(stt(out=y_t[:, at + i, :], in0=t(src)[:, c], scalar=par(par_name, l, i), in1=r,
                              op0=ALU.mult, op1=ALU.mult).then_inc(mix_v.sem, 1), f"y{name}{i}")

            def ffn():
                mods = list(MOD_PARTS)
                for j in range(NJ):
                    at = tmp[:, 2 + 2 * (j % 2):4 + 2 * (j % 2), :]
                    for i in range(2):
                        eng.wait_ge(ffn_a.sem, ffn_a.at(f"s{i}", j))
                        eng.wait_ge(ffn_t.sem, ffn_t.at(f"h3_{i}", j))
                        if j >= 2:
                            eng.wait_ge(ffn_w.sem, ffn_w.at("w", j - 2))
                        done(eng, tt_(at[:, i, :], tmp[:, i, :], bank[2 + i][:, :], ALU.mult).then_inc(ffn_v.sem, 1),
                             ffn_v, f"a{i}", j)
                    if 1 <= j <= 4:
                        mod_columns(1, MOD_PARTS[j - 1])
                    if mods:
                        mod_part(1, mods.pop(0))

            def routing():
                done_ = lambda ins, name: done(eng, ins, route_v, name)
                R = route
                lg, eq, cand, sel1, lg2, sel2, w, pos, sel, wt = (R[:, i, :, :] for i in range(10))
                m1, f1, m2, d, r, er = (route_c[:, i, :, :] for i in range(6))
                wide_ = lambda c: c.to_broadcast([P, TT, NE])
                ids = iota_f[:, 0:NE].unsqueeze(1).to_broadcast([P, TT, NE])
                eng.wait_ge(route_t.sem, route_t.at("logits"))
                done_(nc.vector.tensor_copy(lg, bank[2][:, 0:TT * NE].rearrange("p (t e) -> p t e", t=TT)).then_inc(route_v.sem, 1),
                      "lg")
                for n, (src, m, s) in enumerate(((lg, m1, sel1), (lg2, m2, sel2))):
                    done_(nc.vector.tensor_reduce(m, src, X, ALU.max).then_inc(route_v.sem, 1), f"max{n}")
                    done_(tt_(eq, src, wide_(m), ALU.is_equal).then_inc(route_v.sem, 1), f"eq{n}")
                    done_(stt(out=cand, in0=eq, scalar=-100.0, in1=ids, op0=ALU.mult, op1=ALU.add).then_inc(route_v.sem, 1),
                          f"cand{n}")
                    done_(nc.vector.tensor_reduce(f1, cand, X, ALU.min).then_inc(route_v.sem, 1), f"first{n}")
                    done_(tt_(s, cand, wide_(f1), ALU.is_equal).then_inc(route_v.sem, 1), f"pick{n}")
                    if n == 0:
                        done_(stt(out=lg2, in0=s, scalar=-3e38, in1=lg, op0=ALU.mult, op1=ALU.add).then_inc(route_v.sem, 1),
                              "lg2")
                done_(tt_(sel, sel1, sel2, ALU.add).then_inc(route_v.sem, 1), "sel")
                done_(tt_(d, m2, m1, ALU.subtract).then_inc(route_v.sem, 1), "diff")
                eng.wait_ge(route_a.sem, route_a.at("exp"))
                done_(ts_(r, er, 1.0, None, ALU.add).then_inc(route_v.sem, 1), "one")
                done_(nc.vector.reciprocal(r, r).then_inc(route_v.sem, 1), "w1")
                done_(tt_(er, er, r, ALU.mult).then_inc(route_v.sem, 1), "w2")
                done_(tt_(w, sel1, wide_(r), ALU.mult).then_inc(route_v.sem, 1), "sw1")
                done_(tt_(wt, sel2, wide_(er), ALU.mult).then_inc(route_v.sem, 1), "sw2")
                done_(tt_(wt, wt, w, ALU.add).then_inc(route_v.sem, 1), "wt")
                eng.wait_ge(route_t.sem, route_t.at("pos"))
                done_(nc.vector.tensor_copy(pos, bank[2][:, 64:64 + TT * NE].rearrange("p (t e) -> p t e", t=TT)).then_inc(route_v.sem, 1),
                      "pos")
                done_(nc.vector.tensor_reduce(most[:, 0:1], bank[2][:, 64 + 2 * NE:64 + 3 * NE], X, ALU.max).then_inc(route_v.sem, 1),
                      "most")
                done_(nc.vector.tensor_copy(most_i[:, :], most[:, 0:1]).then_inc(route_v.sem, 1), "most_i")
                done_(nc.vector.memset(dispatch[:, :, NE, :], 0.0).then_inc(route_v.sem, 1), "idle")
                for n in range(4):
                    done(eng, nc.vector.memset(moe_sum[:, n // 2, n % 2 * W:(n % 2 + 1) * W], 0.0).then_inc(sum_v.sem, 1),
                         sum_v, f"a{n}", 0)

            def fill_half(b, first, e, rep, s, name, u):
                eng.wait_ge(s.sem, s.at(name, e))
                for k in range(4):
                    kb = first + k
                    done(eng, ts_(x_slots[:, u, kb, :], b[:, k * P:(k + 1) * P], mod_col[:, 7, kb:kb + 1],
                                  mod_col[:, 6, kb:kb + 1], ALU.mult, ALU.add).then_inc(fill_v.sem, 1),
                         fill_v, f"x{kb}", rep)

            def experts(q):
                pos, sel, wt = (route[:, i, :, :] for i in (7, 8, 9))
                done(eng, ts_(route[:, 10, :, :], pos, float(-q * SLOTS), None, ALU.add).then_inc(slot_v.sem, 1),
                     slot_v, "pos", q)
                for e in range(NE):
                    if e >= 2:
                        eng.wait_ge(slot_t.sem, slot_t.at(f"tr{e - 2}", q))
                    for tt in range(TT):
                        p = route[:, 10, tt, e:e + 1]
                        done(eng, ts_(dispatch[:, tt, e, :], iota_f, p, sel[:, tt, e:e + 1], ALU.is_equal, ALU.mult).then_inc(slot_v.sem, 1),
                             slot_v, f"d{e}_{tt}", q)
                    for tt in range(TT):
                        done(eng, ts_(act_t[:, e % 2, tt * P:(tt + 1) * P], dispatch[:, tt, e, :], wt[:, tt, e:e + 1],
                                      None, ALU.mult).then_inc(slot_v.sem, 1), slot_v, f"wd{e}_{tt}", q)
                    if e == 1:
                        fill_half(bank[5], 4, q, q * (NE + 1), slot_t, "g1", 0)
                with eng.Fori(0, NE // PAIR) as g:
                    for u in range(PAIR):
                        r = expert(q, g, u)
                        fill = q * (NE + 1) + g * PAIR + u
                        eng.wait_ge(slot_a.sem, slot_a.at(f"sp{NE - 1}", q))
                        done(eng, nc.vector.tensor_copy(
                            spread_e[:, :], spread[:, bass.ds(g * PAIR + u, 1), :].rearrange("p o n -> p (o n)")).then_inc(moe_v.sem, 1),
                             moe_v, "spread", r)
                        for j in range(NJ):
                            eng.wait_ge(moe_a.sem, moe_a.at(f"s{j}", r))
                            eng.wait_ge(moe_t.sem, moe_t.at(f"h3_{j}", r))
                            done(eng, tt_(act_m[:, j % 2, :], act_s[:, j % 2, :], bank[2 + j % 2][:, :], ALU.mult).then_inc(moe_v.sem, 1),
                                 moe_v, f"m{j}", r)
                        eng.wait_ge(moe_t.sem, moe_t.at(f"w_{NJ - 1}", r))
                        done(eng, nc.vector.tensor_copy(y_slots[:, W:D], bank[5][:, :]).then_inc(moe_v.sem, 1),
                             moe_v, "y1", r)
                        fill_half(bank[7], 4, r, fill + 1, moe_t, "gb", (u + 1) % 2)
                        for n, b in enumerate((1, 3, 6, 7)):
                            eng.wait_ge(moe_t.sem, moe_t.at(f"c{n}", r))
                            m = moe_sum[:, n // 2, n % 2 * W:(n % 2 + 1) * W]
                            done(eng, tt_(m, bank[b][:, :], m, ALU.add).then_inc(sum_v.sem, 1), sum_v, f"a{n}", r + 1)

            eng.wait_ge(pre_t.sem, pre_t.at("rows"))
            done(eng, nc.vector.tensor_copy(params[:, :, :],
                                            bank[7][:, 0:DEPTH * P].rearrange("p (l n) -> p l n", l=DEPTH)[:, :, 0:NROWS]).then_inc(pre_v.sem, 1),
                 pre_v, "params")
            pv = lambda ins, name: done(eng, ins, pre_v, name)
            eng.wait_ge(pre_a.sem, pre_a.at("c"))
            mod_part(0, "sh1")
            mod_part(0, "sc1")
            mod_columns(0, "sh1")
            mod_columns(0, "sc1")
            r = ROWS["lambda"][0]
            lam = params[:, :, r:r + CB]
            sm = lambda i: small[:, i, 0:DEPTH * CB].rearrange("p (l b) -> p l b", l=DEPTH)
            pv(ts_(sm(0), lam, -1.0, None, ALU.mult).then_inc(pre_v.sem, 1), "neg")
            pv(tt_(sm(1), sm(0), lam, ALU.max).then_inc(pre_v.sem, 1), "abs")
            pv(ts_(sm(2), lam, 0.0, None, ALU.min).then_inc(pre_v.sem, 1), "min")
            r = ROWS["gamma"][0]
            g0, g1 = params[:, 0, r:r + CB], params[:, 0, r + CB:r + 2 * CB]
            pv(tt_(small[:, 3, 0:CB], g0, g1, ALU.max).then_inc(pre_v.sem, 1), "gm")
            pv(tt_(small[:, 4, 0:CB], g0, small[:, 3, 0:CB], ALU.subtract).then_inc(pre_v.sem, 1), "gd0")
            pv(tt_(small[:, 4, CB:2 * CB], g1, small[:, 3, 0:CB], ALU.subtract).then_inc(pre_v.sem, 1), "gd1")
            eng.wait_ge(pre_a.sem, pre_a.at("gexp"))
            e0, e1 = small[:, 5, 0:CB], small[:, 5, CB:2 * CB]
            pv(tt_(small[:, 3, 0:CB], e0, e1, ALU.add).then_inc(pre_v.sem, 1), "gs")
            pv(nc.vector.reciprocal(small[:, 3, 0:CB], small[:, 3, 0:CB]).then_inc(pre_v.sem, 1), "gr")
            pv(tt_(e0, e0, small[:, 3, 0:CB], ALU.mult).then_inc(pre_v.sem, 1), "p0")
            pv(tt_(e1, e1, small[:, 3, 0:CB], ALU.mult).then_inc(pre_v.sem, 1), "p1")
            pv(tt_(e1, e0, e1, ALU.add).then_inc(pre_v.sem, 1), "c1")
            pv(tt_(floor_col[:, 0, 0, :], e0, e0, ALU.subtract).then_inc(pre_v.sem, 1), "lb0")
            pv(tt_(floor_col[:, 1, 0, :], e1, e0, ALU.subtract).then_inc(pre_v.sem, 1), "lb1")
            pv(ts_(floor_col[:, :, 1, :], floor_col[:, :, 0, :], -1.0, 1.0, ALU.mult, ALU.add).then_inc(pre_v.sem, 1),
               "lbo")
            pv(ts_(floor_col[:, :, 2, :], floor_col[:, :, 0, :], 1.0, -1.0, ALU.mult, ALU.add).then_inc(pre_v.sem, 1),
               "lbn")
            eng.wait_ge(pre_a.sem, pre_a.at("lln"))
            pv(tt_(sm(2), sm(2), sm(7), ALU.subtract).then_inc(pre_v.sem, 1), "ls")
            pv(ts_(lru_k[:, :, 0, :], sm(2), LRU_C, None, ALU.mult).then_inc(pre_v.sem, 1), "lk0")
            pv(ts_(lru_k[:, :, 1, :], sm(2), -LRU_C, None, ALU.mult).then_inc(pre_v.sem, 1), "lk1")
            for l in range(DEPTH):
                norm(2 * l)
                mixers(l)
                if l == 0:
                    mod_part(0, "sh2")
                    mod_part(0, "sc2")
                    mod_columns(0, "sh2")
                    mod_columns(0, "sc2")
                    mod_part(0, "g1")
                gate(l, 0, (bank[5], bank[7]))
                residual(2 * l, [bank[n][:, :] for n in range(4)], [[(mix_t, f"wout{n}", l)] for n in range(4)])
                norm(2 * l + 1)
                if l == 0:
                    mod_part(0, "g2")
                gate(l, 1, (bank[0], bank[1]))
                if l == 0:
                    ffn()
                    residual(1, [bank[4 + n][:, :] for n in range(4)], [[(ffn_w, "w", NJ - 1)]] * 4)
            routing()
            experts(0)
            with eng.If(eng.value_load(most_i[0:1, 0:1], min_val=0, max_val=T) > SLOTS):
                experts(1)
            residual(3, [moe_sum[:, n // 2, n % 2 * W:(n % 2 + 1) * W] for n in range(4)], [[]] * 4)
            eng.wait_ge(end_a.sem, end_a.at("rt"))
            done(eng, nc.vector.reciprocal(norm_s[:, 2, :], norm_s[:, 1, :]).then_inc(end_v.sem, 1), end_v, "rc")
            eng.wait_ge(s_gate, 16 * (2 * DEPTH + 1))
            for tt in range(TT):
                done(eng, stt(out=xn[:, tt, :], in0=x[:, tt, :], scalar=norm_s[:, 2, tt:tt + 1], in1=gate_row[:, :],
                              op0=ALU.mult, op1=ALU.mult).then_inc(end_v.sem, 1), end_v, f"out{tt}")

        @block.scalar
        def _(eng):
            act = nc.scalar.activation

            def mean_square(s, rep):
                for tt in range(TT):
                    done(eng, act(xn[:, tt, :], x[:, tt, :], ACT.Square, accum_out=norm_s[:, 0, tt:tt + 1]).then_inc(s.sem, 1),
                         s, f"sq{tt}", rep)
                done(eng, act(norm_s[:, 1, :], norm_s[:, 0, :], ACT.Sqrt, bias=eps_col[:, 0:1], scale=1.0 / D).then_inc(s.sem, 1),
                     s, "rt", rep)

            def norm(q):
                if q == 0:
                    eng.wait_ge(s_x, 16)
                else:
                    eng.wait_ge(res_v.sem, res_v.at("r7", q - 1))
                mean_square(norm_a, q)
                eng.wait_ge(mod_e.sem, mod_e.at("fin", 2 * q + 1))
                for b in (0, 2):
                    eng.wait_ge(norm_t.sem, norm_t.at(f"t{b}", q))
                    for i in range(2):
                        k = 2 * b + i
                        done(eng, act(h_t[:, k, :], bank[4 + b][:, i * T:(i + 1) * T], ACT.Identity,
                                      bias=mod_col[:, 2 * q, k:k + 1], scale=mod_col[:, 2 * q + 1, k:k + 1]).then_inc(norm_a.sem, 1),
                             norm_a, f"h{k}", q)

            def mixers(l):
                def s(ins, name):
                    done(eng, ins, mix_a, name, l)

                def t(i):
                    return tmp[:, i, :]

                eng.wait_ge(mix_t.sem, mix_t.at("dfz", l))
                s(act(t(0), bank[0][:, :], ACT.Sigmoid).then_inc(mix_a.sem, 1), "sig")
                eng.wait_ge(mix_v.sem, mix_v.at("fa", l))
                s(act(t(3), t(3), ACT.Ln).then_inc(mix_a.sem, 1), "lna")
                eng.wait_ge(mix_v.sem, mix_v.at("fb", l))
                s(act(t(4), t(4), ACT.Ln, scale=1.0 / LN_FLOOR).then_inc(mix_a.sem, 1), "lnb")
                eng.wait_ge(mix_v.sem, mix_v.at("kc", l))
                s(act(t(2), t(2), ACT.Ln).then_inc(mix_a.sem, 1), "lnk")
                eng.wait_ge(mix_v.sem, mix_v.at("b1", l))
                s(act(t(3), t(1), ACT.Exp).then_inc(mix_a.sem, 1), "eb")
                ends = t(1).rearrange("p (n s) -> p n s", s=C)[:, :, C - 1]
                s(act(small[:, 8:12, :].rearrange("p a b -> p (a b)"), ends, ACT.Exp).then_inc(mix_a.sem, 1), "ea")
                eng.wait_ge(mix_v.sem, mix_v.at("kd", l))
                s(act(t(4), t(4), ACT.Exp).then_inc(mix_a.sem, 1), "kh")

                def exps(i):
                    for r in range(C):
                        rep = (l * CB + i) * C + r
                        eng.wait_ge(tri_d.sem, tri_d.at("d", rep))
                        done(eng, act(tri[:, r, :, 0:r + 1], tri[:, r, :, 0:r + 1], ACT.Exp).then_inc(tri_e.sem, 1),
                             tri_e, "e", rep)

                exps(0)
                eng.wait_ge(mix_t.sem, mix_t.at("dq", l))
                s(act(t(0), bank[2][:, :], ACT.Silu).then_inc(mix_a.sem, 1), "q")
                eng.wait_ge(mix_t.sem, mix_t.at("kt", l))
                s(act(t(5), bank[4][:, :], ACT.Copy).then_inc(mix_a.sem, 1), "kt")
                eng.wait_ge(mix_t.sem, mix_t.at("px", l))
                if l:
                    eng.wait_ge(mix_v.sem, mix_v.at("xc1", l - 1))
                s(act(x_pad[:, :, CONV - 1:], rows2(bank[0][:, :]), ACT.Copy).then_inc(mix_a.sem, 1), "xp")
                eng.wait_ge(mix_t.sem, mix_t.at("pg", l))
                s(act(t(12), bank[1][:, :], ACT.Gelu_apprx_tanh).then_inc(mix_a.sem, 1), "gate_c")
                eng.wait_ge(mix_t.sem, mix_t.at("pv", l))
                for tt in range(TT):
                    c = slice(tt * G, (tt + 1) * G)
                    s(act(t(4)[:, c], bank[2][:, c], ACT.Gelu_apprx_tanh, accum_out=small[:, 0, tt:tt + 1]).then_inc(mix_a.sem, 1),
                      f"gv{tt}")
                exps(1)
                for name, b, dst, bias in (("r", 4, 8, "lru_ba"), ("i", 5, 9, "lru_bx")):
                    eng.wait_ge(mix_t.sem, mix_t.at("wa" if name == "r" else "wx", l))
                    for i in range(CB):
                        c = slice(i * T, (i + 1) * T)
                        s(act(t(dst)[:, c], bank[b][:, c], ACT.Sigmoid, bias=par(bias, l, i)).then_inc(mix_a.sem, 1),
                          f"{name}{i}")
                for i in range(CB):
                    c = slice(i * T, (i + 1) * T)
                    s(act(t(10)[:, c], t(8)[:, c], ACT.Exp, scale=lru_k[:, l, 0, i:i + 1]).then_inc(mix_a.sem, 1),
                      f"a{i}")
                for i in range(CB):
                    c = slice(i * T, (i + 1) * T)
                    s(act(t(8)[:, c], t(8)[:, c], ACT.Tanh, scale=lru_k[:, l, 1, i:i + 1]).then_inc(mix_a.sem, 1),
                      f"th{i}")
                eng.wait_ge(mix_v.sem, mix_v.at("m0", l))
                s(act(t(11), t(11), ACT.Sqrt).then_inc(mix_a.sem, 1), "sm")
                eng.wait_ge(mix_t.sem, mix_t.at("dg", l))
                s(act(t(13), bank[0][:, :], ACT.Silu).then_inc(mix_a.sem, 1), "gate_d")
                eng.wait_ge(mix_v.sem, mix_v.at("yc_raw", l))
                s(act(t(8), t(12), ACT.Square).then_inc(mix_a.sem, 1), "sqc")
                eng.wait_ge(mix_v.sem, mix_v.at("vc1", l))
                for tt in range(TT):
                    c = slice(tt * G, (tt + 1) * G)
                    s(act(t(5)[:, c], t(4)[:, c], ACT.Square, accum_out=small[:, 2, tt:tt + 1]).then_inc(mix_a.sem, 1),
                      f"sv{tt}")
                s(act(small[:, 3, 0:2], small[:, 2, 0:2], ACT.Sqrt, bias=eps_col[:, 0:1], scale=1.0 / G).then_inc(mix_a.sem, 1),
                  "rv")
                eng.wait_ge(mix_t.sem, mix_t.at("pu", l))
                s(act(t(7), bank[1][:, :], ACT.Gelu_apprx_tanh).then_inc(mix_a.sem, 1), "gu")
                eng.wait_ge(mix_t.sem, mix_t.at("pa", l))
                s(act(t(11), bank[2][:, :], ACT.Copy).then_inc(mix_a.sem, 1), "pa")
                eng.wait_ge(mix_t.sem, mix_t.at("o", l))
                s(act(t(2), bank[3][:, :], ACT.Square).then_inc(mix_a.sem, 1), "sqd")
                eng.wait_ge(mix_t.sem, mix_t.at("ssd", l))
                s(act(t(5), bank[7][:, :], ACT.Sqrt, bias=eps_col[:, 0:1], scale=1.0 / HD).then_inc(mix_a.sem, 1),
                  "rtd")
                eng.wait_ge(mix_t.sem, mix_t.at("ssc", l))
                s(act(t(9)[:, 0:T], bank[5][:, 0:T], ACT.Sqrt, bias=eps_col[:, 0:1], scale=1.0 / G).then_inc(mix_a.sem, 1),
                  "rtc")
                eng.wait_ge(mix_t.sem, mix_t.at("aband", l))
                s(act(t(6), bank[6][:, :], ACT.Copy).then_inc(mix_a.sem, 1), "pd")
                eng.wait_ge(mix_v.sem, mix_v.at("yb_raw", l))
                s(act(t(4), t(7), ACT.Square).then_inc(mix_a.sem, 1), "sqb")
                eng.wait_ge(mix_t.sem, mix_t.at("ssb", l))
                s(act(t(10)[:, 0:T], bank[7][:, 0:T], ACT.Sqrt, bias=eps_col[:, 0:1], scale=1.0 / G).then_inc(mix_a.sem, 1),
                  "rtb")
                eng.wait_ge(mix_t.sem, mix_t.at("apool", l))
                for i in range(CB):
                    c = slice(i * T, (i + 1) * T)
                    s(act(t(3)[:, c], bank[4][:, c], ACT.Copy, scale=par("pool_scale", l, i)).then_inc(mix_a.sem, 1),
                      f"ps{i}")
                s(act(t(1), t(3), ACT.Square).then_inc(mix_a.sem, 1), "sqa")
                eng.wait_ge(mix_t.sem, mix_t.at("ssa", l))
                eng.wait_ge(mix_v.sem, mix_v.at("od", l))
                eng.wait_ge(mix_v.sem, mix_v.at("yd1", l))
                s(act(t(2)[:, 0:T], bank[5][:, 0:T], ACT.Sqrt, bias=eps_col[:, 0:1], scale=1.0 / G).then_inc(mix_a.sem, 1),
                  "rta")

            def ffn():
                for j in range(NJ):
                    for i in range(2):
                        eng.wait_ge(ffn_t.sem, ffn_t.at(f"h1_{i}", j))
                        if j:
                            eng.wait_ge(ffn_v.sem, ffn_v.at(f"a{i}", j - 1))
                        done(eng, act(tmp[:, i, :], bank[i][:, :], ACT.Silu).then_inc(ffn_a.sem, 1),
                             ffn_a, f"s{i}", j)

            def fill_half(b, first, e, rep, s, name, u):
                eng.wait_ge(s.sem, s.at(name, e))
                for k in range(4):
                    kb = first + k
                    done(eng, act(x_slots[:, u, kb, :], b[:, k * P:(k + 1) * P], ACT.Identity,
                                  bias=mod_col[:, 6, kb:kb + 1], scale=mod_col[:, 7, kb:kb + 1]).then_inc(fill_a.sem, 1),
                         fill_a, f"x{kb}", rep)

            def experts(q):
                fill_half(bank[4], 0, q, q * (NE + 1), slot_t, "g0", 0)
                for e in range(NE):
                    eng.wait_ge(slot_t.sem, slot_t.at(f"tr{e}", q))
                    done(eng, act(spread[:, e, :], bank[e % 2][:, 0:T], ACT.Copy).then_inc(slot_a.sem, 1),
                         slot_a, f"sp{e}", q)
                with eng.Fori(0, NE // PAIR) as g:
                    for u in range(PAIR):
                        r = expert(q, g, u)
                        fill = q * (NE + 1) + g * PAIR + u
                        for j in range(NJ + 1):
                            if j < NJ:
                                eng.wait_ge(moe_t.sem, moe_t.at(f"h1_{j}", r))
                                if j >= 2:
                                    eng.wait_ge(moe_v.sem, moe_v.at(f"m{j - 2}", r))
                                done(eng, act(act_s[:, j % 2, :], bank[j % 2][:, :], ACT.Silu).then_inc(moe_a.sem, 1),
                                     moe_a, f"s{j}", r)
                            if j:
                                eng.wait_ge(moe_t.sem, moe_t.at(f"t{j - 1}", r))
                                done(eng, act(act_t[:, (j - 1) % 2, :], bank[6][:, :], ACT.Copy).then_inc(moe_a.sem, 1),
                                     moe_a, f"at{j - 1}", r)
                        fill_half(bank[7], 0, r, fill + 1, moe_t, "ga", (u + 1) % 2)
                        eng.wait_ge(moe_t.sem, moe_t.at(f"w_{NJ - 1}", r))
                        done(eng, act(y_slots[:, 0:W], bank[4][:, :], ACT.Copy).then_inc(moe_a.sem, 1),
                             moe_a, "y0", r)

            eng.wait_ge(pre_v.sem, pre_v.at("params"))
            r = ROWS["c"][0]
            done(eng, act(c_act[:, :], params[:, 0, r:r + KB], ACT.Silu).then_inc(pre_a.sem, 1), pre_a, "c")
            eng.wait_ge(pre_v.sem, pre_v.at("gd1"))
            done(eng, act(small[:, 5, 0:2 * CB], small[:, 4, 0:2 * CB], ACT.Exp).then_inc(pre_a.sem, 1),
                 pre_a, "gexp")
            done(eng, act(small[:, 6, 0:DEPTH * CB], small[:, 1, 0:DEPTH * CB], ACT.Exp, scale=-1.0).then_inc(pre_a.sem, 1),
                 pre_a, "lexp")
            done(eng, act(small[:, 7, 0:DEPTH * CB], small[:, 6, 0:DEPTH * CB], ACT.Ln, bias=1.0).then_inc(pre_a.sem, 1),
                 pre_a, "lln")
            for l in range(DEPTH):
                norm(2 * l)
                mixers(l)
                norm(2 * l + 1)
                if l == 0:
                    ffn()
            eng.wait_ge(route_v.sem, route_v.at("diff"))
            done(eng, act(route_c[:, 5, :, :], route_c[:, 3, :, :], ACT.Exp).then_inc(route_a.sem, 1), route_a, "exp")
            experts(0)
            eng.wait_ge(route_v.sem, route_v.at("most_i"))
            with eng.If(eng.value_load(most_i[0:1, 0:1], min_val=0, max_val=T) > SLOTS):
                experts(1)
            eng.wait_ge(res_v.sem, res_v.at("r7", 3))
            mean_square(end_a, 0)


_INS = ['x', 'c', 'w_mod', 'b_mod', 'norm_mix', 'norm_ffn', 'norm_final', 'w_in', 'w_out', 'pool_w', 'pool_scale',
        'pool_out_norm', 'sgu_ws', 'sgu_b', 'sgu_out_norm', 'conv_w', 'conv_b', 'lru_wa', 'lru_ba', 'lru_wx', 'lru_bx',
        'lru_lambda', 'lru_out_norm', 'hgrn_gamma', 'hgrn_out_norm', 'ffn_w1', 'ffn_w3', 'ffn_w2', 'router_w',
        'router_b', 'moe_w1', 'moe_w3', 'moe_w2']
_OUTS = [((1, T, D), 'float32')]


def kernel(**inputs):
    import numpy as _np
    import concourse.bacc as _bacc
    from concourse import mybir as _mybir
    from concourse.bass_utils import run_bass_kernel_spmd as _run

    nc = _bacc.Bacc("TRN2", target_bir_lowering=False, num_devices=1)
    arrays, args = {}, {}
    for name in _INS:
        v = _np.ascontiguousarray(inputs[name])
        arrays[f"in_{name}_dram"] = v
        args[name] = nc.dram_tensor(f"in_{name}_dram", v.shape, _mybir.dt.from_np(v.dtype), kind="ExternalInput").ap()
    out = nc.dram_tensor("out_0_dram", _OUTS[0][0], _mybir.dt.float32, kind="ExternalOutput").ap()
    hybrid_stream_block(nc, args, out)
    r = _run(nc, [arrays], core_ids=[0])
    return r.results[0]["out_0_dram"]
```

```python
from contextlib import ExitStack

import concourse.bass as bass
from concourse import mybir

P = 128
D = 1024
KB = D // P
T = 256
TT = T // P
DEPTH = 2
G = 256
CB = G // P
HD = 64
NH = G // HD
WINDOWS = (2, 4, 8, 16)
CONV = 4
LRU_C = 8.0
DFF = 7 * D // 2
W = 512
NJ = DFF // W
HB = W // P
NE = 8
SLOTS = P
EPS = 1e-6
MIN_FORGET = 1e-30
C = 16
NC = T // C
CT_ = P // C
RING = 6
EDGE = P + 16
LN_FLOOR = 2.0 ** -60

F32 = mybir.dt.float32
F32R = mybir.dt.float32r
I32 = mybir.dt.int32
ALU = mybir.AluOpType
ACT = mybir.ActivationFunctionType
X = mybir.AxisListType.X

ROWS = {}
_at = 0
for _name, _n in (("norm_mix", KB), ("norm_ffn", KB), ("pool_scale", CB), ("pool_out", CB), ("sgu_out", CB),
                  ("conv_w", CONV * CB), ("conv_b", CB), ("lru_ba", CB), ("lru_bx", CB), ("lambda", CB),
                  ("lru_out", CB), ("hgrn_out", CB), ("gamma", DEPTH * CB), ("c", KB),
                  ("b_sh1", KB), ("b_sc1", KB), ("b_sh2", KB), ("b_sc2", KB)):
    ROWS[_name] = (_at, _n)
    _at += _n
NROWS = _at

COLS = {n: i * G for i, n in enumerate(("pa", "pu", "pv", "px", "pg", "dq", "dfz", "di", "dg"))}
GROUPS = ("dfz", "di", "dq", "px", "pg", "pv", "dg", "pu", "pa")
WIN_ORDER = (3, 2, 1, 4, 0)
MOD_PARTS = ("sh1", "sc1", "sh2", "sc2", "g1", "g2")
MOD_COL = {"sh1": 0, "sc1": 1, "g1": 2, "sh2": 3, "sc2": 4, "g2": 5}
FFN_ORDER = ([("w1", 0), ("w3", 0)]
             + [x for j in range(1, NJ) for x in (("w1", j), ("w3", j), ("w2", j - 1))] + [("w2", NJ - 1)])
NCH = len(FFN_ORDER)
GATHER = 4
UNITS = 2 * NCH
HIGHS = 3
assert UNITS % HIGHS == 0
PAIR = 2
assert PAIR * NCH % RING == 0 and NE % PAIR == 0


class Steps:

    def __init__(self, sem, names):
        self.sem, self.names = sem, names
        self.count = 0
        self.index = {n: i + 1 for i, n in enumerate(names)}

    def at(self, name, rep=0):
        return rep * len(self.names) + self.index[name]

    def said(self, name):
        assert self.names[self.count % len(self.names)] == name, (self.names[self.count % len(self.names)], name)
        self.count += 1



N_ROW_LOADS = 25
N_CONSTS = 81
CHAIN = CB * (NC - 1)

STEPS = {
    "pre_v":
        ("params neg abs min gm gd0 gd1 gs gr p0 p1 c1 lb0 lb1 lbo lbn ls lk0 lk1").split(),
    "pre_a":
        ("c gexp lexp lln").split(),
    "pre_t":
        ("rows").split(),
    "mod_v":
        ("c0k0 c0k1 c0k2 c0k3 c0k4 c0k5 c0k6 c0k7 c1k0 c1k1 c1k2 c1k3 c1k4 c1k5 c1k6 c1k7").split(),
    "mod_t":
        ("sum").split(),
    "mod_e":
        ("add fin").split(),
    "gate_t":
        ("sum").split(),
    "gate_v":
        ("g0 g1").split(),
    "norm_v":
        ("rc xn0 xn1 h2 h3 h6 h7").split(),
    "norm_a":
        ("sq0 sq1 rt h0 h1 h4 h5").split(),
    "norm_t":
        ("t0 t1 t2 t3").split(),
    "mix_v":
        ("wst f0 f1 k0 k1 fa fb kc lf b0 b1 bk kd v vx0 vx1 vx2 vx3 vx4 vx5 vx6 vx7 cv00 cv01 cv02 xc0 "
         "cv10 cv11 cv12 xc1 qt a2 m m0 ix bb hs0 hs1 yc_raw sf0 sf1 mu vc0 vc1 rvr vn0 vn1 yb_raw rec_d "
         "od yd0 yd1 rec_c yc0 yc1 rec_b yb0 yb1 rec_a ya0 ya1").split(),
    "mix_a":
        ("sig lna lnb lnk eb ea kh q kt xp gate_c gv0 gv1 r0 r1 i0 i1 a0 a1 th0 th1 sm gate_d sqc sv0 sv1 "
         "rv gu pa sqd rtd rtc pd sqb rtb ps0 ps1 sqa rta").split(),
    "mix_t":
        ("ws dfz di dq kt px u0 u1 u2 u3 u4 u5 u6 u7 pg pv wa wx sc0 dg pu pa sc1 o z ssd ssc aband ssb "
         "apool ssa wout0 wout1 wout2 wout3").split(),
    "tri_d":
        ("d").split(),
    "tri_e":
        ("e").split(),
    "tri_q":
        ("q").split(),
    "chain_v":
        ("s").split(),
    "res_v":
        ("r0 r1 r2 r3 r4 r5 r6 r7").split(),
    "ffn_v":
        ("a0 a1").split(),
    "ffn_a":
        ("s0 s1").split(),
    "ffn_t":
        ("h1_0 h3_0 h1_1 h3_1").split(),
    "ffn_w":
        ("w").split(),
    "route_v":
        ("lg max0 eq0 cand0 first0 pick0 lg2 max1 eq1 cand1 first1 pick1 sel diff one w1 w2 sw1 sw2 wt pos "
         "most most_i idle ch0 ch1 ch2").split(),
    "route_a":
        ("exp").split(),
    "route_t":
        ("logits pos").split(),
    "slot_v":
        ("choice d0 disp").split(),
    "slot_t":
        ("g0 g1").split(),
    "slot_pos":
        ("pos").split(),
    "moe_v":
        ("m0 al0 m1 choice d0 disp al1 m2 al2 m3 al3 m4 al4 m5 al5 m6 al6 yl0 yl1").split(),
    "moe_a":
        ("s0 s1 ah0 spread s2 ah1 s3 ah2 s4 ah3 s5 ah4 s6 ah5 ah6 yh0 yh1").split(),
    "moe_t":
        ("t0 spread t1 t2 t3 ga t4 gb t5 t6 c0 c1 c2 c3").split(),
    "fill_v":
        ("la lb").split(),
    "fill_a":
        ("x0 x1 x2 x3 h0 x4 x5 x6 x7 h1").split(),
    "sum_v":
        ("a0 a1 a2 a3").split(),
    "end_v":
        ("rc out0 out1").split(),
    "end_a":
        ("sq0 sq1 rt").split(),
}


def hybrid_stream_block(nc, a, out):
    ctx = ExitStack()
    with ctx:
        def sb(name, shape, dt=F32):
            return ctx.enter_context(nc.sbuf_tensor(name, shape, dt))

        def sem(name):
            return ctx.enter_context(nc.semaphore(name))

        shared = ExitStack()
        ring = shared.enter_context(nc.sbuf_tensor("ring", [P, RING, KB * W], F32))
        shared.close()
        ring_low = sb("ring_low", [P, RING, KB * W], F32R)
        x = sb("x", [P, TT, D])
        xn = sb("xn", [P, TT, D])
        y_t = xn[:, :, :].rearrange("p t (b c) -> p (t b) c", c=T)
        mod_tmp = sb("mod_tmp", [P, KB])
        mod_col = sb("mod_col", [P, DEPTH * 4, KB])
        gate_row = sb("gate_row", [P, D])
        consts = sb("consts", [P, 7, P])
        ident, ones, head_ones, triu, lower, before, iota_f = (consts[:, i, :] for i in range(7))
        scan_keep = sb("scan_keep", [P, T])
        chunk_of = sb("chunk_of", [P, CT_])
        head_sel = sb("head_sel", [P, 2])
        row_sel = sb("row_sel", [NH, CB, P])
        eps_col = sb("eps_col", [P, 1])
        params = sb("params", [P, DEPTH, NROWS])
        c_act = sb("c_act", [P, KB])
        lru_k = sb("lru_k", [P, DEPTH, 2, CB])
        floor_col = sb("floor_col", [P, DEPTH, 3, CB])
        small = sb("small", [P, 16, 8])
        sgu_bias = sb("sgu_bias", [NH, P])
        norm_s = sb("norm_s", [P, 4, TT])
        low = ExitStack()
        h_t = low.enter_context(nc.sbuf_tensor("h_t", [P, KB, T], F32))
        mod_acc = low.enter_context(nc.sbuf_tensor("mod_acc", [P, 2, D], F32))
        tmp = low.enter_context(nc.sbuf_tensor("tmp", [P, 14, G * CB], F32))
        v_wide = low.enter_context(nc.sbuf_tensor("v_wide", [P, 2, W], F32))
        tri = low.enter_context(nc.sbuf_tensor("tri", [P, C, NC, C], F32))
        state = low.enter_context(nc.sbuf_tensor("state", [P, CB, NC, HD], F32))
        band_a = low.enter_context(nc.sbuf_tensor("band_a", [P, NH, EDGE], F32))
        band_b = low.enter_context(nc.sbuf_tensor("band_b", [P, NH, P], F32))
        blocks = low.enter_context(nc.sbuf_tensor("blocks", [P, 3, CB, P], F32))
        ws_t = low.enter_context(nc.sbuf_tensor("ws_t", [P, NH, P], F32))
        x_pad = low.enter_context(nc.sbuf_tensor("x_pad", [P, CB, CONV - 1 + T], F32))
        s_full = v_wide[:, :, :].rearrange("p t (h n) -> p t h n", h=NH)
        prow = tmp[0:NROWS, 0, 0:DEPTH * P].rearrange("p (l n) -> p l n", l=DEPTH)
        low.close()
        moe_mem = ExitStack()

        def mb(name, shape, dt=F32):
            return moe_mem.enter_context(nc.sbuf_tensor(name, shape, dt))

        w_high = mb("w_high", [P, HIGHS, KB * W // 2], F32R)
        x_slots = mb("x_slots", [P, 4, SLOTS])
        x_high = mb("x_high", [P, 2, KB, SLOTS], F32R)
        x_low = mb("x_low", [P, 2, KB, SLOTS], F32R)
        dispatch = mb("dispatch", [P, 2, TT, SLOTS])
        choice = mb("choice", [P, 2, 3, TT])
        chosen = mb("chosen", [P, 3, NE + 1, TT])
        spread = mb("spread", [P, T], F32R)
        moe_sum = mb("moe_sum", [P, TT, D])
        act_s = mb("act_s", [P, 2, W])
        act_m = mb("act_m", [P, 2, W])
        act_high = mb("act_high", [P, 2, W], F32R)
        act_low = mb("act_low", [P, 2, W], F32R)
        y_high = mb("y_high", [P, D], F32R)
        y_low = mb("y_low", [P, D], F32R)
        route = mb("route", [P, 14, TT, NE])
        route_c = mb("route_c", [P, 6, TT, 1])
        router = mb("router", [P, KB, NE])
        router_bias = mb("router_bias", [1, NE])
        most = mb("most", [P, 4])
        most_i = mb("most_i", [P, 1], I32)
        moe_mem.close()
        bank = [ctx.enter_context(nc.psum_tensor(f"bank{i}", [P, W], F32)) for i in range(8)]

        landed = [sem(f"landed_{i}") for i in range(RING)]
        s_x = sem("x_loaded")
        s_rows = sem("rows_loaded")
        s_blk = sem("blocks_loaded")
        s_ws = sem("ws_loaded")
        s_gate = sem("gate_bias_loaded")
        s_router = sem("router_loaded")
        high_made = sem("high_made")
        low_made = sem("low_made")
        unit_used = sem("unit_used")
        s_const = sem("constants_made")
        s_out = sem("out_stored")

        def steps(name):
            return Steps(sem(name), STEPS[name])

        pre_v, pre_a, pre_t = steps("pre_v"), steps("pre_a"), steps("pre_t")
        mod_v, mod_t, mod_e = steps("mod_v"), steps("mod_t"), steps("mod_e")
        gate_t, gate_v = steps("gate_t"), steps("gate_v")
        norm_v, norm_a, norm_t = steps("norm_v"), steps("norm_a"), steps("norm_t")
        mix_v, mix_a, mix_t = steps("mix_v"), steps("mix_a"), steps("mix_t")
        tri_d, tri_e, tri_q = steps("tri_d"), steps("tri_e"), steps("tri_q")
        chain_v = steps("chain_v")
        res_v = steps("res_v")
        ffn_v, ffn_a, ffn_t, ffn_w = steps("ffn_v"), steps("ffn_a"), steps("ffn_t"), steps("ffn_w")
        route_v, route_a, route_t = steps("route_v"), steps("route_a"), steps("route_t")
        slot_v, slot_t, slot_pos = steps("slot_v"), steps("slot_t"), steps("slot_pos")
        moe_v, moe_a, moe_t = steps("moe_v"), steps("moe_a"), steps("moe_t")
        fill_v, fill_a, sum_v = steps("fill_v"), steps("fill_a"), steps("sum_v")
        end_v, end_a = steps("end_v"), steps("end_a")

        def done(eng, ins, s, name, rep=0):
            s.said(name)
            eng.wait_ge(s.sem, s.at(name, rep))

        def mark(ins, s, name):
            s.said(name)

        def par(name, l, i=0, n=1):
            r = ROWS[name][0] + i
            return params[:, l, r:r + n]

        def mod_src(l, part, half):
            col = MOD_COL[part] * D + half * W
            return a["w_mod"][l].rearrange("(k p) n -> p k n", p=P)[:, :, col:col + W]

        def win_src(l, c):
            return a["w_in"][l].rearrange("(k p) n -> p k n", p=P)[:, :, c * W:min((c + 1) * W, 9 * G)]

        def wout_src(l, half):
            return a["w_out"][l].rearrange("(k p) n -> p k n", p=P)[:, :, half * W:(half + 1) * W]

        def ffn_src(kind, j):
            if kind == "w2":
                return a["ffn_w2"][0].rearrange("(b p) n -> p b n", p=P)[:, j * W // P:(j + 1) * W // P, :]
            return a[f"ffn_{kind}"][0].rearrange("(k p) n -> p k n", p=P)[:, :, j * W:(j + 1) * W]

        chunks = []

        def mod_chunks(l, part):
            for half in range(2):
                chunks.append((("mod", l, part, half), mod_src(l, part, half),
                               (mod_v, f"c{half}k{KB - 1}", 6 * l + MOD_PARTS.index(part))))

        def win_chunks(l):
            last = {3: "di", 2: "pg", 1: "pv", 4: "dg", 0: "pa"}
            for c in WIN_ORDER:
                chunks.append((("win", l, c), win_src(l, c), (mix_t, last[c], l)))

        def wout_chunks(l):
            for half in range(2):
                chunks.append((("wout", l, half), wout_src(l, half), (mix_t, "wout3", l)))

        mod_chunks(0, "sh1")
        mod_chunks(0, "sc1")
        win_chunks(0)
        mod_chunks(0, "sh2")
        mod_chunks(0, "sc2")
        wout_chunks(0)
        mod_chunks(0, "g1")
        mod_chunks(0, "g2")
        freed = {"w1": (ffn_t, "h1_1"), "w3": (ffn_t, "h3_1"), "w2": (ffn_w, "w")}
        mods = list(MOD_PARTS)
        for kind, j in FFN_ORDER:
            chunks.append((("ffn", kind, j), ffn_src(kind, j), (*freed[kind], j)))
            if kind == "w3" and mods:
                mod_chunks(1, mods.pop(0))
        win_chunks(1)
        wout_chunks(1)
        NPRE = len(chunks)
        number = {key: n for n, (key, _, _) in enumerate(chunks)}

        def slot(n):
            return ring[:, n % RING, :]

        def wide(key):
            cols = 9 * G - 4 * W if key[0] == "win" and key[2] == 4 else W
            return slot(number[key])[:, 0:KB * cols].rearrange("p (k n) -> p k n", n=cols)

        def arrived(eng, key):
            n = number[key]
            eng.wait_ge(landed[n % RING], 16 * (n // RING + 1))

        def moe_slot(u, i):
            return slot(NPRE + u * NCH + i)

        def moe_low(u, i):
            return ring_low[:, (NPRE + u * NCH + i) % RING, :]

        def moe_arrived(eng, q, g, u, i):
            n = NPRE + u * NCH + i
            turns = PAIR * NCH // RING
            eng.wait_ge(landed[n % RING], ((n // RING + 1) + turns * (q * (NE // PAIR) + g)) * 16)

        def unit_at(r, m):
            return r * UNITS + m + 1

        def used_at(r, m):
            return HIGHS + r * UNITS + m + 1

        def expert(q, g, u):
            return q * NE + g * PAIR + u

        block = ctx.enter_context(nc.Block())

        @block.sync
        def _(eng):
            for n, (key, src, _) in enumerate(chunks):
                if n >= RING:
                    s, name, rep = chunks[n - RING][2]
                    eng.wait_ge(s.sem, s.at(name, rep))
                if key[0] == "ffn" and key[1] == "w2":
                    dst = slot(n).rearrange("p (b n) -> p b n", n=D)
                else:
                    dst = wide(key)
                eng.dma_start(dst, src).then_inc(landed[n % RING], 16)

            def load_expert(q, g, u, i, g_src):
                n = u * NCH + i - RING
                if n >= 0:
                    eng.wait_ge(unit_used, used_at(expert(q, g, n // NCH), 2 * (n % NCH) + 1))
                elif q == 0 and g_src is None:
                    s, name, rep = chunks[NPRE + n][2]
                    eng.wait_ge(s.sem, s.at(name, rep))
                else:
                    eng.wait_ge(unit_used, used_at(expert(q, g - 1, PAIR - 1), 2 * (NCH + n) + 1))
                kind, j = FFN_ORDER[i]
                w = a[f"moe_{kind}"][0]
                e = 0 if g_src is None else g_src * PAIR
                we = w[bass.ds(e + u, 1)] if g_src is not None else w[u:u + 1]
                if kind == "w2":
                    src = we.rearrange("e (b p) n -> (e p) b n", p=P)[:, j * W // P:(j + 1) * W // P, :]
                    dst = moe_slot(u, i).rearrange("p (b n) -> p b n", n=D)
                else:
                    src = we.rearrange("e (k p) n -> (e p) k n", p=P)[:, :, j * W:(j + 1) * W]
                    dst = moe_slot(u, i).rearrange("p (k n) -> p k n", n=W)
                eng.dma_start(dst, src).then_inc(landed[(NPRE + u * NCH + i) % RING], 16)

            def load_pass(q):
                for i in range(RING):
                    load_expert(q, 0, 0, i, None)
                with eng.Fori(0, NE // PAIR - 1) as g:
                    for c in range(RING, PAIR * NCH):
                        load_expert(q, g, c // NCH, c % NCH, g)
                    for i in range(RING):
                        load_expert(q, g + 1, 0, i, g + 1)
                last = NE // PAIR - 1
                for c in range(RING, PAIR * NCH):
                    load_expert(q, last, c // NCH, c % NCH, last)

            load_pass(0)
            eng.wait_ge(route_v.sem, route_v.at("most_i"))
            with eng.If(eng.value_load(most_i[0:1, 0:1], min_val=0, max_val=T) > SLOTS):
                load_pass(1)
            for tt in range(TT):
                eng.wait_ge(end_v.sem, end_v.at(f"out{tt}"))
                eng.dma_start(out[0, tt * P:(tt + 1) * P, :], xn[:, tt, :]).then_inc(s_out, 16)
            eng.wait_ge(s_out, 16 * TT)

        @block.gpsimd
        def _(eng):
            eng.dma_start(x[:, :, :], a["x"][0].rearrange("(t p) d -> p t d", p=P)).then_inc(s_x, 16)
            per_l = (("norm_mix", a["norm_mix"]), ("norm_ffn", a["norm_ffn"]), ("pool_scale", a["pool_scale"]),
                     ("pool_out", a["pool_out_norm"]), ("sgu_out", a["sgu_out_norm"]), ("conv_b", a["conv_b"]),
                     ("lru_ba", a["lru_ba"]), ("lru_bx", a["lru_bx"]), ("lambda", a["lru_lambda"]),
                     ("lru_out", a["lru_out_norm"]), ("hgrn_out", a["hgrn_out_norm"]))
            n = 0
            for name, src in per_l:
                r, k = ROWS[name]
                eng.dma_start(prow[r:r + k, :, :], src.rearrange("l (r p) -> r l p", p=P)).then_inc(s_rows, 16)
                n += 1
            for l in range(DEPTH):
                r, k = ROWS["conv_w"]
                eng.dma_start(prow[r:r + k, l, :], a["conv_w"][l].rearrange("k (r p) -> (k r) p", p=P))\
                   .then_inc(s_rows, 16)
                r, k = ROWS["gamma"]
                eng.dma_start(prow[r:r + k, l, :], a["hgrn_gamma"].rearrange("l (r p) -> (l r) p", p=P))\
                   .then_inc(s_rows, 16)
                r, k = ROWS["c"]
                eng.dma_start(prow[r:r + k, l, :], a["c"].rearrange("o (r p) -> (o r) p", p=P)).then_inc(s_rows, 16)
                for part in ("sh1", "sc1", "sh2", "sc2"):
                    r, k = ROWS["b_" + part]
                    col = MOD_COL[part] * D
                    eng.dma_start(prow[r:r + k, l, :], a["b_mod"][l, col:col + D].rearrange("(r p) -> r p", p=P))\
                       .then_inc(s_rows, 16)
                    n += 1
                n += 3
            assert n == N_ROW_LOADS

            consts_made = 0

            def made(ins):
                nonlocal consts_made
                consts_made += 1
                ins.then_inc(s_const, 1)
                eng.wait_ge(s_const, consts_made)

            made(eng.memset(consts[:, :, :], 1.0))
            made(eng.affine_select(out=ident, in_=ident, compare_op=ALU.is_equal, fill=0.0, base=0,
                                   pattern=[[-1, P]], channel_multiplier=1))
            made(eng.affine_select(out=triu, in_=triu, compare_op=ALU.is_ge, fill=0.0, base=0,
                                   pattern=[[1, P]], channel_multiplier=-1))
            made(eng.affine_select(out=before, in_=before, compare_op=ALU.is_ge, fill=0.0, base=-1,
                                   pattern=[[1, P]], channel_multiplier=-1))
            made(eng.affine_select(out=head_ones[:, 0:HD], in_=head_ones[:, 0:HD], compare_op=ALU.is_ge, fill=0.0,
                                   base=HD - 1, pattern=[[0, HD]], channel_multiplier=-1))
            made(eng.affine_select(out=head_ones[:, HD:P], in_=head_ones[:, HD:P], compare_op=ALU.is_ge, fill=0.0,
                                   base=-HD, pattern=[[0, HD]], channel_multiplier=1))
            made(eng.iota(iota_f, [[1, P]], base=0, channel_multiplier=0, allow_small_or_imprecise_dtypes=True))
            made(eng.tensor_copy(head_sel[:, 0:1], head_ones[:, 0:1]))
            made(eng.tensor_copy(head_sel[:, 1:2], head_ones[:, HD:HD + 1]))
            made(eng.memset(eps_col[:, :], EPS))
            made(eng.memset(scan_keep[:, :], 1.0))
            made(eng.memset(scan_keep[:, 0:T:C], 0.0))
            made(eng.memset(chunk_of[:, :], 1.0))
            made(eng.affine_select(out=chunk_of[:, :], in_=chunk_of[:, :], compare_op=ALU.is_ge, fill=0.0, base=0,
                                   pattern=[[-C, CT_]], channel_multiplier=1))
            made(eng.affine_select(out=chunk_of[:, :], in_=chunk_of[:, :], compare_op=ALU.is_ge, fill=0.0,
                                   base=C - 1, pattern=[[C, CT_]], channel_multiplier=-1))
            made(eng.memset(row_sel[:, :, :], 1.0))
            made(eng.affine_select(out=row_sel[:, :, :], in_=row_sel[:, :, :], compare_op=ALU.is_ge, fill=0.0,
                                   base=HD - 1, pattern=[[-P, CB], [-1, P]], channel_multiplier=HD))
            made(eng.affine_select(out=row_sel[:, :, :], in_=row_sel[:, :, :], compare_op=ALU.is_ge, fill=0.0,
                                   base=0, pattern=[[P, CB], [1, P]], channel_multiplier=-HD))
            made(eng.memset(x_pad[:, :, :], 0.0))
            made(eng.memset(blocks[:, :, :, :], 0.0))
            made(eng.memset(tri[:, :, :, :], 0.0))
            made(eng.memset(state[:, :, 0, :], 0.0))
            pos = band_b[:, 0, 0:1]
            made(eng.memset(band_a[:, :, :], 1.0))
            for g, win in enumerate(WINDOWS):
                made(eng.memset(band_a[:, g, :], 1.0 / win))
                for t in range(win - 1):
                    made(eng.memset(band_a[:, g, t:t + 1], 1.0 / (t + 1)))
                made(eng.memset(band_b[:, g, :], 1.0 / win))
                for m, n in ((band_a[:, g, :], EDGE), (band_b[:, g, :], P)):
                    made(eng.affine_select(out=m, in_=m, compare_op=ALU.is_ge, fill=0.0, base=0,
                                           pattern=[[1, n]], channel_multiplier=-1))
                    made(eng.affine_select(out=m, in_=m, compare_op=ALU.is_ge, fill=0.0, base=win - 1,
                                           pattern=[[-1, n]], channel_multiplier=1))
                    made(eng.tensor_tensor(m[:, 0:P], m[:, 0:P], ident, ALU.subtract))
            assert consts_made == N_CONSTS

            for l in range(DEPTH):
                if l:
                    eng.wait_ge(mix_t.sem, mix_t.at("apool", l - 1))
                for k, w in enumerate((a["pool_w"], a["lru_wa"], a["lru_wx"])):
                    for q in range(2):
                        eng.dma_start(blocks[q * HD:(q + 1) * HD, k, :, q * HD:(q + 1) * HD],
                                      w[l].rearrange("(b q) i j -> q i b j", q=2)[q]).then_inc(s_blk, 16)
                if l:
                    eng.wait_ge(res_v.sem, res_v.at("r7", 2 * l - 1))
                    eng.wait_ge(mix_v.sem, mix_v.at("yd1", l - 1))
                else:
                    eng.wait_ge(pre_t.sem, pre_t.at("rows"))
                eng.dma_start(tmp[:, 13, :].rearrange("p (h s) -> p h s", h=NH),
                              a["sgu_ws"][l].rearrange("h t s -> t h s")).then_inc(s_ws, 16)
                eng.dma_start(sgu_bias[:, :], a["sgu_b"][l]).then_inc(s_ws, 16)
                eng.dma_start(gate_row[:, :], a["b_mod"][l:l + 1, 2 * D:3 * D].to_broadcast([P, D]))\
                   .then_inc(s_gate, 16)
                eng.wait_ge(res_v.sem, res_v.at("r7", 2 * l))
                eng.dma_start(gate_row[:, :], a["b_mod"][l:l + 1, 5 * D:6 * D].to_broadcast([P, D]))\
                   .then_inc(s_gate, 16)
            eng.dma_start(router[:, :, :], a["router_w"][0].rearrange("(k p) e -> p k e", p=P)).then_inc(s_router, 16)
            eng.dma_start(router_bias[:, :], a["router_b"][0:1, :]).then_inc(s_router, 16)
            eng.wait_ge(res_v.sem, res_v.at("r7", 2 * DEPTH - 1))
            eng.dma_start(gate_row[:, :], a["norm_final"].rearrange("(o d) -> o d", o=1).to_broadcast([P, D]))\
               .then_inc(s_gate, 16)

        @block.tensor
        def _(eng):
            mm = nc.tensor.matmul

            def row_sum_columns(l, part):
                n = MOD_PARTS.index(part)
                eng.wait_ge(mod_v.sem, mod_v.at(f"c1k{KB - 1}", 6 * l + n))
                b = bank[6] if l == 0 and n >= 2 else bank[0]
                if 4 * l + n > 0:
                    eng.wait_ge(mod_e.sem, mod_e.at("fin", 4 * l + n - 1))
                if l == 1:
                    eng.wait_ge(ffn_a.sem, ffn_a.at("s0", n + 1))
                for k in range(KB):
                    ins = mm(b[:, k:k + 1], mod_acc[:, n % 2, k * P:(k + 1) * P], ones[:, 0:1], start=True, stop=True)
                mark(ins.then_inc(mod_t.sem, 1), mod_t, "sum")

            def row_sum_wide(l, which, b):
                n = 4 + which
                eng.wait_ge(mod_v.sem, mod_v.at(f"c1k{KB - 1}", 6 * l + n))
                for half in range(2):
                    ins = mm(b[half][:, :], ones, mod_acc[:, n % 2, half * W:(half + 1) * W], start=True, stop=True)
                mark(ins.then_inc(gate_t.sem, 1), gate_t, "sum")

            def turn_xn(q):
                eng.wait_ge(norm_v.sem, norm_v.at("xn1", q))
                for b in range(4):
                    for i in range(2):
                        for tt in range(TT):
                            ins = nc.tensor.transpose(bank[4 + b][:, i * T + tt * P:i * T + (tt + 1) * P],
                                                      xn[:, tt, (2 * b + i) * P:(2 * b + i + 1) * P], ident)
                    mark(ins.then_inc(norm_t.sem, 1), norm_t, f"t{b}")

            def mixers(l):
                eng.wait_ge(s_ws, 32 * (l + 1))
                for h in range(NH):
                    ins = nc.tensor.transpose(bank[3][:, h * P:(h + 1) * P], tmp[:, 13, h * P:(h + 1) * P], ident)
                mark(ins.then_inc(mix_t.sem, 1), mix_t, "ws")

                free = {"px": (mix_a, "sig"), "pg": (mix_v, "v"), "pv": (mix_a, "q"), "dg": (mix_a, "xp"),
                        "pu": (mix_a, "gate_c"), "pa": (mix_a, "gv1")}

                def project(name):
                    b = bank[GROUPS.index(name) % 3]
                    c, off = COLS[name] // W, COLS[name] % W
                    arrived(eng, ("win", l, c))
                    if name in free:
                        s, reader = free[name]
                        eng.wait_ge(s.sem, s.at(reader, l))
                    w = wide(("win", l, c))
                    for i in range(2):
                        for k in range(KB):
                            if name in ("di", "pv", "pa"):
                                ins = mm(b[:, i * G:(i + 1) * G], h_t[:, k, i * P:(i + 1) * P], w[:, k, off:off + G],
                                         start=k == 0, stop=k == KB - 1)
                            else:
                                ins = mm(b[:, i * T:(i + 1) * T], w[:, k, off + i * P:off + (i + 1) * P], h_t[:, k, :],
                                         start=k == 0, stop=k == KB - 1)
                    mark(ins.then_inc(mix_t.sem, 1), mix_t, name)

                def channel_sum(b, src, name):
                    for i in range(CB):
                        ins = mm(b[:, 0:T], ones, src[:, i * T:(i + 1) * T], start=i == 0, stop=i == CB - 1)
                    mark(ins.then_inc(mix_t.sem, 1), mix_t, name)

                eng.wait_ge(norm_a.sem, norm_a.at("h5", 2 * l))
                eng.wait_ge(norm_v.sem, norm_v.at("h7", 2 * l))
                project("dfz")
                project("di")
                project("dq")
                eng.wait_ge(mix_a.sem, mix_a.at("kh", l))
                for tt in range(TT):
                    for i in range(CB):
                        ins = nc.tensor.transpose(bank[4][:, tt * G + i * P:tt * G + (i + 1) * P],
                                                  tmp[:, 4, i * T + tt * P:i * T + (tt + 1) * P], ident)
                mark(ins.then_inc(mix_t.sem, 1), mix_t, "kt")
                project("px")
                eng.wait_ge(mix_a.sem, mix_a.at("kt", l))
                for n, (i, tt, q) in enumerate((i, tt, q) for i in range(CB) for tt in range(TT) for q in range(2)):
                    h = 2 * i + q
                    eng.wait_ge(mix_v.sem, mix_v.at(f"vx{n}", l))
                    b = bank[6 + tt] if i == 0 else bank[4 + tt]
                    ins = mm(b[q * HD:(q + 1) * HD, :], tmp[:, 5, tt * G + h * HD:tt * G + (h + 1) * HD],
                             v_wide[:, n % 2, :], start=True, stop=True)
                    mark(ins.then_inc(mix_t.sem, 1), mix_t, f"u{n}")
                project("pg")
                project("pv")
                eng.wait_ge(mix_v.sem, mix_v.at("xc1", l))
                eng.wait_ge(s_blk, 96 * (l + 1))
                eng.wait_ge(chain_v.sem, chain_v.at("s", l * CHAIN + CHAIN - 1))
                for k, name in ((1, "wa"), (2, "wx")):
                    for i in range(CB):
                        ins = mm(bank[3 + k][:, i * T:(i + 1) * T], blocks[:, k, i, :], tmp[:, 7, i * T:(i + 1) * T],
                                 start=True, stop=True)
                    mark(ins.then_inc(mix_t.sem, 1), mix_t, name)
                def scores(i):
                    for r in range(C):
                        eng.wait_ge(tri_q.sem, tri_q.at("q", (l * CB + i) * C + r))
                        for tt in range(TT):
                            c0 = (tt * CB + i) * 2 * C
                            ins = mm(bank[6][:, c0 + r:c0 + 2 * C:C],
                                     tri[:, r, tt * CT_:(tt + 1) * CT_, :].rearrange("p i s -> p (i s)"),
                                     head_sel[:, :], start=True, stop=True)
                    mark(ins.then_inc(mix_t.sem, 1), mix_t, f"sc{i}")

                scores(0)
                project("dg")
                project("pu")
                project("pa")
                scores(1)
                eng.wait_ge(mix_v.sem, mix_v.at("wst", l))
                for tt in range(TT):
                    eng.wait_ge(mix_v.sem, mix_v.at(f"sf{tt}", l))
                    for h in range(NH):
                        q, i = h % 2, h // 2
                        mm(bank[3][q * HD:(q + 1) * HD, i * T + tt * P:i * T + (tt + 1) * P],
                           tmp[:, 6, tt * G + h * HD:tt * G + (h + 1) * HD], s_full[:, tt, h, :],
                           start=tt == 0 and i == 0, stop=False, skip_group_check=True)
                eng.wait_ge(mix_v.sem, mix_v.at("qt", l))
                for h in range(NH):
                    q, i = h % 2, h // 2
                    for c in range(1, NC):
                        ins = mm(bank[3][q * HD:(q + 1) * HD, i * T + c * C:i * T + (c + 1) * C],
                                 state[q * HD:(q + 1) * HD, i, c, :],
                                 tmp[q * HD:(q + 1) * HD, 3, i * T + c * C:i * T + (c + 1) * C],
                                 start=False, stop=h >= 2 and c == NC - 1, skip_group_check=True)
                mark(ins.then_inc(mix_t.sem, 1), mix_t, "o")
                eng.wait_ge(mix_v.sem, mix_v.at("vn1", l))
                eng.wait_ge(mix_v.sem, mix_v.at("wst", l))
                eng.wait_ge(mix_a.sem, mix_a.at("r1", l))
                for tt in range(TT):
                    for i in range(CB):
                        mm(bank[4][:, i * T + tt * P:i * T + (tt + 1) * P], row_sel[:, i, :], sgu_bias[:, :],
                           start=tt == 0 and i == 0, stop=False, skip_group_check=True)
                for tt in range(TT):
                    for h in range(NH):
                        q, i = h % 2, h // 2
                        ins = mm(bank[4][q * HD:(q + 1) * HD, i * T + tt * P:i * T + (tt + 1) * P],
                                 tmp[:, 4, tt * G + h * HD:tt * G + (h + 1) * HD], ws_t[:, h, :],
                                 start=False, stop=True, skip_group_check=True)
                mark(ins.then_inc(mix_t.sem, 1), mix_t, "z")
                eng.wait_ge(mix_a.sem, mix_a.at("sqd", l))
                eng.wait_ge(chain_v.sem, chain_v.at("s", l * CHAIN + CHAIN - 1))
                mark(mm(bank[7][:, :], head_ones, tmp[:, 2, :], start=True, stop=True).then_inc(mix_t.sem, 1),
                     mix_t, "ssd")
                eng.wait_ge(mix_a.sem, mix_a.at("sqc", l))
                eng.wait_ge(mix_a.sem, mix_a.at("i1", l))
                channel_sum(bank[5], tmp[:, 8, :], "ssc")
                eng.wait_ge(mix_a.sem, mix_a.at("pa", l))
                eng.wait_ge(mix_v.sem, mix_v.at("sf1", l))
                for g in range(NH):
                    q, i = g % 2, g // 2
                    mm(bank[6][q * HD:(q + 1) * HD, i * T:i * T + EDGE], tmp[:, 11, g * HD:(g + 1) * HD],
                       band_a[:, g, :], start=i == 0, stop=False, skip_group_check=True)
                    ins = mm(bank[6][q * HD:(q + 1) * HD, i * T + P:(i + 1) * T],
                             tmp[:, 11, G + g * HD:G + (g + 1) * HD], band_b[:, g, :],
                             start=False, stop=True, skip_group_check=True)
                mark(ins.then_inc(mix_t.sem, 1), mix_t, "aband")
                eng.wait_ge(mix_a.sem, mix_a.at("sqb", l))
                eng.wait_ge(mix_a.sem, mix_a.at("rtd", l))
                channel_sum(bank[7], tmp[:, 4, :], "ssb")
                eng.wait_ge(mix_a.sem, mix_a.at("pd", l))
                eng.wait_ge(mix_v.sem, mix_v.at("yb_raw", l))
                for i in range(CB):
                    ins = mm(bank[4][:, i * T:(i + 1) * T], blocks[:, 0, i, :], tmp[:, 6, i * T:(i + 1) * T],
                             start=True, stop=True)
                mark(ins.then_inc(mix_t.sem, 1), mix_t, "apool")
                eng.wait_ge(mix_a.sem, mix_a.at("sqa", l))
                eng.wait_ge(mix_a.sem, mix_a.at("rtc", l))
                channel_sum(bank[5], tmp[:, 1, :], "ssa")
                for half in range(2):
                    arrived(eng, ("wout", l, half))
                for name in ("gate_d", "gu", "pa"):
                    eng.wait_ge(mix_a.sem, mix_a.at(name, l))
                eng.wait_ge(mix_v.sem, mix_v.at("od", l))
                for n, (name, g) in enumerate((("yc1", 2), ("yd1", 3), ("yb1", 1), ("ya1", 0))):
                    eng.wait_ge(mix_v.sem, mix_v.at(name, l))
                    for tt in range(TT):
                        for half in range(2):
                            for i in range(2 * g, 2 * g + 2):
                                ins = mm(bank[2 * tt + half][:, :], y_t[:, i, tt * P:(tt + 1) * P],
                                         wide(("wout", l, half))[:, i, :], start=n == 0 and i == 2 * g,
                                         stop=n == 3 and i == 2 * g + 1)
                            if n == 3:
                                mark(ins.then_inc(mix_t.sem, 1), mix_t, f"wout{2 * tt + half}")
                if l == 0:
                    row_sum_columns(0, "sh2")
                    row_sum_columns(0, "sc2")
                eng.wait_ge(mix_v.sem, mix_v.at("ya1", l))
                row_sum_wide(l, 0, (bank[5], bank[7]))

            def ffn():
                for j in range(NJ + 1):
                    if j < NJ:
                        for i in range(2):
                            for name, b, (s, ev) in (("w1", bank[i], (ffn_a, f"s{i}")),
                                                     ("w3", bank[2 + i], (ffn_v, f"a{i}"))):
                                arrived(eng, ("ffn", name, j))
                                if j:
                                    eng.wait_ge(s.sem, s.at(ev, j - 1))
                                if name == "w1" and i == 0 and 2 <= j:
                                    if j - 2 < 4:
                                        eng.wait_ge(mod_e.sem, mod_e.at("fin", 4 + j - 2))
                                w = wide(("ffn", name, j))
                                for hb in range(2):
                                    for k in range(KB):
                                        c = (2 * i + hb) * P
                                        ins = mm(b[:, hb * T:(hb + 1) * T], w[:, k, c:c + P], h_t[:, k, :],
                                                 start=k == 0, stop=k == KB - 1)
                                mark(ins.then_inc(ffn_t.sem, 1), ffn_t, f"h{name[1]}_{i}")
                        if 1 <= j <= 4:
                            row_sum_columns(1, MOD_PARTS[j - 1])
                    if j:
                        jj = j - 1
                        arrived(eng, ("ffn", "w2", jj))
                        eng.wait_ge(ffn_v.sem, ffn_v.at("a1", jj))
                        w = slot(number[("ffn", "w2", jj)]).rearrange("p (b n) -> p b n", n=D)
                        at = tmp[:, 2 + 2 * (jj % 2):4 + 2 * (jj % 2), :].rearrange("p a (b t) -> p (a b) t", t=T)
                        for tt in range(TT):
                            for half in range(2):
                                for hb in range(W // P):
                                    ins = mm(bank[4 + 2 * tt + half][:, :], at[:, hb, tt * P:(tt + 1) * P],
                                             w[:, hb, half * W:(half + 1) * W], start=jj == 0 and hb == 0,
                                             stop=jj == NJ - 1 and hb == W // P - 1)
                        mark(ins.then_inc(ffn_w.sem, 1), ffn_w, "w")

            def routing():
                eng.wait_ge(s_router, 32)
                for tt in range(TT):
                    for k in range(KB):
                        ins = mm(bank[2][:, tt * NE:(tt + 1) * NE], h_t[:, k, tt * P:(tt + 1) * P], router[:, k, :],
                                 start=k == 0, stop=False)
                        if tt == 0 and k < HIGHS:
                            ins.then_inc(unit_used, 1)
                    ins = mm(bank[2][:, tt * NE:(tt + 1) * NE], ones[0:1, :], router_bias[:, :], start=False, stop=True)
                mark(ins.then_inc(route_t.sem, 1), route_t, "logits")
                eng.wait_ge(route_v.sem, route_v.at("sel", 0))
                mm(bank[2][:, 64:64 + NE], before, route[:, 8, 0, :], start=True, stop=True)
                mm(bank[2][:, 64 + NE:64 + 2 * NE], ones, route[:, 8, 0, :], start=True, stop=False)
                mm(bank[2][:, 64 + NE:64 + 2 * NE], before, route[:, 8, 1, :], start=False, stop=True)
                mm(bank[2][:, 64 + 2 * NE:64 + 3 * NE], ones, route[:, 8, 0, :], start=True, stop=False)
                ins = mm(bank[2][:, 64 + 2 * NE:64 + 3 * NE], ones, route[:, 8, 1, :], start=False, stop=True)
                mark(ins.then_inc(route_t.sem, 1), route_t, "pos")
                eng.wait_ge(gate_v.sem, gate_v.at("g1", 2 * DEPTH - 1))

            def gather(b, u, first, name, s):
                for k in range(4):
                    for tt in range(TT):
                        ins = mm(b[:, k * P:(k + 1) * P], xn[:, tt, (first + k) * P:(first + k + 1) * P],
                                 dispatch[:, u, tt, :], start=tt == 0, stop=tt == TT - 1)
                mark(ins.then_inc(s.sem, 1), s, name)

            def experts(q):
                eng.wait_ge(slot_v.sem, slot_v.at("disp", q))
                gather(bank[4], 0, 0, "g0", slot_t)
                gather(bank[5], 0, 4, "g1", slot_t)
                with eng.Fori(0, NE // PAIR) as g:
                    for u in range(PAIR):
                        one_expert(q, g, u)

            def one_expert(q, g, u):
                r = expert(q, g, u)
                fill = q * (NE + 1) + g * PAIR + u

                def three(out_, x_h, x_l, w_h, w_l, first, last):
                    mm(out_, x_h, w_h, start=first, stop=False)
                    mm(out_, x_h, w_l, start=False, stop=False)
                    return mm(out_, x_l, w_h, start=False, stop=last)

                def up(j, name, b):
                    i = FFN_ORDER.index((name, j))
                    w_l = moe_low(u, i).rearrange("p (k n) -> p k n", n=W)
                    for part in range(2):
                        m = 2 * i + part
                        w_h = w_high[:, m % HIGHS, :].rearrange("p (k n) -> p k n", n=W)
                        eng.wait_ge(low_made, unit_at(r, m))
                        for kk in range(KB // 2):
                            k = part * KB // 2 + kk
                            ins = three(b[:, :], x_high[:, u % 2, k, :], x_low[:, u % 2, k, :], w_h[:, kk, :],
                                        w_l[:, k, :], k == 0, k == KB - 1)
                        ins.then_inc(unit_used, 1)

                def turn(j):
                    eng.wait_ge(moe_v.sem, moe_v.at(f"m{j}", r))
                    if j == 0:
                        eng.wait_ge(sum_v.sem, sum_v.at("a2", r))
                    if j:
                        eng.wait_ge(moe_v.sem, moe_v.at(f"al{j - 1}", r))
                    for hb in range(W // P):
                        ins = nc.tensor.transpose(bank[6][:, hb * P:(hb + 1) * P],
                                                  act_m[:, j % 2, hb * P:(hb + 1) * P], ident)
                    mark(ins.then_inc(moe_t.sem, 1), moe_t, f"t{j}")

                def down(j):
                    i = FFN_ORDER.index(("w2", j))
                    eng.wait_ge(moe_v.sem, moe_v.at(f"al{j}", r))
                    w_l = moe_low(u, i).rearrange("p (b n) -> p b n", n=D)
                    for part in range(2):
                        m = 2 * i + part
                        w_h = w_high[:, m % HIGHS, :].rearrange("p (b n) -> p b n", n=D)
                        eng.wait_ge(low_made, unit_at(r, m))
                        for half in range(2):
                            c = slice(half * W, (half + 1) * W)
                            for bb in range(HB // 2):
                                hb = part * HB // 2 + bb
                                h = slice(hb * P, (hb + 1) * P)
                                ins = three(bank[4 + half][:, :], act_high[:, j % 2, h], act_low[:, j % 2, h],
                                            w_h[:, bb, c], w_l[:, hb, c], j == 0 and hb == 0,
                                            j == NJ - 1 and hb == HB - 1)
                        ins.then_inc(unit_used, 1)

                for j in range(NJ):
                    if j == 0:
                        eng.wait_ge(fill_v.sem, fill_v.at("lb", fill))
                    if j == 1:
                        eng.wait_ge(sum_v.sem, sum_v.at("a1", r))
                    if j >= 2:
                        eng.wait_ge(moe_a.sem, moe_a.at(f"s{j - 2}", r))
                    up(j, "w1", bank[j % 2])
                    if j:
                        turn(j - 1)
                    if j == 1:
                        eng.wait_ge(sum_v.sem, sum_v.at("a3", r))
                        for tt in range(TT):
                            ins = nc.tensor.transpose(bank[7][:, tt * P:(tt + 1) * P], dispatch[:, u, tt, :], ident)
                        mark(ins.then_inc(moe_t.sem, 1), moe_t, "spread")
                    if j == GATHER:
                        eng.wait_ge(moe_v.sem, moe_v.at("disp", r))
                        eng.wait_ge(moe_a.sem, moe_a.at("spread", r))
                        gather(bank[7], (u + 1) % 2, 0, "ga", moe_t)
                    if j == GATHER + 1:
                        eng.wait_ge(fill_a.sem, fill_a.at("x3", fill + 1))
                        gather(bank[7], (u + 1) % 2, 4, "gb", moe_t)
                    if j >= 2:
                        eng.wait_ge(moe_v.sem, moe_v.at(f"m{j - 2}", r))
                    up(j, "w3", bank[2 + j % 2])
                    if j:
                        down(j - 1)
                turn(NJ - 1)
                down(NJ - 1)
                eng.wait_ge(moe_a.sem, moe_a.at("yh0", r))
                eng.wait_ge(moe_v.sem, moe_v.at("yl1", r))
                for n, b in enumerate((1, 3, 6, 7)):
                    tt, half = n // 2, n % 2
                    if b == 7:
                        eng.wait_ge(fill_a.sem, fill_a.at("x7", fill + 1))
                    mm(bank[b][:, :], spread[:, tt * P:(tt + 1) * P], y_high[:, half * W:(half + 1) * W],
                       start=True, stop=False)
                    mark(mm(bank[b][:, :], spread[:, tt * P:(tt + 1) * P], y_low[:, half * W:(half + 1) * W],
                            start=False, stop=True).then_inc(moe_t.sem, 1), moe_t, f"c{n}")

            eng.wait_ge(s_const, N_CONSTS)
            eng.wait_ge(s_rows, 16 * N_ROW_LOADS)
            for l in range(DEPTH):
                ins = nc.tensor.transpose(bank[7][:, l * P:l * P + NROWS], prow[:, l, :], ident[0:NROWS, 0:NROWS])
            mark(ins.then_inc(pre_t.sem, 1), pre_t, "rows")
            row_sum_columns(0, "sh1")
            row_sum_columns(0, "sc1")
            for l in range(DEPTH):
                turn_xn(2 * l)
                mixers(l)
                turn_xn(2 * l + 1)
                if l == 0:
                    row_sum_wide(l, 1, (bank[0], bank[1]))
                    eng.wait_ge(gate_v.sem, gate_v.at("g1", 2 * l + 1))
                    eng.wait_ge(norm_a.sem, norm_a.at("h5", 2 * l + 1))
                    eng.wait_ge(norm_v.sem, norm_v.at("h7", 2 * l + 1))
                    ffn()
            row_sum_wide(1, 1, (bank[0], bank[1]))
            eng.wait_ge(norm_a.sem, norm_a.at("h5", 3))
            eng.wait_ge(norm_v.sem, norm_v.at("h7", 3))
            routing()
            experts(0)
            eng.wait_ge(route_v.sem, route_v.at("most_i"))
            with eng.If(eng.value_load(most_i[0:1, 0:1], min_val=0, max_val=T) > SLOTS):
                experts(1)

        def rows2(ap):
            return ap.rearrange("p (b t) -> p b t", b=CB)

        @block.vector
        def _(eng):
            tt_, ts_, stt = nc.vector.tensor_tensor, nc.vector.tensor_scalar, nc.vector.scalar_tensor_tensor

            def mod_part(l, part):
                n = MOD_PARTS.index(part)
                rep = 6 * l + n
                if n >= 2:
                    eng.wait_ge(mod_t.sem, mod_t.at("sum", 4 * l + n - 2))
                elif l:
                    eng.wait_ge(gate_t.sem, gate_t.at("sum", 2 * (l - 1) + n))
                for half in range(2):
                    key = ("mod", l, part, half)
                    arrived(eng, key)
                    dst = mod_acc[:, n % 2, half * W:(half + 1) * W]
                    for k in range(KB):
                        if k == 0:
                            ins = ts_(dst, wide(key)[:, 0, :], c_act[:, 0:1], None, ALU.mult)
                        else:
                            ins = stt(out=dst, in0=wide(key)[:, k, :], scalar=c_act[:, k:k + 1], in1=dst,
                                      op0=ALU.mult, op1=ALU.add)
                        done(eng, ins.then_inc(mod_v.sem, 1), mod_v, f"c{half}k{k}", rep)

            def mod_columns(l, part):
                n = MOD_PARTS.index(part)
                rep = 4 * l + n
                eng.wait_ge(mod_t.sem, mod_t.at("sum", rep))
                b = bank[6] if l == 0 and n >= 2 else bank[0]
                bias = par("b_" + part, l, 0, KB)
                gain = par("norm_mix" if n < 2 else "norm_ffn", l, 0, KB)
                if part.startswith("sh"):
                    done(eng, tt_(mod_tmp[:, :], b[:, 0:KB], bias, ALU.add).then_inc(mod_e.sem, 1), mod_e, "add", rep)
                    done(eng, nc.vector.tensor_copy(mod_col[:, rep, :], mod_tmp[:, :]).then_inc(mod_e.sem, 1),
                         mod_e, "fin", rep)
                else:
                    done(eng, stt(out=mod_tmp[:, :], in0=b[:, 0:KB], scalar=1.0, in1=bias, op0=ALU.add, op1=ALU.add).then_inc(mod_e.sem, 1),
                         mod_e, "add", rep)
                    done(eng, tt_(mod_col[:, rep, :], mod_tmp[:, :], gain, ALU.mult).then_inc(mod_e.sem, 1),
                         mod_e, "fin", rep)

            def gate(l, which, b):
                rep = 2 * l + which
                eng.wait_ge(s_gate, 16 * (rep + 1))
                eng.wait_ge(gate_t.sem, gate_t.at("sum", rep))
                for half in range(2):
                    g = gate_row[:, half * W:(half + 1) * W]
                    done(eng, tt_(g, b[half][:, :], g, ALU.add).then_inc(gate_v.sem, 1), gate_v, f"g{half}", rep)

            def norm(q):
                eng.wait_ge(norm_a.sem, norm_a.at("rt", q))
                done(eng, nc.vector.reciprocal(norm_s[:, 2, :], norm_s[:, 1, :]).then_inc(norm_v.sem, 1),
                     norm_v, "rc", q)
                for tt in range(TT):
                    done(eng, ts_(xn[:, tt, :], x[:, tt, :], norm_s[:, 2, tt:tt + 1], None, ALU.mult).then_inc(norm_v.sem, 1),
                         norm_v, f"xn{tt}", q)
                for b in (1, 3):
                    eng.wait_ge(norm_t.sem, norm_t.at(f"t{b}", q))
                    for i in range(2):
                        k = 2 * b + i
                        done(eng, ts_(h_t[:, k, :], bank[4 + b][:, i * T:(i + 1) * T],
                                      mod_col[:, 2 * q + 1, k:k + 1], mod_col[:, 2 * q, k:k + 1], ALU.mult, ALU.add).then_inc(norm_v.sem, 1),
                             norm_v, f"h{k}", q)

            def residual(rep, src, waits):
                t = h_t[:, 0:2, :].rearrange("p k t -> p (k t)") if rep < 3 else act_s[:, 0, :]
                for n in range(4):
                    tt, half = n // 2, n % 2
                    for s, name, last in waits[n]:
                        eng.wait_ge(s.sem, s.at(name, last))
                    c = slice(half * W, (half + 1) * W)
                    done(eng, tt_(t, src[n], gate_row[:, c], ALU.mult).then_inc(res_v.sem, 1),
                         res_v, f"r{2 * n}", rep)
                    done(eng, tt_(x[:, tt, c], x[:, tt, c], t, ALU.add).then_inc(res_v.sem, 1),
                         res_v, f"r{2 * n + 1}", rep)

            def mixers(l):
                def v(ins, name):
                    done(eng, ins, mix_v, name, l)

                def t(i):
                    return tmp[:, i, :]

                eng.wait_ge(mix_t.sem, mix_t.at("ws", l))
                v(tt_(ws_t[:, :, :], bank[3][:, :].rearrange("p (h n) -> p h n", h=NH),
                      triu.unsqueeze(1).to_broadcast([P, NH, P]), ALU.mult).then_inc(mix_v.sem, 1), "wst")
                eng.wait_ge(mix_a.sem, mix_a.at("sig", l))
                for i in range(CB):
                    c = slice(i * T, (i + 1) * T)
                    v(ts_(t(1)[:, c], t(0)[:, c], floor_col[:, l, 1, i:i + 1], floor_col[:, l, 0, i:i + 1],
                          ALU.mult, ALU.add).then_inc(mix_v.sem, 1), f"f{i}")
                for i in range(CB):
                    c = slice(i * T, (i + 1) * T)
                    v(ts_(t(2)[:, c], t(0)[:, c], floor_col[:, l, 2, i:i + 1], floor_col[:, l, 1, i:i + 1],
                          ALU.mult, ALU.add).then_inc(mix_v.sem, 1), f"k{i}")
                v(ts_(t(3), t(1), LN_FLOOR, None, ALU.max).then_inc(mix_v.sem, 1), "fa")
                v(ts_(t(4), t(1), MIN_FORGET, LN_FLOOR, ALU.max, ALU.min).then_inc(mix_v.sem, 1), "fb")
                v(ts_(t(2), t(2), LN_FLOOR, None, ALU.max).then_inc(mix_v.sem, 1), "kc")
                eng.wait_ge(mix_a.sem, mix_a.at("lnb", l))
                v(tt_(t(3), t(3), t(4), ALU.add).then_inc(mix_v.sem, 1), "lf")
                for i in range(CB):
                    c = slice(i * T, (i + 1) * T)
                    v(nc.vector.tensor_tensor_scan(t(1)[:, c], scan_keep[:, :], t(3)[:, c], 0.0, ALU.mult, ALU.add).then_inc(mix_v.sem, 1),
                      f"b{i}")
                eng.wait_ge(mix_a.sem, mix_a.at("lnk", l))
                v(tt_(t(2), t(1), t(2), ALU.subtract).then_inc(mix_v.sem, 1), "bk")
                b4 = t(1).rearrange("p (n s) -> p n s", s=C)
                bk4 = t(2).rearrange("p (n s) -> p n s", s=C)
                v(tt_(t(4).rearrange("p (n s) -> p n s", s=C), b4[:, :, C - 1:C].to_broadcast([P, CB * NC, C]), bk4,
                      ALU.subtract).then_inc(mix_v.sem, 1), "kd")

                def differences(i):
                    for r in range(C):
                        rep = (l * CB + i) * C + r
                        if i or l:
                            if i:
                                eng.wait_ge(mix_t.sem, mix_t.at(f"sc{i - 1}", l))
                            else:
                                eng.wait_ge(mix_t.sem, mix_t.at(f"sc{CB - 1}", l - 1))
                        n = slice(i * NC, (i + 1) * NC)
                        done(eng, tt_(tri[:, r, :, 0:r + 1], b4[:, n, r:r + 1].to_broadcast([P, NC, r + 1]),
                                      bk4[:, n, 0:r + 1], ALU.subtract).then_inc(tri_d.sem, 1), tri_d, "d", rep)

                def times_q(i):
                    q4 = t(0).rearrange("p (n s) -> p n s", s=C)
                    for r in range(C):
                        rep = (l * CB + i) * C + r
                        eng.wait_ge(tri_e.sem, tri_e.at("e", rep))
                        n = slice(i * NC, (i + 1) * NC)
                        done(eng, tt_(tri[:, r, :, 0:r + 1], tri[:, r, :, 0:r + 1],
                                      q4[:, n, r:r + 1].to_broadcast([P, NC, r + 1]), ALU.mult).then_inc(tri_q.sem, 1),
                             tri_q, "q", rep)

                def values_by_chunk(n):
                    i, tt, q = n // (2 * TT), n // 2 % TT, n % 2
                    h = 2 * i + q
                    if n >= 2:
                        eng.wait_ge(mix_t.sem, mix_t.at(f"u{n - 2}", l))
                    src = t(6)[:, tt * G + h * HD:tt * G + (h + 1) * HD]
                    v(tt_(v_wide[:, n % 2, :].rearrange("p (j c) -> p j c", j=CT_),
                          src.unsqueeze(1).to_broadcast([P, CT_, HD]),
                          chunk_of[:, :].unsqueeze(2).to_broadcast([P, CT_, HD]), ALU.mult).then_inc(mix_v.sem, 1),
                      f"vx{n}")

                eng.wait_ge(mix_t.sem, mix_t.at("di", l))
                v(nc.vector.tensor_copy(t(6), bank[1][:, :]).then_inc(mix_v.sem, 1), "v")
                differences(0)
                values_by_chunk(0)
                values_by_chunk(1)
                eng.wait_ge(mix_a.sem, mix_a.at("q", l))
                times_q(0)
                for n in range(2, 8):
                    values_by_chunk(n)
                eng.wait_ge(mix_a.sem, mix_a.at("xp", l))
                for i in range(CB):
                    c = slice(i * T, (i + 1) * T)
                    v(ts_(t(7)[:, c], x_pad[:, i, 0:T], par("conv_w", l, i), par("conv_b", l, i), ALU.mult, ALU.add).then_inc(mix_v.sem, 1),
                      f"cv{i}0")
                    for k in range(1, CONV):
                        v(stt(out=t(7)[:, c], in0=x_pad[:, i, k:k + T], scalar=par("conv_w", l, k * CB + i),
                              in1=t(7)[:, c], op0=ALU.mult, op1=ALU.add).then_inc(mix_v.sem, 1),
                          f"cv{i}{k}" if k < CONV - 1 else f"xc{i}")
                eng.wait_ge(mix_a.sem, mix_a.at("ea", l))
                eng.wait_ge(mix_t.sem, mix_t.at("u7", l))
                if l:
                    eng.wait_ge(mix_t.sem, mix_t.at("o", l - 1))
                ea = small[:, 8:12, :].rearrange("p a b -> p (a b)")
                for c in range(NC - 1):
                    for i in range(CB):
                        u = bank[(6 if i == 0 else 4) + c // CT_][:, (c % CT_) * HD:(c % CT_ + 1) * HD]
                        done(eng, stt(out=state[:, i, c + 1, :], in0=state[:, i, c, :],
                                      scalar=ea[:, i * NC + c:i * NC + c + 1], in1=u, op0=ALU.mult, op1=ALU.add).then_inc(chain_v.sem, 1),
                             chain_v, "s", l * CHAIN + c * CB + i)
                v(tt_(t(3), t(3), t(0), ALU.mult).then_inc(mix_v.sem, 1), "qt")
                differences(1)
                times_q(1)
                eng.wait_ge(mix_a.sem, mix_a.at("a1", l))
                v(tt_(t(11), t(10), t(10), ALU.mult).then_inc(mix_v.sem, 1), "a2")
                eng.wait_ge(mix_a.sem, mix_a.at("th1", l))
                v(stt(out=t(11), in0=t(11), scalar=1.0, in1=t(8), op0=ALU.add, op1=ALU.mult).then_inc(mix_v.sem, 1),
                  "m")
                v(ts_(t(11), t(11), 0.0, None, ALU.max).then_inc(mix_v.sem, 1), "m0")
                v(tt_(t(9), t(9), t(7), ALU.mult).then_inc(mix_v.sem, 1), "ix")
                eng.wait_ge(mix_a.sem, mix_a.at("sm", l))
                v(tt_(t(9), t(11), t(9), ALU.mult).then_inc(mix_v.sem, 1), "bb")
                for i in range(CB):
                    c = slice(i * T, (i + 1) * T)
                    v(nc.vector.tensor_tensor_scan(t(8)[:, c], t(10)[:, c], t(9)[:, c], 0.0, ALU.mult, ALU.add).then_inc(mix_v.sem, 1),
                      f"hs{i}")
                v(tt_(t(12), t(12), t(8), ALU.mult).then_inc(mix_v.sem, 1), "yc_raw")
                eng.wait_ge(mix_t.sem, mix_t.at("u7", l))
                eng.wait_ge(mix_t.sem, mix_t.at("sc1", l))
                for tt in range(TT):
                    sc = bank[6][:, tt * NH * C:(tt + 1) * NH * C].rearrange("p (h r) -> p h r", r=C)
                    v(tt_(s_full[:, tt, :, :].rearrange("p h (j r) -> p h j r", r=C),
                          sc.unsqueeze(2).to_broadcast([P, NH, CT_, C]),
                          chunk_of[:, :].unsqueeze(1).unsqueeze(3).to_broadcast([P, NH, CT_, C]), ALU.mult).then_inc(mix_v.sem, 1),
                      f"sf{tt}")
                eng.wait_ge(mix_a.sem, mix_a.at("gv1", l))
                v(ts_(small[:, 1, 0:2], small[:, 0, 0:2], -1.0 / G, None, ALU.mult).then_inc(mix_v.sem, 1), "mu")
                for tt in range(TT):
                    c = slice(tt * G, (tt + 1) * G)
                    v(ts_(t(4)[:, c], t(4)[:, c], small[:, 1, tt:tt + 1], None, ALU.add).then_inc(mix_v.sem, 1),
                      f"vc{tt}")
                eng.wait_ge(mix_a.sem, mix_a.at("rv", l))
                v(nc.vector.reciprocal(small[:, 4, 0:2], small[:, 3, 0:2]).then_inc(mix_v.sem, 1), "rvr")
                for tt in range(TT):
                    c = slice(tt * G, (tt + 1) * G)
                    v(ts_(t(4)[:, c], t(4)[:, c], small[:, 4, tt:tt + 1], None, ALU.mult).then_inc(mix_v.sem, 1),
                      f"vn{tt}")
                eng.wait_ge(mix_t.sem, mix_t.at("z", l))
                eng.wait_ge(mix_a.sem, mix_a.at("gu", l))
                v(tt_(t(7), t(7), bank[4][:, :], ALU.mult).then_inc(mix_v.sem, 1), "yb_raw")
                eng.wait_ge(mix_a.sem, mix_a.at("rtd", l))
                v(nc.vector.reciprocal(t(5), t(5)).then_inc(mix_v.sem, 1), "rec_d")
                v(tt_(t(2), bank[3][:, :], t(5), ALU.mult).then_inc(mix_v.sem, 1), "od")
                for i in range(CB):
                    c = slice(i * T, (i + 1) * T)
                    v(stt(out=y_t[:, 6 + i, :], in0=t(2)[:, c], scalar=par("hgrn_out", l, i), in1=t(13)[:, c],
                          op0=ALU.mult, op1=ALU.mult).then_inc(mix_v.sem, 1), f"yd{i}")
                for n, (name, at, rt, src, par_name) in enumerate((("c", 4, 9, 12, "lru_out"), ("b", 2, 10, 7, "sgu_out"),
                                                              ("a", 0, 2, 3, "pool_out"))):
                    eng.wait_ge(mix_a.sem, mix_a.at(f"rt{name}", l))
                    r = t(rt)[:, 0:T]
                    v(nc.vector.reciprocal(r, r).then_inc(mix_v.sem, 1), f"rec_{name}")
                    for i in range(CB):
                        c = slice(i * T, (i + 1) * T)
                        v(stt(out=y_t[:, at + i, :], in0=t(src)[:, c], scalar=par(par_name, l, i), in1=r,
                              op0=ALU.mult, op1=ALU.mult).then_inc(mix_v.sem, 1), f"y{name}{i}")

            def ffn():
                mods = list(MOD_PARTS)
                for j in range(NJ):
                    at = tmp[:, 2 + 2 * (j % 2):4 + 2 * (j % 2), :]
                    for i in range(2):
                        eng.wait_ge(ffn_a.sem, ffn_a.at(f"s{i}", j))
                        eng.wait_ge(ffn_t.sem, ffn_t.at(f"h3_{i}", j))
                        if j >= 2:
                            eng.wait_ge(ffn_w.sem, ffn_w.at("w", j - 2))
                        done(eng, tt_(at[:, i, :], tmp[:, i, :], bank[2 + i][:, :], ALU.mult).then_inc(ffn_v.sem, 1),
                             ffn_v, f"a{i}", j)
                    if 1 <= j <= 4:
                        mod_columns(1, MOD_PARTS[j - 1])
                    if mods:
                        mod_part(1, mods.pop(0))

            def routing():
                done_ = lambda ins, name: done(eng, ins, route_v, name)
                R = route
                lg, eq, cand, sel1, lg2, sel2, w, pos, sel, wt = (R[:, i, :, :] for i in range(10))
                m1, f1, m2, d, r, er = (route_c[:, i, :, :] for i in range(6))
                wide_ = lambda c: c.to_broadcast([P, TT, NE])
                ids = iota_f[:, 0:NE].unsqueeze(1).to_broadcast([P, TT, NE])
                eng.wait_ge(route_t.sem, route_t.at("logits"))
                done_(nc.vector.tensor_copy(lg, bank[2][:, 0:TT * NE].rearrange("p (t e) -> p t e", t=TT)).then_inc(route_v.sem, 1),
                      "lg")
                for n, (src, m, s) in enumerate(((lg, m1, sel1), (lg2, m2, sel2))):
                    done_(nc.vector.tensor_reduce(m, src, X, ALU.max).then_inc(route_v.sem, 1), f"max{n}")
                    done_(tt_(eq, src, wide_(m), ALU.is_equal).then_inc(route_v.sem, 1), f"eq{n}")
                    done_(stt(out=cand, in0=eq, scalar=-100.0, in1=ids, op0=ALU.mult, op1=ALU.add).then_inc(route_v.sem, 1),
                          f"cand{n}")
                    done_(nc.vector.tensor_reduce(f1, cand, X, ALU.min).then_inc(route_v.sem, 1), f"first{n}")
                    done_(tt_(s, cand, wide_(f1), ALU.is_equal).then_inc(route_v.sem, 1), f"pick{n}")
                    if n == 0:
                        done_(stt(out=lg2, in0=s, scalar=-3e38, in1=lg, op0=ALU.mult, op1=ALU.add).then_inc(route_v.sem, 1),
                              "lg2")
                done_(tt_(sel, sel1, sel2, ALU.add).then_inc(route_v.sem, 1), "sel")
                done_(tt_(d, m2, m1, ALU.subtract).then_inc(route_v.sem, 1), "diff")
                eng.wait_ge(route_a.sem, route_a.at("exp"))
                done_(ts_(r, er, 1.0, None, ALU.add).then_inc(route_v.sem, 1), "one")
                done_(nc.vector.reciprocal(r, r).then_inc(route_v.sem, 1), "w1")
                done_(tt_(er, er, r, ALU.mult).then_inc(route_v.sem, 1), "w2")
                done_(tt_(w, sel1, wide_(r), ALU.mult).then_inc(route_v.sem, 1), "sw1")
                done_(tt_(wt, sel2, wide_(er), ALU.mult).then_inc(route_v.sem, 1), "sw2")
                done_(tt_(wt, wt, w, ALU.add).then_inc(route_v.sem, 1), "wt")
                eng.wait_ge(route_t.sem, route_t.at("pos"))
                done_(nc.vector.tensor_copy(pos, bank[2][:, 64:64 + TT * NE].rearrange("p (t e) -> p t e", t=TT)).then_inc(route_v.sem, 1),
                      "pos")
                done_(nc.vector.tensor_reduce(most[:, 0:1], bank[2][:, 64 + 2 * NE:64 + 3 * NE], X, ALU.max).then_inc(route_v.sem, 1),
                      "most")
                done_(nc.vector.tensor_copy(most_i[:, :], most[:, 0:1]).then_inc(route_v.sem, 1), "most_i")
                done_(nc.vector.memset(chosen[:, :, NE, :], 0.0).then_inc(route_v.sem, 1), "idle")
                for n, c in enumerate((pos, sel, wt)):
                    done_(nc.vector.tensor_copy(chosen[:, n, 0:NE, :].rearrange("p e t -> p t e"), c).then_inc(route_v.sem, 1),
                          f"ch{n}")
                for n in range(4):
                    done(eng, nc.vector.memset(moe_sum[:, n // 2, n % 2 * W:(n % 2 + 1) * W], 0.0).then_inc(sum_v.sem, 1),
                         sum_v, f"a{n}", 0)

            def fill_low(part, rep, u):
                eng.wait_ge(fill_a.sem, fill_a.at(f"h{part}", rep))
                k = 4 * part
                done(eng, tt_(x_low[:, u, k:k + 4, :], x_slots[:, :, :], x_high[:, u, k:k + 4, :].bitcast(F32),
                              ALU.subtract).then_inc(fill_v.sem, 1), fill_v, "lb" if part else "la", rep)

            def dispatch_of(e, u, s, rep):
                src = chosen[:, :, e, :] if isinstance(e, int) else \
                    chosen[:, :, bass.ds(e, 1), :].rearrange("p c o t -> p c (o t)")
                done(eng, nc.vector.tensor_copy(choice[:, u, :, :], src).then_inc(s.sem, 1), s, "choice", rep)
                for tt in range(TT):
                    done(eng, ts_(dispatch[:, u, tt, :], iota_f, choice[:, u, 0, tt:tt + 1],
                                  choice[:, u, 1, tt:tt + 1], ALU.is_equal, ALU.mult).then_inc(s.sem, 1),
                         s, "disp" if tt == TT - 1 else f"d{tt}", rep)

            def low(r, u, m):
                c = slice(m % 2 * (KB * W // 2), (m % 2 + 1) * (KB * W // 2))
                eng.wait_ge(high_made, unit_at(r, m))
                tt_(moe_low(u, m // 2)[:, c], moe_slot(u, m // 2)[:, c], w_high[:, m % HIGHS, :].bitcast(F32),
                    ALU.subtract).then_inc(low_made, 1)

            def experts(q):
                if q:
                    done(eng, ts_(chosen[:, 0, 0:NE, :], chosen[:, 0, 0:NE, :], float(-SLOTS), None, ALU.add).then_inc(slot_pos.sem, 1),
                         slot_pos, "pos")
                dispatch_of(0, 0, slot_v, q)
                for part in range(2):
                    fill_low(part, q * (NE + 1), 0)
                with eng.Fori(0, NE // PAIR) as g:
                    for u in range(PAIR):
                        r = expert(q, g, u)
                        fill = q * (NE + 1) + g * PAIR + u

                        def product(j):
                            eng.wait_ge(moe_a.sem, moe_a.at(f"s{j}", r))
                            eng.wait_ge(unit_used, used_at(r, 2 * FFN_ORDER.index(("w3", j)) + 1))
                            done(eng, tt_(act_m[:, j % 2, :], act_s[:, j % 2, :], bank[2 + j % 2][:, :], ALU.mult).then_inc(moe_v.sem, 1),
                                 moe_v, f"m{j}", r)

                        def act_lows(j):
                            eng.wait_ge(moe_a.sem, moe_a.at(f"ah{j}", r))
                            done(eng, tt_(act_low[:, j % 2, :], bank[6][:, :], act_high[:, j % 2, :].bitcast(F32),
                                          ALU.subtract).then_inc(moe_v.sem, 1), moe_v, f"al{j}", r)

                        for m in range(UNITS):
                            low(r, u, m)
                            if m >= 8 and m % 6 == 2 and m < UNITS - 1:
                                act_lows(m // 6 - 1)
                            if m == 5:
                                product(0)
                            if m >= 10 and m % 6 == 4:
                                product(m // 6)
                            if m == 12:
                                dispatch_of(g * PAIR + u + 1, (u + 1) % 2, moe_v, r)
                            if m == 6 * GATHER + 5:
                                fill_low(0, fill + 1, (u + 1) % 2)
                            if m == 6 * GATHER + 11:
                                fill_low(1, fill + 1, (u + 1) % 2)
                        act_lows(NJ - 1)
                        for half in range(2):
                            c = slice(half * W, (half + 1) * W)
                            eng.wait_ge(moe_a.sem, moe_a.at(f"yh{half}", r))
                            done(eng, tt_(y_low[:, c], bank[4 + half][:, :], y_high[:, c].bitcast(F32),
                                          ALU.subtract).then_inc(moe_v.sem, 1), moe_v, f"yl{half}", r)
                        for n, b in enumerate((1, 3, 6, 7)):
                            eng.wait_ge(moe_t.sem, moe_t.at(f"c{n}", r))
                            m = moe_sum[:, n // 2, n % 2 * W:(n % 2 + 1) * W]
                            done(eng, stt(out=m, in0=bank[b][:, :], scalar=choice[:, u, 2, n // 2:n // 2 + 1], in1=m,
                                          op0=ALU.mult, op1=ALU.add).then_inc(sum_v.sem, 1), sum_v, f"a{n}", r + 1)

            eng.wait_ge(pre_t.sem, pre_t.at("rows"))
            done(eng, nc.vector.tensor_copy(params[:, :, :],
                                            bank[7][:, 0:DEPTH * P].rearrange("p (l n) -> p l n", l=DEPTH)[:, :, 0:NROWS]).then_inc(pre_v.sem, 1),
                 pre_v, "params")
            pv = lambda ins, name: done(eng, ins, pre_v, name)
            eng.wait_ge(pre_a.sem, pre_a.at("c"))
            mod_part(0, "sh1")
            mod_part(0, "sc1")
            mod_columns(0, "sh1")
            mod_columns(0, "sc1")
            r = ROWS["lambda"][0]
            lam = params[:, :, r:r + CB]
            sm = lambda i: small[:, i, 0:DEPTH * CB].rearrange("p (l b) -> p l b", l=DEPTH)
            pv(ts_(sm(0), lam, -1.0, None, ALU.mult).then_inc(pre_v.sem, 1), "neg")
            pv(tt_(sm(1), sm(0), lam, ALU.max).then_inc(pre_v.sem, 1), "abs")
            pv(ts_(sm(2), lam, 0.0, None, ALU.min).then_inc(pre_v.sem, 1), "min")
            r = ROWS["gamma"][0]
            g0, g1 = params[:, 0, r:r + CB], params[:, 0, r + CB:r + 2 * CB]
            pv(tt_(small[:, 3, 0:CB], g0, g1, ALU.max).then_inc(pre_v.sem, 1), "gm")
            pv(tt_(small[:, 4, 0:CB], g0, small[:, 3, 0:CB], ALU.subtract).then_inc(pre_v.sem, 1), "gd0")
            pv(tt_(small[:, 4, CB:2 * CB], g1, small[:, 3, 0:CB], ALU.subtract).then_inc(pre_v.sem, 1), "gd1")
            eng.wait_ge(pre_a.sem, pre_a.at("gexp"))
            e0, e1 = small[:, 5, 0:CB], small[:, 5, CB:2 * CB]
            pv(tt_(small[:, 3, 0:CB], e0, e1, ALU.add).then_inc(pre_v.sem, 1), "gs")
            pv(nc.vector.reciprocal(small[:, 3, 0:CB], small[:, 3, 0:CB]).then_inc(pre_v.sem, 1), "gr")
            pv(tt_(e0, e0, small[:, 3, 0:CB], ALU.mult).then_inc(pre_v.sem, 1), "p0")
            pv(tt_(e1, e1, small[:, 3, 0:CB], ALU.mult).then_inc(pre_v.sem, 1), "p1")
            pv(tt_(e1, e0, e1, ALU.add).then_inc(pre_v.sem, 1), "c1")
            pv(tt_(floor_col[:, 0, 0, :], e0, e0, ALU.subtract).then_inc(pre_v.sem, 1), "lb0")
            pv(tt_(floor_col[:, 1, 0, :], e1, e0, ALU.subtract).then_inc(pre_v.sem, 1), "lb1")
            pv(ts_(floor_col[:, :, 1, :], floor_col[:, :, 0, :], -1.0, 1.0, ALU.mult, ALU.add).then_inc(pre_v.sem, 1),
               "lbo")
            pv(ts_(floor_col[:, :, 2, :], floor_col[:, :, 0, :], 1.0, -1.0, ALU.mult, ALU.add).then_inc(pre_v.sem, 1),
               "lbn")
            eng.wait_ge(pre_a.sem, pre_a.at("lln"))
            pv(tt_(sm(2), sm(2), sm(7), ALU.subtract).then_inc(pre_v.sem, 1), "ls")
            pv(ts_(lru_k[:, :, 0, :], sm(2), LRU_C, None, ALU.mult).then_inc(pre_v.sem, 1), "lk0")
            pv(ts_(lru_k[:, :, 1, :], sm(2), -LRU_C, None, ALU.mult).then_inc(pre_v.sem, 1), "lk1")
            for l in range(DEPTH):
                norm(2 * l)
                mixers(l)
                if l == 0:
                    mod_part(0, "sh2")
                    mod_part(0, "sc2")
                    mod_columns(0, "sh2")
                    mod_columns(0, "sc2")
                    mod_part(0, "g1")
                gate(l, 0, (bank[5], bank[7]))
                residual(2 * l, [bank[n][:, :] for n in range(4)], [[(mix_t, f"wout{n}", l)] for n in range(4)])
                norm(2 * l + 1)
                if l == 0:
                    mod_part(0, "g2")
                gate(l, 1, (bank[0], bank[1]))
                if l == 0:
                    ffn()
                    residual(1, [bank[4 + n][:, :] for n in range(4)], [[(ffn_w, "w", NJ - 1)]] * 4)
            routing()
            experts(0)
            with eng.If(eng.value_load(most_i[0:1, 0:1], min_val=0, max_val=T) > SLOTS):
                experts(1)
            residual(3, [moe_sum[:, n // 2, n % 2 * W:(n % 2 + 1) * W] for n in range(4)], [[]] * 4)
            eng.wait_ge(end_a.sem, end_a.at("rt"))
            done(eng, nc.vector.reciprocal(norm_s[:, 2, :], norm_s[:, 1, :]).then_inc(end_v.sem, 1), end_v, "rc")
            eng.wait_ge(s_gate, 16 * (2 * DEPTH + 1))
            for tt in range(TT):
                done(eng, stt(out=xn[:, tt, :], in0=x[:, tt, :], scalar=norm_s[:, 2, tt:tt + 1], in1=gate_row[:, :],
                              op0=ALU.mult, op1=ALU.mult).then_inc(end_v.sem, 1), end_v, f"out{tt}")

        @block.scalar
        def _(eng):
            act = nc.scalar.activation

            def mean_square(s, rep):
                for tt in range(TT):
                    done(eng, act(xn[:, tt, :], x[:, tt, :], ACT.Square, accum_out=norm_s[:, 0, tt:tt + 1]).then_inc(s.sem, 1),
                         s, f"sq{tt}", rep)
                done(eng, act(norm_s[:, 1, :], norm_s[:, 0, :], ACT.Sqrt, bias=eps_col[:, 0:1], scale=1.0 / D).then_inc(s.sem, 1),
                     s, "rt", rep)

            def norm(q):
                if q == 0:
                    eng.wait_ge(s_x, 16)
                else:
                    eng.wait_ge(res_v.sem, res_v.at("r7", q - 1))
                mean_square(norm_a, q)
                eng.wait_ge(mod_e.sem, mod_e.at("fin", 2 * q + 1))
                for b in (0, 2):
                    eng.wait_ge(norm_t.sem, norm_t.at(f"t{b}", q))
                    for i in range(2):
                        k = 2 * b + i
                        done(eng, act(h_t[:, k, :], bank[4 + b][:, i * T:(i + 1) * T], ACT.Identity,
                                      bias=mod_col[:, 2 * q, k:k + 1], scale=mod_col[:, 2 * q + 1, k:k + 1]).then_inc(norm_a.sem, 1),
                             norm_a, f"h{k}", q)

            def mixers(l):
                def s(ins, name):
                    done(eng, ins, mix_a, name, l)

                def t(i):
                    return tmp[:, i, :]

                eng.wait_ge(mix_t.sem, mix_t.at("dfz", l))
                s(act(t(0), bank[0][:, :], ACT.Sigmoid).then_inc(mix_a.sem, 1), "sig")
                eng.wait_ge(mix_v.sem, mix_v.at("fa", l))
                s(act(t(3), t(3), ACT.Ln).then_inc(mix_a.sem, 1), "lna")
                eng.wait_ge(mix_v.sem, mix_v.at("fb", l))
                s(act(t(4), t(4), ACT.Ln, scale=1.0 / LN_FLOOR).then_inc(mix_a.sem, 1), "lnb")
                eng.wait_ge(mix_v.sem, mix_v.at("kc", l))
                s(act(t(2), t(2), ACT.Ln).then_inc(mix_a.sem, 1), "lnk")
                eng.wait_ge(mix_v.sem, mix_v.at("b1", l))
                s(act(t(3), t(1), ACT.Exp).then_inc(mix_a.sem, 1), "eb")
                ends = t(1).rearrange("p (n s) -> p n s", s=C)[:, :, C - 1]
                s(act(small[:, 8:12, :].rearrange("p a b -> p (a b)"), ends, ACT.Exp).then_inc(mix_a.sem, 1), "ea")
                eng.wait_ge(mix_v.sem, mix_v.at("kd", l))
                s(act(t(4), t(4), ACT.Exp).then_inc(mix_a.sem, 1), "kh")

                def exps(i):
                    for r in range(C):
                        rep = (l * CB + i) * C + r
                        eng.wait_ge(tri_d.sem, tri_d.at("d", rep))
                        done(eng, act(tri[:, r, :, 0:r + 1], tri[:, r, :, 0:r + 1], ACT.Exp).then_inc(tri_e.sem, 1),
                             tri_e, "e", rep)

                exps(0)
                eng.wait_ge(mix_t.sem, mix_t.at("dq", l))
                s(act(t(0), bank[2][:, :], ACT.Silu).then_inc(mix_a.sem, 1), "q")
                eng.wait_ge(mix_t.sem, mix_t.at("kt", l))
                s(act(t(5), bank[4][:, :], ACT.Copy).then_inc(mix_a.sem, 1), "kt")
                eng.wait_ge(mix_t.sem, mix_t.at("px", l))
                if l:
                    eng.wait_ge(mix_v.sem, mix_v.at("xc1", l - 1))
                s(act(x_pad[:, :, CONV - 1:], rows2(bank[0][:, :]), ACT.Copy).then_inc(mix_a.sem, 1), "xp")
                eng.wait_ge(mix_t.sem, mix_t.at("pg", l))
                s(act(t(12), bank[1][:, :], ACT.Gelu_apprx_tanh).then_inc(mix_a.sem, 1), "gate_c")
                eng.wait_ge(mix_t.sem, mix_t.at("pv", l))
                for tt in range(TT):
                    c = slice(tt * G, (tt + 1) * G)
                    s(act(t(4)[:, c], bank[2][:, c], ACT.Gelu_apprx_tanh, accum_out=small[:, 0, tt:tt + 1]).then_inc(mix_a.sem, 1),
                      f"gv{tt}")
                exps(1)
                for name, b, dst, bias in (("r", 4, 8, "lru_ba"), ("i", 5, 9, "lru_bx")):
                    eng.wait_ge(mix_t.sem, mix_t.at("wa" if name == "r" else "wx", l))
                    for i in range(CB):
                        c = slice(i * T, (i + 1) * T)
                        s(act(t(dst)[:, c], bank[b][:, c], ACT.Sigmoid, bias=par(bias, l, i)).then_inc(mix_a.sem, 1),
                          f"{name}{i}")
                for i in range(CB):
                    c = slice(i * T, (i + 1) * T)
                    s(act(t(10)[:, c], t(8)[:, c], ACT.Exp, scale=lru_k[:, l, 0, i:i + 1]).then_inc(mix_a.sem, 1),
                      f"a{i}")
                for i in range(CB):
                    c = slice(i * T, (i + 1) * T)
                    s(act(t(8)[:, c], t(8)[:, c], ACT.Tanh, scale=lru_k[:, l, 1, i:i + 1]).then_inc(mix_a.sem, 1),
                      f"th{i}")
                eng.wait_ge(mix_v.sem, mix_v.at("m0", l))
                s(act(t(11), t(11), ACT.Sqrt).then_inc(mix_a.sem, 1), "sm")
                eng.wait_ge(mix_t.sem, mix_t.at("dg", l))
                s(act(t(13), bank[0][:, :], ACT.Silu).then_inc(mix_a.sem, 1), "gate_d")
                eng.wait_ge(mix_v.sem, mix_v.at("yc_raw", l))
                s(act(t(8), t(12), ACT.Square).then_inc(mix_a.sem, 1), "sqc")
                eng.wait_ge(mix_v.sem, mix_v.at("vc1", l))
                for tt in range(TT):
                    c = slice(tt * G, (tt + 1) * G)
                    s(act(t(5)[:, c], t(4)[:, c], ACT.Square, accum_out=small[:, 2, tt:tt + 1]).then_inc(mix_a.sem, 1),
                      f"sv{tt}")
                s(act(small[:, 3, 0:2], small[:, 2, 0:2], ACT.Sqrt, bias=eps_col[:, 0:1], scale=1.0 / G).then_inc(mix_a.sem, 1),
                  "rv")
                eng.wait_ge(mix_t.sem, mix_t.at("pu", l))
                s(act(t(7), bank[1][:, :], ACT.Gelu_apprx_tanh).then_inc(mix_a.sem, 1), "gu")
                eng.wait_ge(mix_t.sem, mix_t.at("pa", l))
                s(act(t(11), bank[2][:, :], ACT.Copy).then_inc(mix_a.sem, 1), "pa")
                eng.wait_ge(mix_t.sem, mix_t.at("o", l))
                s(act(t(2), bank[3][:, :], ACT.Square).then_inc(mix_a.sem, 1), "sqd")
                eng.wait_ge(mix_t.sem, mix_t.at("ssd", l))
                s(act(t(5), bank[7][:, :], ACT.Sqrt, bias=eps_col[:, 0:1], scale=1.0 / HD).then_inc(mix_a.sem, 1),
                  "rtd")
                eng.wait_ge(mix_t.sem, mix_t.at("ssc", l))
                s(act(t(9)[:, 0:T], bank[5][:, 0:T], ACT.Sqrt, bias=eps_col[:, 0:1], scale=1.0 / G).then_inc(mix_a.sem, 1),
                  "rtc")
                eng.wait_ge(mix_t.sem, mix_t.at("aband", l))
                s(act(t(6), bank[6][:, :], ACT.Copy).then_inc(mix_a.sem, 1), "pd")
                eng.wait_ge(mix_v.sem, mix_v.at("yb_raw", l))
                s(act(t(4), t(7), ACT.Square).then_inc(mix_a.sem, 1), "sqb")
                eng.wait_ge(mix_t.sem, mix_t.at("ssb", l))
                s(act(t(10)[:, 0:T], bank[7][:, 0:T], ACT.Sqrt, bias=eps_col[:, 0:1], scale=1.0 / G).then_inc(mix_a.sem, 1),
                  "rtb")
                eng.wait_ge(mix_t.sem, mix_t.at("apool", l))
                for i in range(CB):
                    c = slice(i * T, (i + 1) * T)
                    s(act(t(3)[:, c], bank[4][:, c], ACT.Copy, scale=par("pool_scale", l, i)).then_inc(mix_a.sem, 1),
                      f"ps{i}")
                s(act(t(1), t(3), ACT.Square).then_inc(mix_a.sem, 1), "sqa")
                eng.wait_ge(mix_t.sem, mix_t.at("ssa", l))
                eng.wait_ge(mix_v.sem, mix_v.at("od", l))
                eng.wait_ge(mix_v.sem, mix_v.at("yd1", l))
                s(act(t(2)[:, 0:T], bank[5][:, 0:T], ACT.Sqrt, bias=eps_col[:, 0:1], scale=1.0 / G).then_inc(mix_a.sem, 1),
                  "rta")

            def ffn():
                for j in range(NJ):
                    for i in range(2):
                        eng.wait_ge(ffn_t.sem, ffn_t.at(f"h1_{i}", j))
                        if j:
                            eng.wait_ge(ffn_v.sem, ffn_v.at(f"a{i}", j - 1))
                        done(eng, act(tmp[:, i, :], bank[i][:, :], ACT.Silu).then_inc(ffn_a.sem, 1),
                             ffn_a, f"s{i}", j)

            def fill_half(b, part, e, rep, s, name, u):
                eng.wait_ge(s.sem, s.at(name, e))
                if part:
                    eng.wait_ge(fill_v.sem, fill_v.at("la", rep))
                for k in range(4):
                    kb = 4 * part + k
                    done(eng, act(x_slots[:, k, :], b[:, k * P:(k + 1) * P], ACT.Identity,
                                  bias=mod_col[:, 6, kb:kb + 1], scale=mod_col[:, 7, kb:kb + 1]).then_inc(fill_a.sem, 1),
                         fill_a, f"x{kb}", rep)
                k = 4 * part
                done(eng, act(x_high[:, u, k:k + 4, :], x_slots[:, :, :], ACT.Copy).then_inc(fill_a.sem, 1),
                     fill_a, f"h{part}", rep)

            def high(q, g, u, m):
                r = expert(q, g, u)
                if m % 2 == 0:
                    moe_arrived(eng, q, g, u, m // 2)
                eng.wait_ge(unit_used, used_at(r, m - HIGHS))
                c = slice(m % 2 * (KB * W // 2), (m % 2 + 1) * (KB * W // 2))
                act(w_high[:, m % HIGHS, :], moe_slot(u, m // 2)[:, c], ACT.Copy).then_inc(high_made, 1)

            def experts(q):
                for part in range(2):
                    fill_half(bank[4 + part], part, q, q * (NE + 1), slot_t, f"g{part}", 0)
                with eng.Fori(0, NE // PAIR) as g:
                    for u in range(PAIR):
                        r = expert(q, g, u)
                        fill = q * (NE + 1) + g * PAIR + u

                        def act_highs(j):
                            eng.wait_ge(moe_t.sem, moe_t.at(f"t{j}", r))
                            done(eng, act(act_high[:, j % 2, :], bank[6][:, :], ACT.Copy).then_inc(moe_a.sem, 1),
                                 moe_a, f"ah{j}", r)

                        for m in range(UNITS):
                            high(q, g, u, m)
                            if m == 4 or m >= 8 and m % 6 == 2:
                                j = m // 6
                                eng.wait_ge(unit_used, used_at(r, 2 * FFN_ORDER.index(("w1", j)) + 1))
                                done(eng, act(act_s[:, j % 2, :], bank[j % 2][:, :], ACT.Silu).then_inc(moe_a.sem, 1),
                                     moe_a, f"s{j}", r)
                                if j:
                                    act_highs(j - 1)
                            if m == 10:
                                eng.wait_ge(moe_t.sem, moe_t.at("spread", r))
                                done(eng, act(spread[:, :], bank[7][:, 0:T], ACT.Copy).then_inc(moe_a.sem, 1),
                                     moe_a, "spread", r)
                            if m == 6 * GATHER + 4:
                                fill_half(bank[7], 0, r, fill + 1, moe_t, "ga", (u + 1) % 2)
                            if m == 6 * GATHER + 10:
                                fill_half(bank[7], 1, r, fill + 1, moe_t, "gb", (u + 1) % 2)
                        act_highs(NJ - 1)
                        eng.wait_ge(unit_used, used_at(r, UNITS - 1))
                        for half in range(2):
                            done(eng, act(y_high[:, half * W:(half + 1) * W], bank[4 + half][:, :], ACT.Copy).then_inc(moe_a.sem, 1),
                                 moe_a, f"yh{half}", r)

            eng.wait_ge(pre_v.sem, pre_v.at("params"))
            r = ROWS["c"][0]
            done(eng, act(c_act[:, :], params[:, 0, r:r + KB], ACT.Silu).then_inc(pre_a.sem, 1), pre_a, "c")
            eng.wait_ge(pre_v.sem, pre_v.at("gd1"))
            done(eng, act(small[:, 5, 0:2 * CB], small[:, 4, 0:2 * CB], ACT.Exp).then_inc(pre_a.sem, 1),
                 pre_a, "gexp")
            done(eng, act(small[:, 6, 0:DEPTH * CB], small[:, 1, 0:DEPTH * CB], ACT.Exp, scale=-1.0).then_inc(pre_a.sem, 1),
                 pre_a, "lexp")
            done(eng, act(small[:, 7, 0:DEPTH * CB], small[:, 6, 0:DEPTH * CB], ACT.Ln, bias=1.0).then_inc(pre_a.sem, 1),
                 pre_a, "lln")
            for l in range(DEPTH):
                norm(2 * l)
                mixers(l)
                norm(2 * l + 1)
                if l == 0:
                    ffn()
            eng.wait_ge(route_v.sem, route_v.at("diff"))
            done(eng, act(route_c[:, 5, :, :], route_c[:, 3, :, :], ACT.Exp).then_inc(route_a.sem, 1), route_a, "exp")
            experts(0)
            eng.wait_ge(route_v.sem, route_v.at("most_i"))
            with eng.If(eng.value_load(most_i[0:1, 0:1], min_val=0, max_val=T) > SLOTS):
                experts(1)
            eng.wait_ge(res_v.sem, res_v.at("r7", 3))
            mean_square(end_a, 0)


_INS = ['x', 'c', 'w_mod', 'b_mod', 'norm_mix', 'norm_ffn', 'norm_final', 'w_in', 'w_out', 'pool_w', 'pool_scale',
        'pool_out_norm', 'sgu_ws', 'sgu_b', 'sgu_out_norm', 'conv_w', 'conv_b', 'lru_wa', 'lru_ba', 'lru_wx', 'lru_bx',
        'lru_lambda', 'lru_out_norm', 'hgrn_gamma', 'hgrn_out_norm', 'ffn_w1', 'ffn_w3', 'ffn_w2', 'router_w',
        'router_b', 'moe_w1', 'moe_w3', 'moe_w2']
_OUTS = [((1, T, D), 'float32')]


def kernel(**inputs):
    import numpy as _np
    import concourse.bacc as _bacc
    from concourse import mybir as _mybir
    from concourse.bass_utils import run_bass_kernel_spmd as _run

    nc = _bacc.Bacc("TRN2", target_bir_lowering=False, num_devices=1)
    arrays, args = {}, {}
    for name in _INS:
        v = _np.ascontiguousarray(inputs[name])
        arrays[f"in_{name}_dram"] = v
        args[name] = nc.dram_tensor(f"in_{name}_dram", v.shape, _mybir.dt.from_np(v.dtype), kind="ExternalInput").ap()
    out = nc.dram_tensor("out_0_dram", _OUTS[0][0], _mybir.dt.float32, kind="ExternalOutput").ap()
    hybrid_stream_block(nc, args, out)
    r = _run(nc, [arrays], core_ids=[0])
    return r.results[0]["out_0_dram"]
```

```python
from contextlib import ExitStack

import concourse.bass as bass
from concourse import mybir

P = 128
D = 1024
KB = D // P
T = 256
TT = T // P
DEPTH = 2
G = 256
CB = G // P
HD = 64
NH = G // HD
WINDOWS = (2, 4, 8, 16)
CONV = 4
LRU_C = 8.0
DFF = 7 * D // 2
W = 512
NJ = DFF // W
HB = W // P
NE = 8
SLOTS = P
EPS = 1e-6
MIN_FORGET = 1e-30
C = 16
NC = T // C
CT_ = P // C
RING = 6
EDGE = P + 16
LN_FLOOR = 2.0 ** -60

F32 = mybir.dt.float32
F32R = mybir.dt.float32r
I32 = mybir.dt.int32
ALU = mybir.AluOpType
ACT = mybir.ActivationFunctionType
X = mybir.AxisListType.X

ROWS = {}
_at = 0
for _name, _n in (("norm_mix", KB), ("norm_ffn", KB), ("pool_scale", CB), ("pool_out", CB), ("sgu_out", CB),
                  ("conv_w", CONV * CB), ("conv_b", CB), ("lru_ba", CB), ("lru_bx", CB), ("lambda", CB),
                  ("lru_out", CB), ("hgrn_out", CB), ("gamma", DEPTH * CB),
                  ("b_sh1", KB), ("b_sc1", KB), ("b_sh2", KB), ("b_sc2", KB)):
    ROWS[_name] = (_at, _n)
    _at += _n
NROWS = _at

COLS = {n: i * G for i, n in enumerate(("pa", "pu", "pv", "px", "pg", "dq", "dfz", "di", "dg"))}
GROUPS = ("dfz", "di", "dq", "px", "pg", "pv", "dg", "pu", "pa")
WIN_ORDER = (3, 2, 1, 4, 0)
MOD_PARTS = ("sh1", "sc1", "sh2", "sc2", "g1", "g2")
MOD_COL = {"sh1": 0, "sc1": 1, "g1": 2, "sh2": 3, "sc2": 4, "g2": 5}
FFN_ORDER = ([("w1", 0), ("w3", 0)]
             + [x for j in range(1, NJ) for x in (("w1", j), ("w3", j), ("w2", j - 1))] + [("w2", NJ - 1)])
NCH = len(FFN_ORDER)
GATHER = 4
UNITS = 2 * NCH
HIGHS = 3
assert UNITS % HIGHS == 0
QUARTERS = [u for j in range(NJ + 1) for u in
            ([(w, j, 2 * i + hb) for i in range(2) for w in ("w1", "w3") for hb in range(2)] if j < NJ else [])
            + ([("w2", j - 1, hb) for hb in range(HB)] if j else [])]
QUARTER = {u: m for m, u in enumerate(QUARTERS)}
PAIR = 2
assert PAIR * NCH % RING == 0 and NE % PAIR == 0


class Steps:

    def __init__(self, sem, names):
        self.sem, self.names = sem, names
        self.count = 0
        self.index = {n: i + 1 for i, n in enumerate(names)}

    def at(self, name, rep=0):
        return rep * len(self.names) + self.index[name]

    def said(self, name):
        assert self.names[self.count % len(self.names)] == name, (self.names[self.count % len(self.names)], name)
        self.count += 1



N_ROW_LOADS = 17
FIRST_CONSTS = 10
MIX_CONSTS = 22
N_CONSTS = 81
CHAIN = CB * (NC - 1)

STEPS = {
    "pre_v":
        ("params neg abs min gm gd0 gd1 gs gr p0 p1 c1 lb0 lb1 lbo lbn ls lk0 lk1").split(),
    "pre_a":
        ("c gexp lexp lln").split(),
    "pre_t":
        ("c rows").split(),
    "mod_v":
        ("c0k0 c0k1 c0k2 c0k3 c0k4 c0k5 c0k6 c0k7 c1k0 c1k1 c1k2 c1k3 c1k4 c1k5 c1k6 c1k7").split(),
    "mod_p":
        ("c0 s0k4 s0k2 s0k1 c1 s1k4 s1k2 s1k1").split(),
    "mod_t":
        ("sum").split(),
    "mod_e":
        ("add fin").split(),
    "gate_t":
        ("sum").split(),
    "gate_v":
        ("g0 g1").split(),
    "norm_v":
        ("rc xn0 xn1 h2 h3 h6 h7").split(),
    "norm_a":
        ("sq0 sq1 rt h0 h1 h4 h5").split(),
    "norm_t":
        ("t0 t1 t2 t3").split(),
    "mix_v":
        ("wst f0 f1 k0 k1 fa fb kc lf b0 b1 bk kd v vx0 vx1 vx2 vx3 vx4 vx5 vx6 vx7 cv00 cv01 cv02 xc0 "
         "cv10 cv11 cv12 xc1 qt a2 m m0 ix bb hs0 hs1 yc_raw sf0 sf1 mu vc0 vc1 rvr vn0 vn1 yb_raw rec_d "
         "od yd0 yd1 rec_c yc0 yc1 rec_b yb0 yb1 rec_a ya0 ya1").split(),
    "mix_a":
        ("sig lna lnb lnk eb ea kh q kt xp gate_c gv0 gv1 r0 r1 i0 i1 a0 a1 th0 th1 sm gate_d sqc sv0 sv1 "
         "rv gu pa sqd rtd rtc pd sqb rtb ps0 ps1 sqa rta").split(),
    "mix_t":
        ("dfz ws di dq kt px u0 u1 u2 u3 u4 u5 u6 u7 pg pv wa wx sc0 dg pu pa sc1 o z ssd ssc aband ssb "
         "apool ssa wout0 wout1 wout2 wout3").split(),
    "tri_d":
        ("d").split(),
    "tri_e":
        ("e").split(),
    "tri_q":
        ("q").split(),
    "chain_v":
        ("s").split(),
    "res_v":
        ("r0 r1 r2 r3 r4 r5 r6 r7").split(),
    "ffn_v":
        ("a0 a1").split(),
    "ffn_a":
        ("s0 s1").split(),
    "part_a":
        ("h0 h1 a0 a1 a2 a3 a4 a5 a6").split(),
    "part_v":
        ("h0 h1 a0 a1 a2 a3 a4 a5 a6").split(),
    "ffn_h":
        ("q").split(),
    "ffn_l":
        ("q").split(),
    "ffn_u":
        ("q").split(),
    "route_v":
        ("lg max0 eq0 cand0 first0 pick0 lg2 max1 eq1 cand1 first1 pick1 sel diff one w1 w2 sw1 sw2 wt pos "
         "most most_i idle ch0 ch1 ch2").split(),
    "route_a":
        ("exp").split(),
    "route_t":
        ("logits pos").split(),
    "slot_v":
        ("choice d0 disp none").split(),
    "slot_a":
        ("spread").split(),
    "slot_t":
        ("g0 g1").split(),
    "slot_pos":
        ("pos").split(),
    "moe_v":
        ("m0 al0 m1 choice d0 disp al1 m2 al2 m3 al3 m4 al4 m5 al5 m6 al6").split(),
    "moe_a":
        ("s0 s1 ah0 spread s2 ah1 s3 ah2 s4 ah3 s5 ah4 s6 ah5 ah6").split(),
    "moe_t":
        ("t0 spread t1 t2 t3 ga t4 gb t5 t6").split(),
    "comb_v":
        ("yl0 yl1").split(),
    "comb_a":
        ("yh0 yh1").split(),
    "comb_t":
        ("c0 c1 c2 c3").split(),
    "fill_v":
        ("la lb").split(),
    "fill_a":
        ("x0 x1 x2 x3 h0 x4 x5 x6 x7 h1").split(),
    "sum_v":
        ("a0 a1 a2 a3").split(),
    "end_v":
        ("rc out0 out1").split(),
    "end_a":
        ("sq0 sq1 rt").split(),
}


def hybrid_stream_block(nc, a, out):
    ctx = ExitStack()
    with ctx:
        def sb(name, shape, dt=F32):
            return ctx.enter_context(nc.sbuf_tensor(name, shape, dt))

        def sem(name):
            return ctx.enter_context(nc.semaphore(name))

        shared = ExitStack()
        ring = shared.enter_context(nc.sbuf_tensor("ring", [P, RING, KB * W], F32))
        shared.close()
        ring_low = sb("ring_low", [P, RING, KB * W], F32R)
        x = sb("x", [P, TT, D])
        shared = ExitStack()
        h_high = shared.enter_context(nc.sbuf_tensor("h_high", [P, KB, T], F32R))
        shared.close()
        xn = sb("xn", [P, TT, D])
        y_t = xn[:, :, :].rearrange("p t (b c) -> p (t b) c", c=T)
        mod_tmp = sb("mod_tmp", [P, KB])
        mod_col = sb("mod_col", [P, DEPTH * 4, KB])
        gate_row = sb("gate_row", [P, D])
        consts = sb("consts", [P, 7, P])
        ident, ones, head_ones, triu, lower, before, iota_f = (consts[:, i, :] for i in range(7))
        scan_keep = sb("scan_keep", [P, T])
        chunk_of = sb("chunk_of", [P, CT_])
        head_sel = sb("head_sel", [P, 2])
        row_sel = sb("row_sel", [NH, CB, P])
        eps_col = sb("eps_col", [P, 1])
        params = sb("params", [P, DEPTH, NROWS])
        c_row = sb("c_row", [KB, P])
        c_act = sb("c_act", [P, KB])
        lru_k = sb("lru_k", [P, DEPTH, 2, CB])
        floor_col = sb("floor_col", [P, DEPTH, 3, CB])
        small = sb("small", [P, 16, 8])
        sgu_bias = sb("sgu_bias", [NH, P])
        norm_s = sb("norm_s", [P, 4, TT])
        low = ExitStack()
        shared = ExitStack()
        h_low = shared.enter_context(nc.sbuf_tensor("h_low", [P, KB, T], F32R))
        shared.enter_context(nc.sbuf_tensor("mod_acc_place", [P, 2, D], F32R))
        tmp_r = shared.enter_context(nc.sbuf_tensor("tmp_r", [P, 14, G * CB], F32R))
        at_high = shared.enter_context(nc.sbuf_tensor("at_high", [P, 2, W], F32R))
        shared.close()
        h_t = low.enter_context(nc.sbuf_tensor("h_t", [P, KB, T], F32))
        mod_acc = low.enter_context(nc.sbuf_tensor("mod_acc", [P, 2, D], F32))
        tmp = low.enter_context(nc.sbuf_tensor("tmp", [P, 14, G * CB], F32))
        v_wide = low.enter_context(nc.sbuf_tensor("v_wide", [P, 2, W], F32))
        tri = low.enter_context(nc.sbuf_tensor("tri", [P, C, NC, C], F32))
        state = low.enter_context(nc.sbuf_tensor("state", [P, CB, NC, HD], F32))
        band_a = low.enter_context(nc.sbuf_tensor("band_a", [P, NH, EDGE], F32))
        band_b = low.enter_context(nc.sbuf_tensor("band_b", [P, NH, P], F32))
        blocks = low.enter_context(nc.sbuf_tensor("blocks", [P, 3, CB, P], F32))
        ws_t = low.enter_context(nc.sbuf_tensor("ws_t", [P, NH, P], F32))
        x_pad = low.enter_context(nc.sbuf_tensor("x_pad", [P, CB, CONV - 1 + T], F32))
        s_full = v_wide[:, :, :].rearrange("p t (h n) -> p t h n", h=NH)
        prow = tmp[0:NROWS, 0, 0:DEPTH * P].rearrange("p (l n) -> p l n", l=DEPTH)
        low.close()
        moe_mem = ExitStack()

        def mb(name, shape, dt=F32):
            return moe_mem.enter_context(nc.sbuf_tensor(name, shape, dt))

        w_high = mb("w_high", [P, HIGHS, KB * W // 2], F32R)
        x_slots = mb("x_slots", [P, 4, SLOTS])
        x_high = mb("x_high", [P, 2, KB, SLOTS], F32R)
        x_low = mb("x_low", [P, 2, KB, SLOTS], F32R)
        dispatch = mb("dispatch", [P, 2, TT, SLOTS])
        choice = mb("choice", [P, 2, 3, TT])
        chosen = mb("chosen", [P, 3, NE + 1, TT])
        spread = mb("spread", [P, T], F32R)
        moe_sum = mb("moe_sum", [P, TT, D])
        act_s = mb("act_s", [P, 2, W])
        act_m = mb("act_m", [P, 2, W])
        act_high = mb("act_high", [P, 2, W], F32R)
        act_low = mb("act_low", [P, 2, W], F32R)
        y_high = mb("y_high", [P, D], F32R)
        y_low = mb("y_low", [P, D], F32R)
        route = mb("route", [P, 14, TT, NE])
        route_c = mb("route_c", [P, 6, TT, 1])
        router = mb("router", [P, KB, NE])
        router_bias = mb("router_bias", [1, NE])
        most = mb("most", [P, 4])
        most_i = mb("most_i", [P, 1], I32)
        moe_mem.close()
        bank = [ctx.enter_context(nc.psum_tensor(f"bank{i}", [P, W], F32)) for i in range(8)]

        landed = [sem(f"landed_{i}") for i in range(RING)]
        s_x = sem("x_loaded")
        s_c = sem("c_loaded")
        s_rows = sem("rows_loaded")
        s_blk = sem("blocks_loaded")
        s_ws = sem("ws_loaded")
        s_gate = sem("gate_bias_loaded")
        s_router = sem("router_loaded")
        high_made = sem("high_made")
        low_made = sem("low_made")
        unit_used = sem("unit_used")
        s_const = sem("constants_made")
        s_out = sem("out_stored")

        def steps(name):
            return Steps(sem(name), STEPS[name])

        pre_v, pre_a, pre_t = steps("pre_v"), steps("pre_a"), steps("pre_t")
        mod_v, mod_p, mod_t, mod_e = steps("mod_v"), steps("mod_p"), steps("mod_t"), steps("mod_e")
        gate_t, gate_v = steps("gate_t"), steps("gate_v")
        norm_v, norm_a, norm_t = steps("norm_v"), steps("norm_a"), steps("norm_t")
        mix_v, mix_a, mix_t = steps("mix_v"), steps("mix_a"), steps("mix_t")
        tri_d, tri_e, tri_q = steps("tri_d"), steps("tri_e"), steps("tri_q")
        chain_v = steps("chain_v")
        res_v = steps("res_v")
        ffn_v, ffn_a = steps("ffn_v"), steps("ffn_a")
        part_a, part_v = steps("part_a"), steps("part_v")
        ffn_h, ffn_l, ffn_u = steps("ffn_h"), steps("ffn_l"), steps("ffn_u")
        route_v, route_a, route_t = steps("route_v"), steps("route_a"), steps("route_t")
        slot_v, slot_a, slot_t = steps("slot_v"), steps("slot_a"), steps("slot_t")
        slot_pos = steps("slot_pos")
        moe_v, moe_a, moe_t = steps("moe_v"), steps("moe_a"), steps("moe_t")
        comb_v, comb_a, comb_t = steps("comb_v"), steps("comb_a"), steps("comb_t")
        fill_v, fill_a, sum_v = steps("fill_v"), steps("fill_a"), steps("sum_v")
        end_v, end_a = steps("end_v"), steps("end_a")

        def done(eng, ins, s, name, rep=0):
            s.said(name)
            eng.wait_ge(s.sem, s.at(name, rep))

        def mark(ins, s, name):
            s.said(name)

        def par(name, l, i=0, n=1):
            r = ROWS[name][0] + i
            return params[:, l, r:r + n]

        def mod_src(l, part, half):
            col = MOD_COL[part] * D + half * W
            return a["w_mod"][l].rearrange("(k p) n -> p k n", p=P)[:, :, col:col + W]

        def win_src(l, c):
            return a["w_in"][l].rearrange("(k p) n -> p k n", p=P)[:, :, c * W:min((c + 1) * W, 9 * G)]

        def wout_src(l, half):
            return a["w_out"][l].rearrange("(k p) n -> p k n", p=P)[:, :, half * W:(half + 1) * W]

        def ffn_src(kind, j):
            if kind == "w2":
                return a["ffn_w2"][0].rearrange("(b p) n -> p b n", p=P)[:, j * W // P:(j + 1) * W // P, :]
            return a[f"ffn_{kind}"][0].rearrange("(k p) n -> p k n", p=P)[:, :, j * W:(j + 1) * W]

        chunks = []

        def mod_summed(l, n, half=1):
            if l == 0 and n >= 2:
                return mod_p, f"s{half}k1", n - 2
            return mod_v, f"c{half}k{KB - 1}", n if l == 0 else n + 2

        def mod_chunks(l, part):
            for half in range(2):
                n = MOD_PARTS.index(part)
                user = mod_summed(l, n, half)
                chunks.append((("mod", l, part, half), mod_src(l, part, half), user))

        def win_chunks(l):
            last = {3: "di", 2: "pg", 1: "pv", 4: "dg", 0: "pa"}
            for c in WIN_ORDER:
                chunks.append((("win", l, c), win_src(l, c), (mix_t, last[c], l)))

        def wout_chunks(l):
            for half in range(2):
                chunks.append((("wout", l, half), wout_src(l, half), (mix_t, "wout3", l)))

        mod_chunks(0, "sh1")
        mod_chunks(0, "sc1")
        win_chunks(0)
        mod_chunks(0, "sh2")
        mod_chunks(0, "sc2")
        mod_chunks(0, "g1")
        mod_chunks(0, "g2")
        wout_chunks(0)
        mods = list(MOD_PARTS)
        for kind, j in FFN_ORDER:
            chunks.append((("ffn", kind, j), ffn_src(kind, j), (ffn_u, "q", QUARTER[kind, j, 3])))
            if kind == "w3" and mods:
                mod_chunks(1, mods.pop(0))
        win_chunks(1)
        wout_chunks(1)
        NPRE = len(chunks)
        number = {key: n for n, (key, _, _) in enumerate(chunks)}

        def mod_bank(l, n):
            return bank[3] if l == 0 and n >= 2 else bank[n] if l == 0 else bank[0]

        def slot(n):
            return ring[:, n % RING, :]

        def wide(key):
            cols = 9 * G - 4 * W if key[0] == "win" and key[2] == 4 else W
            return slot(number[key])[:, 0:KB * cols].rearrange("p (k n) -> p k n", n=cols)

        def arrived(eng, key):
            n = number[key]
            eng.wait_ge(landed[n % RING], 16 * (n // RING + 1))

        def moe_slot(u, i):
            return slot(NPRE + u * NCH + i)

        def moe_low(u, i):
            return ring_low[:, (NPRE + u * NCH + i) % RING, :]

        def moe_arrived(eng, q, g, u, i):
            n = NPRE + u * NCH + i
            turns = PAIR * NCH // RING
            eng.wait_ge(landed[n % RING], ((n // RING + 1) + turns * (q * (NE // PAIR) + g)) * 16)

        def unit_at(r, m):
            return r * UNITS + m + 1

        def used_at(r, m):
            return HIGHS + r * UNITS + m + 1

        def quarter(tensor, u):
            kind, j, hb = u
            place = tensor[:, number[("ffn", kind, j)] % RING, :]
            if kind == "w2":
                return place.rearrange("p (o b n) -> p o b n", o=1, n=D)[:, :, hb, :]
            return place.rearrange("p (k n) -> p k n", n=W)[:, :, hb * P:(hb + 1) * P]

        def quarter_high(m):
            t = tmp_r[:, 6 + 2 * (m % HIGHS):8 + 2 * (m % HIGHS), :].rearrange("p a n -> p (a n)")
            if QUARTERS[m][0] == "w2":
                return t.rearrange("p (o n) -> p o n", o=1)
            return t.rearrange("p (k n) -> p k n", n=P)

        def expert(q, g, u):
            return q * NE + g * PAIR + u

        block = ctx.enter_context(nc.Block())

        @block.sync
        def _(eng):
            for n, (key, src, _) in enumerate(chunks):
                if key == ("win", 0, WIN_ORDER[0]):
                    eng.wait_ge(s_rows, 16 * N_ROW_LOADS)
                if n >= RING:
                    s, name, rep = chunks[n - RING][2]
                    eng.wait_ge(s.sem, s.at(name, rep))
                if key[0] == "ffn" and key[1] == "w2":
                    dst = slot(n).rearrange("p (b n) -> p b n", n=D)
                else:
                    dst = wide(key)
                eng.dma_start(dst, src).then_inc(landed[n % RING], 16)

            def load_expert(q, g, u, i, g_src):
                n = u * NCH + i - RING
                if n >= 0:
                    eng.wait_ge(unit_used, used_at(expert(q, g, n // NCH), 2 * (n % NCH) + 1))
                elif q == 0 and g_src is None:
                    s, name, rep = chunks[NPRE + n][2]
                    eng.wait_ge(s.sem, s.at(name, rep))
                else:
                    eng.wait_ge(unit_used, used_at(expert(q, g - 1, PAIR - 1), 2 * (NCH + n) + 1))
                kind, j = FFN_ORDER[i]
                w = a[f"moe_{kind}"][0]
                e = 0 if g_src is None else g_src * PAIR
                we = w[bass.ds(e + u, 1)] if g_src is not None else w[u:u + 1]
                if kind == "w2":
                    src = we.rearrange("e (b p) n -> (e p) b n", p=P)[:, j * W // P:(j + 1) * W // P, :]
                    dst = moe_slot(u, i).rearrange("p (b n) -> p b n", n=D)
                else:
                    src = we.rearrange("e (k p) n -> (e p) k n", p=P)[:, :, j * W:(j + 1) * W]
                    dst = moe_slot(u, i).rearrange("p (k n) -> p k n", n=W)
                eng.dma_start(dst, src).then_inc(landed[(NPRE + u * NCH + i) % RING], 16)

            def load_pass(q):
                for i in range(RING):
                    load_expert(q, 0, 0, i, None)
                with eng.Fori(0, NE // PAIR - 1) as g:
                    for c in range(RING, PAIR * NCH):
                        load_expert(q, g, c // NCH, c % NCH, g)
                    for i in range(RING):
                        load_expert(q, g + 1, 0, i, g + 1)
                last = NE // PAIR - 1
                for c in range(RING, PAIR * NCH):
                    load_expert(q, last, c // NCH, c % NCH, last)

            load_pass(0)
            eng.wait_ge(route_v.sem, route_v.at("most_i"))
            with eng.If(eng.value_load(most_i[0:1, 0:1], min_val=0, max_val=T) > SLOTS):
                load_pass(1)
            for tt in range(TT):
                eng.wait_ge(end_v.sem, end_v.at(f"out{tt}"))
                eng.dma_start(out[0, tt * P:(tt + 1) * P, :], xn[:, tt, :]).then_inc(s_out, 16)
            eng.wait_ge(s_out, 16 * TT)

        @block.gpsimd
        def _(eng):
            def load_blocks(l):
                for k, w in enumerate((a["pool_w"], a["lru_wa"], a["lru_wx"])):
                    for q in range(2):
                        eng.dma_start(blocks[q * HD:(q + 1) * HD, k, :, q * HD:(q + 1) * HD],
                                      w[l].rearrange("(b q) i j -> q i b j", q=2)[q]).then_inc(s_blk, 16)

            def load_mask(l):
                eng.dma_start(tmp[:, 13, :].rearrange("p (h s) -> p h s", h=NH),
                              a["sgu_ws"][l].rearrange("h t s -> t h s")).then_inc(s_ws, 16)
                eng.dma_start(sgu_bias[:, :], a["sgu_b"][l]).then_inc(s_ws, 16)

            def load_gate(l, part):
                col = MOD_COL[part] * D
                eng.dma_start(gate_row[:, :], a["b_mod"][l:l + 1, col:col + D].to_broadcast([P, D]))\
                   .then_inc(s_gate, 16)

            consts_made = 0

            def made(ins):
                nonlocal consts_made
                consts_made += 1
                ins.then_inc(s_const, 1)
                eng.wait_ge(s_const, consts_made)

            made(eng.memset(consts[:, :, :], 1.0))
            made(eng.affine_select(out=ident, in_=ident, compare_op=ALU.is_equal, fill=0.0, base=0,
                                   pattern=[[-1, P]], channel_multiplier=1))
            made(eng.affine_select(out=triu, in_=triu, compare_op=ALU.is_ge, fill=0.0, base=0,
                                   pattern=[[1, P]], channel_multiplier=-1))
            made(eng.affine_select(out=before, in_=before, compare_op=ALU.is_ge, fill=0.0, base=-1,
                                   pattern=[[1, P]], channel_multiplier=-1))
            made(eng.affine_select(out=head_ones[:, 0:HD], in_=head_ones[:, 0:HD], compare_op=ALU.is_ge, fill=0.0,
                                   base=HD - 1, pattern=[[0, HD]], channel_multiplier=-1))
            made(eng.affine_select(out=head_ones[:, HD:P], in_=head_ones[:, HD:P], compare_op=ALU.is_ge, fill=0.0,
                                   base=-HD, pattern=[[0, HD]], channel_multiplier=1))
            made(eng.iota(iota_f, [[1, P]], base=0, channel_multiplier=0, allow_small_or_imprecise_dtypes=True))
            made(eng.tensor_copy(head_sel[:, 0:1], head_ones[:, 0:1]))
            made(eng.tensor_copy(head_sel[:, 1:2], head_ones[:, HD:HD + 1]))
            made(eng.memset(eps_col[:, :], EPS))
            assert consts_made == FIRST_CONSTS
            load_mask(0)
            load_gate(0, "g1")
            made(eng.memset(scan_keep[:, :], 1.0))
            made(eng.memset(scan_keep[:, 0:T:C], 0.0))
            made(eng.memset(chunk_of[:, :], 1.0))
            made(eng.affine_select(out=chunk_of[:, :], in_=chunk_of[:, :], compare_op=ALU.is_ge, fill=0.0, base=0,
                                   pattern=[[-C, CT_]], channel_multiplier=1))
            made(eng.affine_select(out=chunk_of[:, :], in_=chunk_of[:, :], compare_op=ALU.is_ge, fill=0.0,
                                   base=C - 1, pattern=[[C, CT_]], channel_multiplier=-1))
            made(eng.memset(row_sel[:, :, :], 1.0))
            made(eng.affine_select(out=row_sel[:, :, :], in_=row_sel[:, :, :], compare_op=ALU.is_ge, fill=0.0,
                                   base=HD - 1, pattern=[[-P, CB], [-1, P]], channel_multiplier=HD))
            made(eng.affine_select(out=row_sel[:, :, :], in_=row_sel[:, :, :], compare_op=ALU.is_ge, fill=0.0,
                                   base=0, pattern=[[P, CB], [1, P]], channel_multiplier=-HD))
            made(eng.memset(x_pad[:, :, :], 0.0))
            made(eng.memset(blocks[:, :, :, :], 0.0))
            made(eng.memset(tri[:, :, :, :], 0.0))
            made(eng.memset(state[:, :, 0, :], 0.0))
            assert consts_made == MIX_CONSTS
            load_blocks(0)
            pos = band_b[:, 0, 0:1]
            made(eng.memset(band_a[:, :, :], 1.0))
            for g, win in enumerate(WINDOWS):
                made(eng.memset(band_a[:, g, :], 1.0 / win))
                for t in range(win - 1):
                    made(eng.memset(band_a[:, g, t:t + 1], 1.0 / (t + 1)))
                made(eng.memset(band_b[:, g, :], 1.0 / win))
                for m, n in ((band_a[:, g, :], EDGE), (band_b[:, g, :], P)):
                    made(eng.affine_select(out=m, in_=m, compare_op=ALU.is_ge, fill=0.0, base=0,
                                           pattern=[[1, n]], channel_multiplier=-1))
                    made(eng.affine_select(out=m, in_=m, compare_op=ALU.is_ge, fill=0.0, base=win - 1,
                                           pattern=[[-1, n]], channel_multiplier=1))
                    made(eng.tensor_tensor(m[:, 0:P], m[:, 0:P], ident, ALU.subtract))
            assert consts_made == N_CONSTS

            def mod_part(n):
                eng.wait_ge(mod_t.sem, mod_t.at("sum", n - 2))
                for half in range(2):
                    key = ("mod", 0, MOD_PARTS[n], half)
                    arrived(eng, key)
                    w = wide(key)
                    done(eng, eng.tensor_tensor(w, w, c_act[:, :].unsqueeze(2).to_broadcast([P, KB, W]), ALU.mult).then_inc(mod_p.sem, 1),
                         mod_p, f"c{half}", n - 2)
                    k = KB // 2
                    while k > 1:
                        done(eng, eng.tensor_tensor(w[:, 0:k, :], w[:, 0:k, :], w[:, k:2 * k, :], ALU.add).then_inc(mod_p.sem, 1),
                             mod_p, f"s{half}k{k}", n - 2)
                        k //= 2
                    done(eng, eng.tensor_tensor(mod_acc[:, n % 2, half * W:(half + 1) * W], w[:, 0, :], w[:, 1, :],
                                                ALU.add).then_inc(mod_p.sem, 1), mod_p, f"s{half}k{k}", n - 2)

            eng.wait_ge(pre_a.sem, pre_a.at("c"))
            for n in range(2, len(MOD_PARTS)):
                mod_part(n)
            eng.wait_ge(res_v.sem, res_v.at("r7", 0))
            load_gate(0, "g2")
            eng.wait_ge(mix_t.sem, mix_t.at("apool", 0))
            load_blocks(1)
            eng.wait_ge(mix_v.sem, mix_v.at("yd1", 0))
            load_mask(1)
            eng.wait_ge(res_v.sem, res_v.at("r7", 1))
            load_gate(1, "g1")
            eng.wait_ge(res_v.sem, res_v.at("r7", 2))
            load_gate(1, "g2")
            eng.dma_start(router[:, :, :], a["router_w"][0].rearrange("(k p) e -> p k e", p=P)).then_inc(s_router, 16)
            eng.dma_start(router_bias[:, :], a["router_b"][0:1, :]).then_inc(s_router, 16)
            eng.wait_ge(res_v.sem, res_v.at("r7", 2 * DEPTH - 1))
            eng.dma_start(gate_row[:, :], a["norm_final"].rearrange("(o d) -> o d", o=1).to_broadcast([P, D]))\
               .then_inc(s_gate, 16)

        @block.tensor
        def _(eng):
            mm = nc.tensor.matmul

            def row_sum_columns(l, part):
                n = MOD_PARTS.index(part)
                s, name, at = mod_summed(l, n)
                eng.wait_ge(s.sem, s.at(name, at))
                b = mod_bank(l, n)
                if 4 * l + n >= 3:
                    eng.wait_ge(mod_e.sem, mod_e.at("fin", 4 * l + n - 1))
                if l == 1:
                    eng.wait_ge(ffn_a.sem, ffn_a.at("s0", n + 1))
                for k in range(KB):
                    ins = mm(b[:, n * KB + k:n * KB + k + 1], mod_acc[:, n % 2, k * P:(k + 1) * P], ones[:, 0:1], start=True, stop=True)
                mark(ins.then_inc(mod_t.sem, 1), mod_t, "sum")

            def row_sum_wide(l, which, b):
                n = 4 + which
                s, name, at = mod_summed(l, n)
                eng.wait_ge(s.sem, s.at(name, at))
                for half in range(2):
                    ins = mm(b[half][:, :], ones, mod_acc[:, n % 2, half * W:(half + 1) * W], start=True, stop=True)
                mark(ins.then_inc(gate_t.sem, 1), gate_t, "sum")

            def turn_xn(q):
                eng.wait_ge(norm_v.sem, norm_v.at("xn1", q))
                for b in range(4):
                    for i in range(2):
                        for tt in range(TT):
                            ins = nc.tensor.transpose(bank[4 + b][:, i * T + tt * P:i * T + (tt + 1) * P],
                                                      xn[:, tt, (2 * b + i) * P:(2 * b + i + 1) * P], ident)
                    mark(ins.then_inc(norm_t.sem, 1), norm_t, f"t{b}")

            def mixers(l):
                free = {"px": (mix_a, "sig"), "pg": (mix_v, "v"), "pv": (mix_a, "q"), "dg": (mix_a, "xp"),
                        "pu": (mix_a, "gate_c"), "pa": (mix_a, "gv1")}

                def project(name):
                    b = bank[GROUPS.index(name) % 3]
                    c, off = COLS[name] // W, COLS[name] % W
                    arrived(eng, ("win", l, c))
                    if name in free:
                        s, reader = free[name]
                        eng.wait_ge(s.sem, s.at(reader, l))
                    w = wide(("win", l, c))
                    for i in range(2):
                        for k in range(KB):
                            if name in ("di", "pv", "pa"):
                                ins = mm(b[:, i * G:(i + 1) * G], h_t[:, k, i * P:(i + 1) * P], w[:, k, off:off + G],
                                         start=k == 0, stop=k == KB - 1)
                            else:
                                ins = mm(b[:, i * T:(i + 1) * T], w[:, k, off + i * P:off + (i + 1) * P], h_t[:, k, :],
                                         start=k == 0, stop=k == KB - 1)
                    mark(ins.then_inc(mix_t.sem, 1), mix_t, name)

                def channel_sum(b, src, name):
                    for i in range(CB):
                        ins = mm(b[:, 0:T], ones, src[:, i * T:(i + 1) * T], start=i == 0, stop=i == CB - 1)
                    mark(ins.then_inc(mix_t.sem, 1), mix_t, name)

                eng.wait_ge(norm_a.sem, norm_a.at("h5", 2 * l))
                eng.wait_ge(norm_v.sem, norm_v.at("h7", 2 * l))
                project("dfz")
                eng.wait_ge(s_ws, 32 * (l + 1))
                for h in range(NH):
                    ins = nc.tensor.transpose(bank[3][:, h * P:(h + 1) * P], tmp[:, 13, h * P:(h + 1) * P], ident)
                mark(ins.then_inc(mix_t.sem, 1), mix_t, "ws")
                project("di")
                project("dq")
                eng.wait_ge(mix_a.sem, mix_a.at("kh", l))
                for tt in range(TT):
                    for i in range(CB):
                        ins = nc.tensor.transpose(bank[4][:, tt * G + i * P:tt * G + (i + 1) * P],
                                                  tmp[:, 4, i * T + tt * P:i * T + (tt + 1) * P], ident)
                mark(ins.then_inc(mix_t.sem, 1), mix_t, "kt")
                project("px")
                eng.wait_ge(mix_a.sem, mix_a.at("kt", l))
                for n, (i, tt, q) in enumerate((i, tt, q) for i in range(CB) for tt in range(TT) for q in range(2)):
                    h = 2 * i + q
                    eng.wait_ge(mix_v.sem, mix_v.at(f"vx{n}", l))
                    b = bank[6 + tt] if i == 0 else bank[4 + tt]
                    ins = mm(b[q * HD:(q + 1) * HD, :], tmp[:, 5, tt * G + h * HD:tt * G + (h + 1) * HD],
                             v_wide[:, n % 2, :], start=True, stop=True)
                    mark(ins.then_inc(mix_t.sem, 1), mix_t, f"u{n}")
                project("pg")
                project("pv")
                eng.wait_ge(mix_v.sem, mix_v.at("xc1", l))
                eng.wait_ge(s_blk, 96 * (l + 1))
                eng.wait_ge(chain_v.sem, chain_v.at("s", l * CHAIN + CHAIN - 1))
                for k, name in ((1, "wa"), (2, "wx")):
                    for i in range(CB):
                        ins = mm(bank[3 + k][:, i * T:(i + 1) * T], blocks[:, k, i, :], tmp[:, 7, i * T:(i + 1) * T],
                                 start=True, stop=True)
                    mark(ins.then_inc(mix_t.sem, 1), mix_t, name)
                def scores(i):
                    for r in range(C):
                        eng.wait_ge(tri_q.sem, tri_q.at("q", (l * CB + i) * C + r))
                        for tt in range(TT):
                            c0 = (tt * CB + i) * 2 * C
                            ins = mm(bank[6][:, c0 + r:c0 + 2 * C:C],
                                     tri[:, r, tt * CT_:(tt + 1) * CT_, :].rearrange("p i s -> p (i s)"),
                                     head_sel[:, :], start=True, stop=True)
                    mark(ins.then_inc(mix_t.sem, 1), mix_t, f"sc{i}")

                scores(0)
                if l == 0:
                    eng.wait_ge(mix_v.sem, mix_v.at("wst", l))
                    row_sum_columns(0, "sh2")
                project("dg")
                project("pu")
                project("pa")
                scores(1)
                if l == 0:
                    row_sum_columns(0, "sc2")
                    eng.wait_ge(mod_e.sem, mod_e.at("fin", 3))
                eng.wait_ge(mix_v.sem, mix_v.at("wst", l))
                for tt in range(TT):
                    eng.wait_ge(mix_v.sem, mix_v.at(f"sf{tt}", l))
                    for h in range(NH):
                        q, i = h % 2, h // 2
                        mm(bank[3][q * HD:(q + 1) * HD, i * T + tt * P:i * T + (tt + 1) * P],
                           tmp[:, 6, tt * G + h * HD:tt * G + (h + 1) * HD], s_full[:, tt, h, :],
                           start=tt == 0 and i == 0, stop=False, skip_group_check=True)
                eng.wait_ge(mix_v.sem, mix_v.at("qt", l))
                for h in range(NH):
                    q, i = h % 2, h // 2
                    for c in range(1, NC):
                        ins = mm(bank[3][q * HD:(q + 1) * HD, i * T + c * C:i * T + (c + 1) * C],
                                 state[q * HD:(q + 1) * HD, i, c, :],
                                 tmp[q * HD:(q + 1) * HD, 3, i * T + c * C:i * T + (c + 1) * C],
                                 start=False, stop=h >= 2 and c == NC - 1, skip_group_check=True)
                mark(ins.then_inc(mix_t.sem, 1), mix_t, "o")
                eng.wait_ge(mix_v.sem, mix_v.at("vn1", l))
                eng.wait_ge(mix_v.sem, mix_v.at("wst", l))
                eng.wait_ge(mix_a.sem, mix_a.at("r1", l))
                for tt in range(TT):
                    for i in range(CB):
                        mm(bank[4][:, i * T + tt * P:i * T + (tt + 1) * P], row_sel[:, i, :], sgu_bias[:, :],
                           start=tt == 0 and i == 0, stop=False, skip_group_check=True)
                for tt in range(TT):
                    for h in range(NH):
                        q, i = h % 2, h // 2
                        ins = mm(bank[4][q * HD:(q + 1) * HD, i * T + tt * P:i * T + (tt + 1) * P],
                                 tmp[:, 4, tt * G + h * HD:tt * G + (h + 1) * HD], ws_t[:, h, :],
                                 start=False, stop=True, skip_group_check=True)
                mark(ins.then_inc(mix_t.sem, 1), mix_t, "z")
                eng.wait_ge(mix_a.sem, mix_a.at("sqd", l))
                eng.wait_ge(chain_v.sem, chain_v.at("s", l * CHAIN + CHAIN - 1))
                mark(mm(bank[7][:, :], head_ones, tmp[:, 2, :], start=True, stop=True).then_inc(mix_t.sem, 1),
                     mix_t, "ssd")
                eng.wait_ge(mix_a.sem, mix_a.at("sqc", l))
                eng.wait_ge(mix_a.sem, mix_a.at("i1", l))
                channel_sum(bank[5], tmp[:, 8, :], "ssc")
                eng.wait_ge(mix_a.sem, mix_a.at("pa", l))
                eng.wait_ge(mix_v.sem, mix_v.at("sf1", l))
                eng.wait_ge(s_const, N_CONSTS)
                for g in range(NH):
                    q, i = g % 2, g // 2
                    mm(bank[6][q * HD:(q + 1) * HD, i * T:i * T + EDGE], tmp[:, 11, g * HD:(g + 1) * HD],
                       band_a[:, g, :], start=i == 0, stop=False, skip_group_check=True)
                    ins = mm(bank[6][q * HD:(q + 1) * HD, i * T + P:(i + 1) * T],
                             tmp[:, 11, G + g * HD:G + (g + 1) * HD], band_b[:, g, :],
                             start=False, stop=True, skip_group_check=True)
                mark(ins.then_inc(mix_t.sem, 1), mix_t, "aband")
                eng.wait_ge(mix_a.sem, mix_a.at("sqb", l))
                eng.wait_ge(mix_a.sem, mix_a.at("rtd", l))
                channel_sum(bank[7], tmp[:, 4, :], "ssb")
                eng.wait_ge(mix_a.sem, mix_a.at("pd", l))
                eng.wait_ge(mix_v.sem, mix_v.at("yb_raw", l))
                for i in range(CB):
                    ins = mm(bank[4][:, i * T:(i + 1) * T], blocks[:, 0, i, :], tmp[:, 6, i * T:(i + 1) * T],
                             start=True, stop=True)
                mark(ins.then_inc(mix_t.sem, 1), mix_t, "apool")
                eng.wait_ge(mix_a.sem, mix_a.at("sqa", l))
                eng.wait_ge(mix_a.sem, mix_a.at("rtc", l))
                channel_sum(bank[5], tmp[:, 1, :], "ssa")
                for half in range(2):
                    arrived(eng, ("wout", l, half))
                for name in ("gate_d", "gu", "pa"):
                    eng.wait_ge(mix_a.sem, mix_a.at(name, l))
                eng.wait_ge(mix_v.sem, mix_v.at("od", l))
                for n, (name, g) in enumerate((("yc1", 2), ("yd1", 3), ("yb1", 1), ("ya1", 0))):
                    eng.wait_ge(mix_v.sem, mix_v.at(name, l))
                    for tt in range(TT):
                        for half in range(2):
                            for i in range(2 * g, 2 * g + 2):
                                ins = mm(bank[2 * tt + half][:, :], y_t[:, i, tt * P:(tt + 1) * P],
                                         wide(("wout", l, half))[:, i, :], start=n == 0 and i == 2 * g,
                                         stop=n == 3 and i == 2 * g + 1)
                            if n == 3:
                                mark(ins.then_inc(mix_t.sem, 1), mix_t, f"wout{2 * tt + half}")
                eng.wait_ge(mix_v.sem, mix_v.at("ya1", l))
                row_sum_wide(l, 0, (bank[5], bank[7]))

            def ffn():
                eng.wait_ge(part_v.sem, part_v.at("h1"))
                for m, (kind, j, hb) in enumerate(QUARTERS):
                    eng.wait_ge(ffn_l.sem, ffn_l.at("q", m))
                    w_h, w_l = quarter_high(m), quarter(ring_low, QUARTERS[m])
                    if kind != "w2":
                        i = hb // 2
                        b = bank[i] if kind == "w1" else bank[2 + i]
                        if hb % 2 == 0 and j:
                            if kind == "w1":
                                eng.wait_ge(ffn_a.sem, ffn_a.at(f"s{i}", j - 1))
                            else:
                                eng.wait_ge(ffn_v.sem, ffn_v.at(f"a{i}", j - 1))
                        if kind == "w1" and hb == 0 and 2 <= j < 6:
                            eng.wait_ge(mod_e.sem, mod_e.at("fin", 4 + j - 2))
                        for k in range(KB):
                            o = b[:, hb % 2 * T:(hb % 2 + 1) * T]
                            mm(o, w_h[:, k, :], h_high[:, k, :], start=k == 0, stop=False)
                            mm(o, w_l[:, k, :], h_high[:, k, :], start=False, stop=False)
                            ins = mm(o, w_h[:, k, :], h_low[:, k, :], start=False, stop=k == KB - 1)
                    else:
                        if hb == 0:
                            if j < 4:
                                row_sum_columns(1, MOD_PARTS[j])
                            eng.wait_ge(part_v.sem, part_v.at(f"a{j}"))
                        high = at_high[:, hb // 2, hb % 2 * T:(hb % 2 + 1) * T]
                        low_ = tmp_r[:, 2 + 2 * (j % 2) + hb // 2, hb % 2 * T:(hb % 2 + 1) * T]
                        for tt in range(TT):
                            for half in range(2):
                                o, c, t = bank[4 + 2 * tt + half][:, :], slice(half * W, (half + 1) * W), slice(tt * P, (tt + 1) * P)
                                mm(o, high[:, t], w_h[:, 0, c], start=j == 0 and hb == 0, stop=False)
                                mm(o, high[:, t], w_l[:, 0, c], start=False, stop=False)
                                ins = mm(o, low_[:, t], w_h[:, 0, c], start=False, stop=j == NJ - 1 and hb == HB - 1)
                    mark(ins.then_inc(ffn_u.sem, 1), ffn_u, "q")

            def routing():
                eng.wait_ge(s_router, 32)
                for tt in range(TT):
                    for k in range(KB):
                        ins = mm(bank[2][:, tt * NE:(tt + 1) * NE], h_t[:, k, tt * P:(tt + 1) * P], router[:, k, :],
                                 start=k == 0, stop=False)
                        if tt == 0 and k < HIGHS:
                            ins.then_inc(unit_used, 1)
                    ins = mm(bank[2][:, tt * NE:(tt + 1) * NE], ones[0:1, :], router_bias[:, :], start=False, stop=True)
                mark(ins.then_inc(route_t.sem, 1), route_t, "logits")
                eng.wait_ge(route_v.sem, route_v.at("sel", 0))
                mm(bank[2][:, 64:64 + NE], before, route[:, 8, 0, :], start=True, stop=True)
                mm(bank[2][:, 64 + NE:64 + 2 * NE], ones, route[:, 8, 0, :], start=True, stop=False)
                mm(bank[2][:, 64 + NE:64 + 2 * NE], before, route[:, 8, 1, :], start=False, stop=True)
                mm(bank[2][:, 64 + 2 * NE:64 + 3 * NE], ones, route[:, 8, 0, :], start=True, stop=False)
                ins = mm(bank[2][:, 64 + 2 * NE:64 + 3 * NE], ones, route[:, 8, 1, :], start=False, stop=True)
                mark(ins.then_inc(route_t.sem, 1), route_t, "pos")
                eng.wait_ge(gate_v.sem, gate_v.at("g1", 2 * DEPTH - 1))

            def gather(b, u, first, name, s):
                for k in range(4):
                    for tt in range(TT):
                        ins = mm(b[:, k * P:(k + 1) * P], xn[:, tt, (first + k) * P:(first + k + 1) * P],
                                 dispatch[:, u, tt, :], start=tt == 0, stop=tt == TT - 1)
                mark(ins.then_inc(s.sem, 1), s, name)

            def experts(q):
                eng.wait_ge(slot_v.sem, slot_v.at("disp", q))
                gather(bank[4], 0, 0, "g0", slot_t)
                gather(bank[5], 0, 4, "g1", slot_t)
                eng.wait_ge(slot_a.sem, slot_a.at("spread", q))
                with eng.Fori(0, NE // PAIR) as g:
                    for u in range(PAIR):
                        one_expert(q, g, u)
                combine(q * (NE + 1) + NE)

            def one_expert(q, g, u):
                r = expert(q, g, u)
                fill = q * (NE + 1) + g * PAIR + u

                def three(out_, x_h, x_l, w_h, w_l, first, last):
                    mm(out_, x_h, w_h, start=first, stop=False)
                    mm(out_, x_h, w_l, start=False, stop=False)
                    return mm(out_, x_l, w_h, start=False, stop=last)

                def up(j, name, b):
                    i = FFN_ORDER.index((name, j))
                    w_l = moe_low(u, i).rearrange("p (k n) -> p k n", n=W)
                    for part in range(2):
                        m = 2 * i + part
                        w_h = w_high[:, m % HIGHS, :].rearrange("p (k n) -> p k n", n=W)
                        eng.wait_ge(low_made, unit_at(r, m))
                        for kk in range(KB // 2):
                            k = part * KB // 2 + kk
                            ins = three(b[:, :], x_high[:, u % 2, k, :], x_low[:, u % 2, k, :], w_h[:, kk, :],
                                        w_l[:, k, :], k == 0, k == KB - 1)
                        ins.then_inc(unit_used, 1)

                def turn(j):
                    eng.wait_ge(moe_v.sem, moe_v.at(f"m{j}", r))
                    if j == 0:
                        eng.wait_ge(sum_v.sem, sum_v.at("a2", fill + 1))
                    if j:
                        eng.wait_ge(moe_v.sem, moe_v.at(f"al{j - 1}", r))
                    for hb in range(W // P):
                        ins = nc.tensor.transpose(bank[6][:, hb * P:(hb + 1) * P],
                                                  act_m[:, j % 2, hb * P:(hb + 1) * P], ident)
                    mark(ins.then_inc(moe_t.sem, 1), moe_t, f"t{j}")

                def down(j):
                    i = FFN_ORDER.index(("w2", j))
                    eng.wait_ge(moe_v.sem, moe_v.at(f"al{j}", r))
                    w_l = moe_low(u, i).rearrange("p (b n) -> p b n", n=D)
                    for part in range(2):
                        m = 2 * i + part
                        w_h = w_high[:, m % HIGHS, :].rearrange("p (b n) -> p b n", n=D)
                        eng.wait_ge(low_made, unit_at(r, m))
                        for half in range(2):
                            c = slice(half * W, (half + 1) * W)
                            for bb in range(HB // 2):
                                hb = part * HB // 2 + bb
                                h = slice(hb * P, (hb + 1) * P)
                                ins = three(bank[4 + half][:, :], act_high[:, j % 2, h], act_low[:, j % 2, h],
                                            w_h[:, bb, c], w_l[:, hb, c], j == 0 and hb == 0,
                                            j == NJ - 1 and hb == HB - 1)
                        ins.then_inc(unit_used, 1)

                for j in range(NJ):
                    if j == 0:
                        eng.wait_ge(fill_v.sem, fill_v.at("lb", fill))
                    if j == 1:
                        eng.wait_ge(sum_v.sem, sum_v.at("a1", fill + 1))
                    if j >= 2:
                        eng.wait_ge(moe_a.sem, moe_a.at(f"s{j - 2}", r))
                    up(j, "w1", bank[j % 2])
                    if j == 0:
                        combine(fill)
                    if j:
                        turn(j - 1)
                    if j == 1:
                        eng.wait_ge(sum_v.sem, sum_v.at("a3", fill + 1))
                        for tt in range(TT):
                            ins = nc.tensor.transpose(bank[7][:, tt * P:(tt + 1) * P], dispatch[:, u, tt, :], ident)
                        mark(ins.then_inc(moe_t.sem, 1), moe_t, "spread")
                    if j == GATHER:
                        eng.wait_ge(moe_v.sem, moe_v.at("disp", r))
                        eng.wait_ge(moe_a.sem, moe_a.at("spread", r))
                        gather(bank[7], (u + 1) % 2, 0, "ga", moe_t)
                    if j == GATHER + 1:
                        eng.wait_ge(fill_a.sem, fill_a.at("x3", fill + 1))
                        gather(bank[7], (u + 1) % 2, 4, "gb", moe_t)
                    if j >= 2:
                        eng.wait_ge(moe_v.sem, moe_v.at(f"m{j - 2}", r))
                    up(j, "w3", bank[2 + j % 2])
                    if j:
                        down(j - 1)
                turn(NJ - 1)
                down(NJ - 1)

            def combine(rep):
                eng.wait_ge(comb_a.sem, comb_a.at("yh0", rep))
                eng.wait_ge(comb_v.sem, comb_v.at("yl1", rep))
                for n, b in enumerate((1, 3, 6, 7)):
                    tt, half = n // 2, n % 2
                    mm(bank[b][:, :], spread[:, tt * P:(tt + 1) * P], y_high[:, half * W:(half + 1) * W],
                       start=True, stop=False)
                    mark(mm(bank[b][:, :], spread[:, tt * P:(tt + 1) * P], y_low[:, half * W:(half + 1) * W],
                            start=False, stop=True).then_inc(comb_t.sem, 1), comb_t, f"c{n}")

            eng.wait_ge(s_const, FIRST_CONSTS)
            eng.wait_ge(s_c, 16)
            mark(nc.tensor.transpose(bank[2][:, 0:KB], c_row[:, :], ident[0:KB, 0:KB]).then_inc(pre_t.sem, 1),
                 pre_t, "c")
            for l in range(DEPTH):
                turn_xn(2 * l)
                if l == 0:
                    eng.wait_ge(s_rows, 16 * N_ROW_LOADS)
                    for ll in range(DEPTH):
                        ins = nc.tensor.transpose(bank[3][:, ll * P:ll * P + NROWS], prow[:, ll, :], ident[0:NROWS, 0:NROWS])
                    mark(ins.then_inc(pre_t.sem, 1), pre_t, "rows")
                    row_sum_columns(0, "sh1")
                    row_sum_columns(0, "sc1")
                    eng.wait_ge(s_const, MIX_CONSTS)
                mixers(l)
                turn_xn(2 * l + 1)
                if l == 0:
                    row_sum_wide(l, 1, (bank[0], bank[1]))
                    eng.wait_ge(gate_v.sem, gate_v.at("g1", 2 * l + 1))
                    eng.wait_ge(norm_a.sem, norm_a.at("h5", 2 * l + 1))
                    eng.wait_ge(norm_v.sem, norm_v.at("h7", 2 * l + 1))
                    ffn()
            row_sum_wide(1, 1, (bank[0], bank[1]))
            eng.wait_ge(norm_a.sem, norm_a.at("h5", 3))
            eng.wait_ge(norm_v.sem, norm_v.at("h7", 3))
            routing()
            experts(0)
            eng.wait_ge(route_v.sem, route_v.at("most_i"))
            with eng.If(eng.value_load(most_i[0:1, 0:1], min_val=0, max_val=T) > SLOTS):
                experts(1)

        def rows2(ap):
            return ap.rearrange("p (b t) -> p b t", b=CB)

        @block.vector
        def _(eng):
            tt_, ts_, stt = nc.vector.tensor_tensor, nc.vector.tensor_scalar, nc.vector.scalar_tensor_tensor

            def mod_part(l, n):
                rep = n if l == 0 else n + 2
                if n >= 2:
                    eng.wait_ge(mod_t.sem, mod_t.at("sum", 4 * l + n - 2))
                elif l:
                    eng.wait_ge(gate_t.sem, gate_t.at("sum", 2 * (l - 1) + n))
                for half in range(2):
                    key = ("mod", l, MOD_PARTS[n], half)
                    arrived(eng, key)
                    dst = mod_acc[:, n % 2, half * W:(half + 1) * W]
                    for k in range(KB):
                        if k == 0:
                            ins = ts_(dst, wide(key)[:, 0, :], c_act[:, 0:1], None, ALU.mult)
                        else:
                            ins = stt(out=dst, in0=wide(key)[:, k, :], scalar=c_act[:, k:k + 1], in1=dst,
                                      op0=ALU.mult, op1=ALU.add)
                        done(eng, ins.then_inc(mod_v.sem, 1), mod_v, f"c{half}k{k}", rep)

            def mod_columns(l, part):
                n = MOD_PARTS.index(part)
                rep = 4 * l + n
                eng.wait_ge(mod_t.sem, mod_t.at("sum", rep))
                b = mod_bank(l, n)[:, n * KB:(n + 1) * KB]
                bias = par("b_" + part, l, 0, KB)
                gain = par("norm_mix" if n < 2 else "norm_ffn", l, 0, KB)
                if part.startswith("sh"):
                    done(eng, tt_(mod_tmp[:, :], b, bias, ALU.add).then_inc(mod_e.sem, 1), mod_e, "add", rep)
                    done(eng, nc.vector.tensor_copy(mod_col[:, rep, :], mod_tmp[:, :]).then_inc(mod_e.sem, 1),
                         mod_e, "fin", rep)
                else:
                    done(eng, stt(out=mod_tmp[:, :], in0=b, scalar=1.0, in1=bias, op0=ALU.add, op1=ALU.add).then_inc(mod_e.sem, 1),
                         mod_e, "add", rep)
                    done(eng, tt_(mod_col[:, rep, :], mod_tmp[:, :], gain, ALU.mult).then_inc(mod_e.sem, 1),
                         mod_e, "fin", rep)

            def gate(l, which, b):
                rep = 2 * l + which
                eng.wait_ge(s_gate, 16 * (rep + 1))
                eng.wait_ge(gate_t.sem, gate_t.at("sum", rep))
                for half in range(2):
                    g = gate_row[:, half * W:(half + 1) * W]
                    done(eng, tt_(g, b[half][:, :], g, ALU.add).then_inc(gate_v.sem, 1), gate_v, f"g{half}", rep)

            def norm_x(q):
                eng.wait_ge(norm_a.sem, norm_a.at("rt", q))
                done(eng, nc.vector.reciprocal(norm_s[:, 2, :], norm_s[:, 1, :]).then_inc(norm_v.sem, 1),
                     norm_v, "rc", q)
                for tt in range(TT):
                    done(eng, ts_(xn[:, tt, :], x[:, tt, :], norm_s[:, 2, tt:tt + 1], None, ALU.mult).then_inc(norm_v.sem, 1),
                         norm_v, f"xn{tt}", q)

            def norm_h(q):
                for b in (1, 3):
                    eng.wait_ge(norm_t.sem, norm_t.at(f"t{b}", q))
                    for i in range(2):
                        k = 2 * b + i
                        done(eng, ts_(h_t[:, k, :], bank[4 + b][:, i * T:(i + 1) * T],
                                      mod_col[:, 2 * q + 1, k:k + 1], mod_col[:, 2 * q, k:k + 1], ALU.mult, ALU.add).then_inc(norm_v.sem, 1),
                             norm_v, f"h{k}", q)

            def residual(rep, src, waits):
                t = h_t[:, 0:2, :].rearrange("p k t -> p (k t)") if rep < 3 else act_s[:, 0, :]
                for n in range(4):
                    tt, half = n // 2, n % 2
                    for s, name, last in waits[n]:
                        eng.wait_ge(s.sem, s.at(name, last))
                    c = slice(half * W, (half + 1) * W)
                    done(eng, tt_(t, src[n], gate_row[:, c], ALU.mult).then_inc(res_v.sem, 1),
                         res_v, f"r{2 * n}", rep)
                    done(eng, tt_(x[:, tt, c], x[:, tt, c], t, ALU.add).then_inc(res_v.sem, 1),
                         res_v, f"r{2 * n + 1}", rep)

            def mixers(l):
                def v(ins, name):
                    done(eng, ins, mix_v, name, l)

                def t(i):
                    return tmp[:, i, :]

                eng.wait_ge(mix_t.sem, mix_t.at("ws", l))
                v(tt_(ws_t[:, :, :], bank[3][:, :].rearrange("p (h n) -> p h n", h=NH),
                      triu.unsqueeze(1).to_broadcast([P, NH, P]), ALU.mult).then_inc(mix_v.sem, 1), "wst")
                eng.wait_ge(mix_a.sem, mix_a.at("sig", l))
                for i in range(CB):
                    c = slice(i * T, (i + 1) * T)
                    v(ts_(t(1)[:, c], t(0)[:, c], floor_col[:, l, 1, i:i + 1], floor_col[:, l, 0, i:i + 1],
                          ALU.mult, ALU.add).then_inc(mix_v.sem, 1), f"f{i}")
                for i in range(CB):
                    c = slice(i * T, (i + 1) * T)
                    v(ts_(t(2)[:, c], t(0)[:, c], floor_col[:, l, 2, i:i + 1], floor_col[:, l, 1, i:i + 1],
                          ALU.mult, ALU.add).then_inc(mix_v.sem, 1), f"k{i}")
                v(ts_(t(3), t(1), LN_FLOOR, None, ALU.max).then_inc(mix_v.sem, 1), "fa")
                v(ts_(t(4), t(1), MIN_FORGET, LN_FLOOR, ALU.max, ALU.min).then_inc(mix_v.sem, 1), "fb")
                v(ts_(t(2), t(2), LN_FLOOR, None, ALU.max).then_inc(mix_v.sem, 1), "kc")
                eng.wait_ge(mix_a.sem, mix_a.at("lnb", l))
                v(tt_(t(3), t(3), t(4), ALU.add).then_inc(mix_v.sem, 1), "lf")
                for i in range(CB):
                    c = slice(i * T, (i + 1) * T)
                    v(nc.vector.tensor_tensor_scan(t(1)[:, c], scan_keep[:, :], t(3)[:, c], 0.0, ALU.mult, ALU.add).then_inc(mix_v.sem, 1),
                      f"b{i}")
                eng.wait_ge(mix_a.sem, mix_a.at("lnk", l))
                v(tt_(t(2), t(1), t(2), ALU.subtract).then_inc(mix_v.sem, 1), "bk")
                b4 = t(1).rearrange("p (n s) -> p n s", s=C)
                bk4 = t(2).rearrange("p (n s) -> p n s", s=C)
                v(tt_(t(4).rearrange("p (n s) -> p n s", s=C), b4[:, :, C - 1:C].to_broadcast([P, CB * NC, C]), bk4,
                      ALU.subtract).then_inc(mix_v.sem, 1), "kd")

                def differences(i):
                    for r in range(C):
                        rep = (l * CB + i) * C + r
                        if i or l:
                            if i:
                                eng.wait_ge(mix_t.sem, mix_t.at(f"sc{i - 1}", l))
                            else:
                                eng.wait_ge(mix_t.sem, mix_t.at(f"sc{CB - 1}", l - 1))
                        n = slice(i * NC, (i + 1) * NC)
                        done(eng, tt_(tri[:, r, :, 0:r + 1], b4[:, n, r:r + 1].to_broadcast([P, NC, r + 1]),
                                      bk4[:, n, 0:r + 1], ALU.subtract).then_inc(tri_d.sem, 1), tri_d, "d", rep)

                def times_q(i):
                    q4 = t(0).rearrange("p (n s) -> p n s", s=C)
                    for r in range(C):
                        rep = (l * CB + i) * C + r
                        eng.wait_ge(tri_e.sem, tri_e.at("e", rep))
                        n = slice(i * NC, (i + 1) * NC)
                        done(eng, tt_(tri[:, r, :, 0:r + 1], tri[:, r, :, 0:r + 1],
                                      q4[:, n, r:r + 1].to_broadcast([P, NC, r + 1]), ALU.mult).then_inc(tri_q.sem, 1),
                             tri_q, "q", rep)

                def values_by_chunk(n):
                    i, tt, q = n // (2 * TT), n // 2 % TT, n % 2
                    h = 2 * i + q
                    if n >= 2:
                        eng.wait_ge(mix_t.sem, mix_t.at(f"u{n - 2}", l))
                    src = t(6)[:, tt * G + h * HD:tt * G + (h + 1) * HD]
                    v(tt_(v_wide[:, n % 2, :].rearrange("p (j c) -> p j c", j=CT_),
                          src.unsqueeze(1).to_broadcast([P, CT_, HD]),
                          chunk_of[:, :].unsqueeze(2).to_broadcast([P, CT_, HD]), ALU.mult).then_inc(mix_v.sem, 1),
                      f"vx{n}")

                eng.wait_ge(mix_t.sem, mix_t.at("di", l))
                v(nc.vector.tensor_copy(t(6), bank[1][:, :]).then_inc(mix_v.sem, 1), "v")
                differences(0)
                values_by_chunk(0)
                values_by_chunk(1)
                eng.wait_ge(mix_a.sem, mix_a.at("q", l))
                times_q(0)
                for n in range(2, 8):
                    values_by_chunk(n)
                eng.wait_ge(mix_a.sem, mix_a.at("xp", l))
                for i in range(CB):
                    c = slice(i * T, (i + 1) * T)
                    v(ts_(t(7)[:, c], x_pad[:, i, 0:T], par("conv_w", l, i), par("conv_b", l, i), ALU.mult, ALU.add).then_inc(mix_v.sem, 1),
                      f"cv{i}0")
                    for k in range(1, CONV):
                        v(stt(out=t(7)[:, c], in0=x_pad[:, i, k:k + T], scalar=par("conv_w", l, k * CB + i),
                              in1=t(7)[:, c], op0=ALU.mult, op1=ALU.add).then_inc(mix_v.sem, 1),
                          f"cv{i}{k}" if k < CONV - 1 else f"xc{i}")
                eng.wait_ge(mix_a.sem, mix_a.at("ea", l))
                eng.wait_ge(mix_t.sem, mix_t.at("u7", l))
                if l:
                    eng.wait_ge(mix_t.sem, mix_t.at("o", l - 1))
                ea = small[:, 8:12, :].rearrange("p a b -> p (a b)")
                for c in range(NC - 1):
                    for i in range(CB):
                        u = bank[(6 if i == 0 else 4) + c // CT_][:, (c % CT_) * HD:(c % CT_ + 1) * HD]
                        done(eng, stt(out=state[:, i, c + 1, :], in0=state[:, i, c, :],
                                      scalar=ea[:, i * NC + c:i * NC + c + 1], in1=u, op0=ALU.mult, op1=ALU.add).then_inc(chain_v.sem, 1),
                             chain_v, "s", l * CHAIN + c * CB + i)
                v(tt_(t(3), t(3), t(0), ALU.mult).then_inc(mix_v.sem, 1), "qt")
                differences(1)
                times_q(1)
                if l == 0:
                    mod_columns(0, "sh2")
                eng.wait_ge(mix_a.sem, mix_a.at("a1", l))
                v(tt_(t(11), t(10), t(10), ALU.mult).then_inc(mix_v.sem, 1), "a2")
                eng.wait_ge(mix_a.sem, mix_a.at("th1", l))
                v(stt(out=t(11), in0=t(11), scalar=1.0, in1=t(8), op0=ALU.add, op1=ALU.mult).then_inc(mix_v.sem, 1),
                  "m")
                v(ts_(t(11), t(11), 0.0, None, ALU.max).then_inc(mix_v.sem, 1), "m0")
                v(tt_(t(9), t(9), t(7), ALU.mult).then_inc(mix_v.sem, 1), "ix")
                eng.wait_ge(mix_a.sem, mix_a.at("sm", l))
                v(tt_(t(9), t(11), t(9), ALU.mult).then_inc(mix_v.sem, 1), "bb")
                for i in range(CB):
                    c = slice(i * T, (i + 1) * T)
                    v(nc.vector.tensor_tensor_scan(t(8)[:, c], t(10)[:, c], t(9)[:, c], 0.0, ALU.mult, ALU.add).then_inc(mix_v.sem, 1),
                      f"hs{i}")
                v(tt_(t(12), t(12), t(8), ALU.mult).then_inc(mix_v.sem, 1), "yc_raw")
                if l == 0:
                    mod_columns(0, "sc2")
                eng.wait_ge(mix_t.sem, mix_t.at("u7", l))
                eng.wait_ge(mix_t.sem, mix_t.at("sc1", l))
                for tt in range(TT):
                    sc = bank[6][:, tt * NH * C:(tt + 1) * NH * C].rearrange("p (h r) -> p h r", r=C)
                    v(tt_(s_full[:, tt, :, :].rearrange("p h (j r) -> p h j r", r=C),
                          sc.unsqueeze(2).to_broadcast([P, NH, CT_, C]),
                          chunk_of[:, :].unsqueeze(1).unsqueeze(3).to_broadcast([P, NH, CT_, C]), ALU.mult).then_inc(mix_v.sem, 1),
                      f"sf{tt}")
                eng.wait_ge(mix_a.sem, mix_a.at("gv1", l))
                v(ts_(small[:, 1, 0:2], small[:, 0, 0:2], -1.0 / G, None, ALU.mult).then_inc(mix_v.sem, 1), "mu")
                for tt in range(TT):
                    c = slice(tt * G, (tt + 1) * G)
                    v(ts_(t(4)[:, c], t(4)[:, c], small[:, 1, tt:tt + 1], None, ALU.add).then_inc(mix_v.sem, 1),
                      f"vc{tt}")
                eng.wait_ge(mix_a.sem, mix_a.at("rv", l))
                v(nc.vector.reciprocal(small[:, 4, 0:2], small[:, 3, 0:2]).then_inc(mix_v.sem, 1), "rvr")
                for tt in range(TT):
                    c = slice(tt * G, (tt + 1) * G)
                    v(ts_(t(4)[:, c], t(4)[:, c], small[:, 4, tt:tt + 1], None, ALU.mult).then_inc(mix_v.sem, 1),
                      f"vn{tt}")
                eng.wait_ge(mix_t.sem, mix_t.at("z", l))
                eng.wait_ge(mix_a.sem, mix_a.at("gu", l))
                v(tt_(t(7), t(7), bank[4][:, :], ALU.mult).then_inc(mix_v.sem, 1), "yb_raw")
                eng.wait_ge(mix_a.sem, mix_a.at("rtd", l))
                v(nc.vector.reciprocal(t(5), t(5)).then_inc(mix_v.sem, 1), "rec_d")
                v(tt_(t(2), bank[3][:, :], t(5), ALU.mult).then_inc(mix_v.sem, 1), "od")
                for i in range(CB):
                    c = slice(i * T, (i + 1) * T)
                    v(stt(out=y_t[:, 6 + i, :], in0=t(2)[:, c], scalar=par("hgrn_out", l, i), in1=t(13)[:, c],
                          op0=ALU.mult, op1=ALU.mult).then_inc(mix_v.sem, 1), f"yd{i}")
                for n, (name, at, rt, src, par_name) in enumerate((("c", 4, 9, 12, "lru_out"), ("b", 2, 10, 7, "sgu_out"),
                                                              ("a", 0, 2, 3, "pool_out"))):
                    eng.wait_ge(mix_a.sem, mix_a.at(f"rt{name}", l))
                    r = t(rt)[:, 0:T]
                    v(nc.vector.reciprocal(r, r).then_inc(mix_v.sem, 1), f"rec_{name}")
                    for i in range(CB):
                        c = slice(i * T, (i + 1) * T)
                        v(stt(out=y_t[:, at + i, :], in0=t(src)[:, c], scalar=par(par_name, l, i), in1=r,
                              op0=ALU.mult, op1=ALU.mult).then_inc(mix_v.sem, 1), f"y{name}{i}")

            def mod_step(n, step):
                half, first = step // (KB // 2), step % (KB // 2) * 2
                if step == 0:
                    if n >= 2:
                        eng.wait_ge(mod_t.sem, mod_t.at("sum", 4 + n - 2))
                    else:
                        eng.wait_ge(gate_t.sem, gate_t.at("sum", n))
                key = ("mod", 1, MOD_PARTS[n], half)
                if first == 0:
                    arrived(eng, key)
                dst = mod_acc[:, n % 2, half * W:(half + 1) * W]
                for k in range(first, first + 2):
                    if k == 0:
                        ins = ts_(dst, wide(key)[:, 0, :], c_act[:, 0:1], None, ALU.mult)
                    else:
                        ins = stt(out=dst, in0=wide(key)[:, k, :], scalar=c_act[:, k:k + 1], in1=dst,
                                  op0=ALU.mult, op1=ALU.add)
                    done(eng, ins.then_inc(mod_v.sem, 1), mod_v, f"c{half}k{k}", n + 2)

            def ffn():
                for half in range(2):
                    k = slice(half * KB // 2, (half + 1) * KB // 2)
                    eng.wait_ge(part_a.sem, part_a.at(f"h{half}"))
                    done(eng, tt_(h_low[:, k, :], h_t[:, k, :], h_high[:, k, :].bitcast(F32), ALU.subtract).then_inc(part_v.sem, 1),
                         part_v, f"h{half}")
                for m, (kind, j, hb) in enumerate(QUARTERS):
                    eng.wait_ge(ffn_h.sem, ffn_h.at("q", m))
                    mark(tt_(quarter(ring_low, QUARTERS[m]), quarter(ring, QUARTERS[m]),
                             quarter_high(m).bitcast(F32), ALU.subtract).then_inc(ffn_l.sem, 1), ffn_l, "q")
                    if m >= 2 and QUARTERS[m - 2][0] == "w3" and QUARTERS[m - 2][2] % 2 == 1:
                        _, jj, hh = QUARTERS[m - 2]
                        i = hh // 2
                        eng.wait_ge(ffn_a.sem, ffn_a.at(f"s{i}", jj))
                        eng.wait_ge(ffn_u.sem, ffn_u.at("q", m - 2))
                        if jj >= 2:
                            eng.wait_ge(ffn_u.sem, ffn_u.at("q", QUARTER["w2", jj - 2, 3]))
                        done(eng, tt_(tmp[:, 2 + 2 * (jj % 2) + i, :], tmp[:, i, :], bank[2 + i][:, :], ALU.mult).then_inc(ffn_v.sem, 1),
                             ffn_v, f"a{i}", jj)
                    if kind != "w2" and j < len(MOD_PARTS):
                        mod_step(j, m - QUARTER["w1", j, 0])
                    if kind == "w2" and hb == 1 and j < 4:
                        mod_columns(1, MOD_PARTS[j])
                    if (kind, hb) == ("w1", 3) and j:
                        at_low(j - 1)
                    if (kind, j, hb) == ("w2", NJ - 1, HIGHS - 1):
                        at_low(j)

            def at_low(j):
                eng.wait_ge(part_a.sem, part_a.at(f"a{j}"))
                a0 = 2 + 2 * (j % 2)
                done(eng, tt_(tmp_r[:, a0:a0 + 2, :], tmp[:, a0:a0 + 2, :], at_high[:, :, :].bitcast(F32),
                              ALU.subtract).then_inc(part_v.sem, 1), part_v, f"a{j}")

            def routing():
                done_ = lambda ins, name: done(eng, ins, route_v, name)
                R = route
                lg, eq, cand, sel1, lg2, sel2, w, pos, sel, wt = (R[:, i, :, :] for i in range(10))
                m1, f1, m2, d, r, er = (route_c[:, i, :, :] for i in range(6))
                wide_ = lambda c: c.to_broadcast([P, TT, NE])
                ids = iota_f[:, 0:NE].unsqueeze(1).to_broadcast([P, TT, NE])
                eng.wait_ge(route_t.sem, route_t.at("logits"))
                done_(nc.vector.tensor_copy(lg, bank[2][:, 0:TT * NE].rearrange("p (t e) -> p t e", t=TT)).then_inc(route_v.sem, 1),
                      "lg")
                for n, (src, m, s) in enumerate(((lg, m1, sel1), (lg2, m2, sel2))):
                    done_(nc.vector.tensor_reduce(m, src, X, ALU.max).then_inc(route_v.sem, 1), f"max{n}")
                    done_(tt_(eq, src, wide_(m), ALU.is_equal).then_inc(route_v.sem, 1), f"eq{n}")
                    done_(stt(out=cand, in0=eq, scalar=-100.0, in1=ids, op0=ALU.mult, op1=ALU.add).then_inc(route_v.sem, 1),
                          f"cand{n}")
                    done_(nc.vector.tensor_reduce(f1, cand, X, ALU.min).then_inc(route_v.sem, 1), f"first{n}")
                    done_(tt_(s, cand, wide_(f1), ALU.is_equal).then_inc(route_v.sem, 1), f"pick{n}")
                    if n == 0:
                        done_(stt(out=lg2, in0=s, scalar=-3e38, in1=lg, op0=ALU.mult, op1=ALU.add).then_inc(route_v.sem, 1),
                              "lg2")
                done_(tt_(sel, sel1, sel2, ALU.add).then_inc(route_v.sem, 1), "sel")
                done_(tt_(d, m2, m1, ALU.subtract).then_inc(route_v.sem, 1), "diff")
                eng.wait_ge(route_a.sem, route_a.at("exp"))
                done_(ts_(r, er, 1.0, None, ALU.add).then_inc(route_v.sem, 1), "one")
                done_(nc.vector.reciprocal(r, r).then_inc(route_v.sem, 1), "w1")
                done_(tt_(er, er, r, ALU.mult).then_inc(route_v.sem, 1), "w2")
                done_(tt_(w, sel1, wide_(r), ALU.mult).then_inc(route_v.sem, 1), "sw1")
                done_(tt_(wt, sel2, wide_(er), ALU.mult).then_inc(route_v.sem, 1), "sw2")
                done_(tt_(wt, wt, w, ALU.add).then_inc(route_v.sem, 1), "wt")
                eng.wait_ge(route_t.sem, route_t.at("pos"))
                done_(nc.vector.tensor_copy(pos, bank[2][:, 64:64 + TT * NE].rearrange("p (t e) -> p t e", t=TT)).then_inc(route_v.sem, 1),
                      "pos")
                done_(nc.vector.tensor_reduce(most[:, 0:1], bank[2][:, 64 + 2 * NE:64 + 3 * NE], X, ALU.max).then_inc(route_v.sem, 1),
                      "most")
                done_(nc.vector.tensor_copy(most_i[:, :], most[:, 0:1]).then_inc(route_v.sem, 1), "most_i")
                done_(nc.vector.memset(chosen[:, :, NE, :], 0.0).then_inc(route_v.sem, 1), "idle")
                for n, c in enumerate((pos, sel, wt)):
                    done_(nc.vector.tensor_copy(chosen[:, n, 0:NE, :].rearrange("p e t -> p t e"), c).then_inc(route_v.sem, 1),
                          f"ch{n}")
                for n in range(4):
                    done(eng, nc.vector.memset(moe_sum[:, n // 2, n % 2 * W:(n % 2 + 1) * W], 0.0).then_inc(sum_v.sem, 1),
                         sum_v, f"a{n}", 0)

            def fill_low(part, rep, u):
                eng.wait_ge(fill_a.sem, fill_a.at(f"h{part}", rep))
                k = 4 * part
                done(eng, tt_(x_low[:, u, k:k + 4, :], x_slots[:, :, :], x_high[:, u, k:k + 4, :].bitcast(F32),
                              ALU.subtract).then_inc(fill_v.sem, 1), fill_v, "lb" if part else "la", rep)

            def dispatch_of(e, u, s, rep):
                src = chosen[:, :, e, :] if isinstance(e, int) else \
                    chosen[:, :, bass.ds(e, 1), :].rearrange("p c o t -> p c (o t)")
                done(eng, nc.vector.tensor_copy(choice[:, u, :, :], src).then_inc(s.sem, 1), s, "choice", rep)
                for tt in range(TT):
                    done(eng, ts_(dispatch[:, u, tt, :], iota_f, choice[:, u, 0, tt:tt + 1],
                                  choice[:, u, 1, tt:tt + 1], ALU.is_equal, ALU.mult).then_inc(s.sem, 1),
                         s, "disp" if tt == TT - 1 else f"d{tt}", rep)

            def low(r, u, m):
                c = slice(m % 2 * (KB * W // 2), (m % 2 + 1) * (KB * W // 2))
                eng.wait_ge(high_made, unit_at(r, m))
                tt_(moe_low(u, m // 2)[:, c], moe_slot(u, m // 2)[:, c], w_high[:, m % HIGHS, :].bitcast(F32),
                    ALU.subtract).then_inc(low_made, 1)

            def y_lows(rep):
                for half in range(2):
                    c = slice(half * W, (half + 1) * W)
                    eng.wait_ge(comb_a.sem, comb_a.at(f"yh{half}", rep))
                    done(eng, tt_(y_low[:, c], bank[4 + half][:, :], y_high[:, c].bitcast(F32),
                                  ALU.subtract).then_inc(comb_v.sem, 1), comb_v, f"yl{half}", rep)

            def sums(rep, u):
                for n, b in enumerate((1, 3, 6, 7)):
                    eng.wait_ge(comb_t.sem, comb_t.at(f"c{n}", rep))
                    m = moe_sum[:, n // 2, n % 2 * W:(n % 2 + 1) * W]
                    done(eng, stt(out=m, in0=bank[b][:, :], scalar=choice[:, u, 2, n // 2:n // 2 + 1], in1=m,
                                  op0=ALU.mult, op1=ALU.add).then_inc(sum_v.sem, 1), sum_v, f"a{n}", rep + 1)

            def experts(q):
                if q:
                    done(eng, ts_(chosen[:, 0, 0:NE, :], chosen[:, 0, 0:NE, :], float(-SLOTS), None, ALU.add).then_inc(slot_pos.sem, 1),
                         slot_pos, "pos")
                dispatch_of(0, 0, slot_v, q)
                done(eng, nc.vector.memset(choice[:, 1, :, :], 0.0).then_inc(slot_v.sem, 1), slot_v, "none", q)
                for part in range(2):
                    fill_low(part, q * (NE + 1), 0)
                with eng.Fori(0, NE // PAIR) as g:
                    for u in range(PAIR):
                        r = expert(q, g, u)
                        fill = q * (NE + 1) + g * PAIR + u

                        def product(j):
                            eng.wait_ge(moe_a.sem, moe_a.at(f"s{j}", r))
                            eng.wait_ge(unit_used, used_at(r, 2 * FFN_ORDER.index(("w3", j)) + 1))
                            done(eng, tt_(act_m[:, j % 2, :], act_s[:, j % 2, :], bank[2 + j % 2][:, :], ALU.mult).then_inc(moe_v.sem, 1),
                                 moe_v, f"m{j}", r)

                        def act_lows(j):
                            eng.wait_ge(moe_a.sem, moe_a.at(f"ah{j}", r))
                            done(eng, tt_(act_low[:, j % 2, :], bank[6][:, :], act_high[:, j % 2, :].bitcast(F32),
                                          ALU.subtract).then_inc(moe_v.sem, 1), moe_v, f"al{j}", r)

                        for m in range(UNITS):
                            low(r, u, m)
                            if m == 1:
                                y_lows(fill)
                            if m == 3:
                                sums(fill, (u + 1) % 2)
                            if m >= 8 and m % 6 == 2 and m < UNITS - 1:
                                act_lows(m // 6 - 1)
                            if m == 5:
                                product(0)
                            if m >= 10 and m % 6 == 4:
                                product(m // 6)
                            if m == 12:
                                dispatch_of(g * PAIR + u + 1, (u + 1) % 2, moe_v, r)
                            if m == 6 * GATHER + 5:
                                fill_low(0, fill + 1, (u + 1) % 2)
                            if m == 6 * GATHER + 11:
                                fill_low(1, fill + 1, (u + 1) % 2)
                        act_lows(NJ - 1)
                y_lows(q * (NE + 1) + NE)
                sums(q * (NE + 1) + NE, 1)

            eng.wait_ge(pre_a.sem, pre_a.at("c"))
            mod_part(0, 0)
            norm_x(0)
            mod_part(0, 1)
            eng.wait_ge(pre_t.sem, pre_t.at("rows"))
            done(eng, nc.vector.tensor_copy(params[:, :, :],
                                            bank[3][:, 0:DEPTH * P].rearrange("p (l n) -> p l n", l=DEPTH)[:, :, 0:NROWS]).then_inc(pre_v.sem, 1),
                 pre_v, "params")
            pv = lambda ins, name: done(eng, ins, pre_v, name)
            mod_columns(0, "sh1")
            mod_columns(0, "sc1")
            norm_h(0)
            r = ROWS["lambda"][0]
            lam = params[:, :, r:r + CB]
            sm = lambda i: small[:, i, 0:DEPTH * CB].rearrange("p (l b) -> p l b", l=DEPTH)
            pv(ts_(sm(0), lam, -1.0, None, ALU.mult).then_inc(pre_v.sem, 1), "neg")
            pv(tt_(sm(1), sm(0), lam, ALU.max).then_inc(pre_v.sem, 1), "abs")
            pv(ts_(sm(2), lam, 0.0, None, ALU.min).then_inc(pre_v.sem, 1), "min")
            r = ROWS["gamma"][0]
            g0, g1 = params[:, 0, r:r + CB], params[:, 0, r + CB:r + 2 * CB]
            pv(tt_(small[:, 3, 0:CB], g0, g1, ALU.max).then_inc(pre_v.sem, 1), "gm")
            pv(tt_(small[:, 4, 0:CB], g0, small[:, 3, 0:CB], ALU.subtract).then_inc(pre_v.sem, 1), "gd0")
            pv(tt_(small[:, 4, CB:2 * CB], g1, small[:, 3, 0:CB], ALU.subtract).then_inc(pre_v.sem, 1), "gd1")
            eng.wait_ge(pre_a.sem, pre_a.at("gexp"))
            e0, e1 = small[:, 5, 0:CB], small[:, 5, CB:2 * CB]
            pv(tt_(small[:, 3, 0:CB], e0, e1, ALU.add).then_inc(pre_v.sem, 1), "gs")
            pv(nc.vector.reciprocal(small[:, 3, 0:CB], small[:, 3, 0:CB]).then_inc(pre_v.sem, 1), "gr")
            pv(tt_(e0, e0, small[:, 3, 0:CB], ALU.mult).then_inc(pre_v.sem, 1), "p0")
            pv(tt_(e1, e1, small[:, 3, 0:CB], ALU.mult).then_inc(pre_v.sem, 1), "p1")
            pv(tt_(e1, e0, e1, ALU.add).then_inc(pre_v.sem, 1), "c1")
            pv(tt_(floor_col[:, 0, 0, :], e0, e0, ALU.subtract).then_inc(pre_v.sem, 1), "lb0")
            pv(tt_(floor_col[:, 1, 0, :], e1, e0, ALU.subtract).then_inc(pre_v.sem, 1), "lb1")
            pv(ts_(floor_col[:, :, 1, :], floor_col[:, :, 0, :], -1.0, 1.0, ALU.mult, ALU.add).then_inc(pre_v.sem, 1),
               "lbo")
            pv(ts_(floor_col[:, :, 2, :], floor_col[:, :, 0, :], 1.0, -1.0, ALU.mult, ALU.add).then_inc(pre_v.sem, 1),
               "lbn")
            eng.wait_ge(pre_a.sem, pre_a.at("lln"))
            pv(tt_(sm(2), sm(2), sm(7), ALU.subtract).then_inc(pre_v.sem, 1), "ls")
            pv(ts_(lru_k[:, :, 0, :], sm(2), LRU_C, None, ALU.mult).then_inc(pre_v.sem, 1), "lk0")
            pv(ts_(lru_k[:, :, 1, :], sm(2), -LRU_C, None, ALU.mult).then_inc(pre_v.sem, 1), "lk1")
            eng.wait_ge(s_const, MIX_CONSTS)
            for l in range(DEPTH):
                if l:
                    norm_x(2 * l)
                    norm_h(2 * l)
                mixers(l)
                gate(l, 0, (bank[5], bank[7]))
                residual(2 * l, [bank[n][:, :] for n in range(4)], [[(mix_t, f"wout{n}", l)] for n in range(4)])
                norm_x(2 * l + 1)
                norm_h(2 * l + 1)
                gate(l, 1, (bank[0], bank[1]))
                if l == 0:
                    ffn()
                    residual(1, [bank[4 + n][:, :] for n in range(4)], [[(ffn_u, "q", len(QUARTERS) - 1)]] * 4)
            routing()
            experts(0)
            with eng.If(eng.value_load(most_i[0:1, 0:1], min_val=0, max_val=T) > SLOTS):
                experts(1)
            residual(3, [moe_sum[:, n // 2, n % 2 * W:(n % 2 + 1) * W] for n in range(4)], [[]] * 4)
            eng.wait_ge(end_a.sem, end_a.at("rt"))
            done(eng, nc.vector.reciprocal(norm_s[:, 2, :], norm_s[:, 1, :]).then_inc(end_v.sem, 1), end_v, "rc")
            eng.wait_ge(s_gate, 16 * (2 * DEPTH + 1))
            for tt in range(TT):
                done(eng, stt(out=xn[:, tt, :], in0=x[:, tt, :], scalar=norm_s[:, 2, tt:tt + 1], in1=gate_row[:, :],
                              op0=ALU.mult, op1=ALU.mult).then_inc(end_v.sem, 1), end_v, f"out{tt}")

        @block.scalar
        def _(eng):
            act = nc.scalar.activation

            def mean_square(s, rep):
                for tt in range(TT):
                    done(eng, act(xn[:, tt, :], x[:, tt, :], ACT.Square, accum_out=norm_s[:, 0, tt:tt + 1]).then_inc(s.sem, 1),
                         s, f"sq{tt}", rep)
                done(eng, act(norm_s[:, 1, :], norm_s[:, 0, :], ACT.Sqrt, bias=eps_col[:, 0:1], scale=1.0 / D).then_inc(s.sem, 1),
                     s, "rt", rep)

            def norm(q):
                if q:
                    eng.wait_ge(res_v.sem, res_v.at("r7", q - 1))
                    mean_square(norm_a, q)
                eng.wait_ge(mod_e.sem, mod_e.at("fin", 2 * q + 1))
                for b in (0, 2):
                    eng.wait_ge(norm_t.sem, norm_t.at(f"t{b}", q))
                    for i in range(2):
                        k = 2 * b + i
                        done(eng, act(h_t[:, k, :], bank[4 + b][:, i * T:(i + 1) * T], ACT.Identity,
                                      bias=mod_col[:, 2 * q, k:k + 1], scale=mod_col[:, 2 * q + 1, k:k + 1]).then_inc(norm_a.sem, 1),
                             norm_a, f"h{k}", q)

            def mixers(l):
                def s(ins, name):
                    done(eng, ins, mix_a, name, l)

                def t(i):
                    return tmp[:, i, :]

                eng.wait_ge(mix_t.sem, mix_t.at("dfz", l))
                s(act(t(0), bank[0][:, :], ACT.Sigmoid).then_inc(mix_a.sem, 1), "sig")
                eng.wait_ge(mix_v.sem, mix_v.at("fa", l))
                s(act(t(3), t(3), ACT.Ln).then_inc(mix_a.sem, 1), "lna")
                eng.wait_ge(mix_v.sem, mix_v.at("fb", l))
                s(act(t(4), t(4), ACT.Ln, scale=1.0 / LN_FLOOR).then_inc(mix_a.sem, 1), "lnb")
                eng.wait_ge(mix_v.sem, mix_v.at("kc", l))
                s(act(t(2), t(2), ACT.Ln).then_inc(mix_a.sem, 1), "lnk")
                eng.wait_ge(mix_v.sem, mix_v.at("b1", l))
                s(act(t(3), t(1), ACT.Exp).then_inc(mix_a.sem, 1), "eb")
                ends = t(1).rearrange("p (n s) -> p n s", s=C)[:, :, C - 1]
                s(act(small[:, 8:12, :].rearrange("p a b -> p (a b)"), ends, ACT.Exp).then_inc(mix_a.sem, 1), "ea")
                eng.wait_ge(mix_v.sem, mix_v.at("kd", l))
                s(act(t(4), t(4), ACT.Exp).then_inc(mix_a.sem, 1), "kh")

                def exps(i):
                    for r in range(C):
                        rep = (l * CB + i) * C + r
                        eng.wait_ge(tri_d.sem, tri_d.at("d", rep))
                        done(eng, act(tri[:, r, :, 0:r + 1], tri[:, r, :, 0:r + 1], ACT.Exp).then_inc(tri_e.sem, 1),
                             tri_e, "e", rep)

                exps(0)
                eng.wait_ge(mix_t.sem, mix_t.at("dq", l))
                s(act(t(0), bank[2][:, :], ACT.Silu).then_inc(mix_a.sem, 1), "q")
                eng.wait_ge(mix_t.sem, mix_t.at("kt", l))
                s(act(t(5), bank[4][:, :], ACT.Copy).then_inc(mix_a.sem, 1), "kt")
                eng.wait_ge(mix_t.sem, mix_t.at("px", l))
                if l:
                    eng.wait_ge(mix_v.sem, mix_v.at("xc1", l - 1))
                s(act(x_pad[:, :, CONV - 1:], rows2(bank[0][:, :]), ACT.Copy).then_inc(mix_a.sem, 1), "xp")
                eng.wait_ge(mix_t.sem, mix_t.at("pg", l))
                s(act(t(12), bank[1][:, :], ACT.Gelu_apprx_tanh).then_inc(mix_a.sem, 1), "gate_c")
                eng.wait_ge(mix_t.sem, mix_t.at("pv", l))
                for tt in range(TT):
                    c = slice(tt * G, (tt + 1) * G)
                    s(act(t(4)[:, c], bank[2][:, c], ACT.Gelu_apprx_tanh, accum_out=small[:, 0, tt:tt + 1]).then_inc(mix_a.sem, 1),
                      f"gv{tt}")
                exps(1)
                for name, b, dst, bias in (("r", 4, 8, "lru_ba"), ("i", 5, 9, "lru_bx")):
                    eng.wait_ge(mix_t.sem, mix_t.at("wa" if name == "r" else "wx", l))
                    for i in range(CB):
                        c = slice(i * T, (i + 1) * T)
                        s(act(t(dst)[:, c], bank[b][:, c], ACT.Sigmoid, bias=par(bias, l, i)).then_inc(mix_a.sem, 1),
                          f"{name}{i}")
                for i in range(CB):
                    c = slice(i * T, (i + 1) * T)
                    s(act(t(10)[:, c], t(8)[:, c], ACT.Exp, scale=lru_k[:, l, 0, i:i + 1]).then_inc(mix_a.sem, 1),
                      f"a{i}")
                for i in range(CB):
                    c = slice(i * T, (i + 1) * T)
                    s(act(t(8)[:, c], t(8)[:, c], ACT.Tanh, scale=lru_k[:, l, 1, i:i + 1]).then_inc(mix_a.sem, 1),
                      f"th{i}")
                eng.wait_ge(mix_v.sem, mix_v.at("m0", l))
                s(act(t(11), t(11), ACT.Sqrt).then_inc(mix_a.sem, 1), "sm")
                eng.wait_ge(mix_t.sem, mix_t.at("dg", l))
                s(act(t(13), bank[0][:, :], ACT.Silu).then_inc(mix_a.sem, 1), "gate_d")
                eng.wait_ge(mix_v.sem, mix_v.at("yc_raw", l))
                s(act(t(8), t(12), ACT.Square).then_inc(mix_a.sem, 1), "sqc")
                eng.wait_ge(mix_v.sem, mix_v.at("vc1", l))
                for tt in range(TT):
                    c = slice(tt * G, (tt + 1) * G)
                    s(act(t(5)[:, c], t(4)[:, c], ACT.Square, accum_out=small[:, 2, tt:tt + 1]).then_inc(mix_a.sem, 1),
                      f"sv{tt}")
                s(act(small[:, 3, 0:2], small[:, 2, 0:2], ACT.Sqrt, bias=eps_col[:, 0:1], scale=1.0 / G).then_inc(mix_a.sem, 1),
                  "rv")
                eng.wait_ge(mix_t.sem, mix_t.at("pu", l))
                s(act(t(7), bank[1][:, :], ACT.Gelu_apprx_tanh).then_inc(mix_a.sem, 1), "gu")
                eng.wait_ge(mix_t.sem, mix_t.at("pa", l))
                s(act(t(11), bank[2][:, :], ACT.Copy).then_inc(mix_a.sem, 1), "pa")
                eng.wait_ge(mix_t.sem, mix_t.at("o", l))
                s(act(t(2), bank[3][:, :], ACT.Square).then_inc(mix_a.sem, 1), "sqd")
                eng.wait_ge(mix_t.sem, mix_t.at("ssd", l))
                s(act(t(5), bank[7][:, :], ACT.Sqrt, bias=eps_col[:, 0:1], scale=1.0 / HD).then_inc(mix_a.sem, 1),
                  "rtd")
                eng.wait_ge(mix_t.sem, mix_t.at("ssc", l))
                s(act(t(9)[:, 0:T], bank[5][:, 0:T], ACT.Sqrt, bias=eps_col[:, 0:1], scale=1.0 / G).then_inc(mix_a.sem, 1),
                  "rtc")
                eng.wait_ge(mix_t.sem, mix_t.at("aband", l))
                s(act(t(6), bank[6][:, :], ACT.Copy).then_inc(mix_a.sem, 1), "pd")
                eng.wait_ge(mix_v.sem, mix_v.at("yb_raw", l))
                s(act(t(4), t(7), ACT.Square).then_inc(mix_a.sem, 1), "sqb")
                eng.wait_ge(mix_t.sem, mix_t.at("ssb", l))
                s(act(t(10)[:, 0:T], bank[7][:, 0:T], ACT.Sqrt, bias=eps_col[:, 0:1], scale=1.0 / G).then_inc(mix_a.sem, 1),
                  "rtb")
                eng.wait_ge(mix_t.sem, mix_t.at("apool", l))
                for i in range(CB):
                    c = slice(i * T, (i + 1) * T)
                    s(act(t(3)[:, c], bank[4][:, c], ACT.Copy, scale=par("pool_scale", l, i)).then_inc(mix_a.sem, 1),
                      f"ps{i}")
                s(act(t(1), t(3), ACT.Square).then_inc(mix_a.sem, 1), "sqa")
                eng.wait_ge(mix_t.sem, mix_t.at("ssa", l))
                eng.wait_ge(mix_v.sem, mix_v.at("od", l))
                eng.wait_ge(mix_v.sem, mix_v.at("yd1", l))
                s(act(t(2)[:, 0:T], bank[5][:, 0:T], ACT.Sqrt, bias=eps_col[:, 0:1], scale=1.0 / G).then_inc(mix_a.sem, 1),
                  "rta")

            def ffn():
                eng.wait_ge(norm_v.sem, norm_v.at("h7", 1))
                for half in range(2):
                    k = slice(half * KB // 2, (half + 1) * KB // 2)
                    done(eng, act(h_high[:, k, :], h_t[:, k, :], ACT.Copy).then_inc(part_a.sem, 1),
                         part_a, f"h{half}")
                for m, (kind, j, hb) in enumerate(QUARTERS):
                    if hb == 0 or kind != "w2" and hb == 2:
                        arrived(eng, ("ffn", kind, j))
                    if m >= HIGHS:
                        eng.wait_ge(ffn_u.sem, ffn_u.at("q", m - HIGHS))
                    mark(act(quarter_high(m), quarter(ring, QUARTERS[m]), ACT.Copy).then_inc(ffn_h.sem, 1),
                         ffn_h, "q")
                    if m >= HIGHS and QUARTERS[m - HIGHS][0] == "w1" and QUARTERS[m - HIGHS][2] % 2 == 1:
                        _, jj, hh = QUARTERS[m - HIGHS]
                        i = hh // 2
                        if jj:
                            eng.wait_ge(ffn_v.sem, ffn_v.at(f"a{i}", jj - 1))
                        done(eng, act(tmp[:, i, :], bank[i][:, :], ACT.Silu).then_inc(ffn_a.sem, 1),
                             ffn_a, f"s{i}", jj)
                    if (kind, hb) == ("w1", 3) and j:
                        at_highs(j - 1)
                    if (kind, j, hb) == ("w2", NJ - 1, HIGHS - 1):
                        at_highs(j)

            def at_highs(j):
                eng.wait_ge(ffn_v.sem, ffn_v.at("a1", j))
                if j:
                    eng.wait_ge(ffn_u.sem, ffn_u.at("q", QUARTER["w2", j - 1, 3]))
                a0 = 2 + 2 * (j % 2)
                done(eng, act(at_high[:, :, :], tmp[:, a0:a0 + 2, :], ACT.Copy).then_inc(part_a.sem, 1),
                     part_a, f"a{j}")

            def fill_half(b, part, e, rep, s, name, u):
                eng.wait_ge(s.sem, s.at(name, e))
                if part:
                    eng.wait_ge(fill_v.sem, fill_v.at("la", rep))
                for k in range(4):
                    kb = 4 * part + k
                    done(eng, act(x_slots[:, k, :], b[:, k * P:(k + 1) * P], ACT.Identity,
                                  bias=mod_col[:, 6, kb:kb + 1], scale=mod_col[:, 7, kb:kb + 1]).then_inc(fill_a.sem, 1),
                         fill_a, f"x{kb}", rep)
                k = 4 * part
                done(eng, act(x_high[:, u, k:k + 4, :], x_slots[:, :, :], ACT.Copy).then_inc(fill_a.sem, 1),
                     fill_a, f"h{part}", rep)

            def high(q, g, u, m):
                r = expert(q, g, u)
                if m % 2 == 0:
                    moe_arrived(eng, q, g, u, m // 2)
                eng.wait_ge(unit_used, used_at(r, m - HIGHS))
                c = slice(m % 2 * (KB * W // 2), (m % 2 + 1) * (KB * W // 2))
                act(w_high[:, m % HIGHS, :], moe_slot(u, m // 2)[:, c], ACT.Copy).then_inc(high_made, 1)

            def y_highs(rep):
                for half in range(2):
                    done(eng, act(y_high[:, half * W:(half + 1) * W], bank[4 + half][:, :], ACT.Copy).then_inc(comb_a.sem, 1),
                         comb_a, f"yh{half}", rep)

            def experts(q):
                eng.wait_ge(slot_v.sem, slot_v.at("disp", q))
                done(eng, act(spread[:, :], dispatch[:, 0, :, :].rearrange("p t n -> p (t n)"), ACT.Copy).then_inc(slot_a.sem, 1),
                     slot_a, "spread", q)
                for part in range(2):
                    fill_half(bank[4 + part], part, q, q * (NE + 1), slot_t, f"g{part}", 0)
                with eng.Fori(0, NE // PAIR) as g:
                    for u in range(PAIR):
                        r = expert(q, g, u)
                        fill = q * (NE + 1) + g * PAIR + u

                        def act_highs(j):
                            eng.wait_ge(moe_t.sem, moe_t.at(f"t{j}", r))
                            done(eng, act(act_high[:, j % 2, :], bank[6][:, :], ACT.Copy).then_inc(moe_a.sem, 1),
                                 moe_a, f"ah{j}", r)

                        for m in range(UNITS):
                            high(q, g, u, m)
                            if m == 1:
                                eng.wait_ge(unit_used, used_at(r, -1))
                                y_highs(fill)
                            if m == 4 or m >= 8 and m % 6 == 2:
                                j = m // 6
                                eng.wait_ge(unit_used, used_at(r, 2 * FFN_ORDER.index(("w1", j)) + 1))
                                done(eng, act(act_s[:, j % 2, :], bank[j % 2][:, :], ACT.Silu).then_inc(moe_a.sem, 1),
                                     moe_a, f"s{j}", r)
                                if j:
                                    act_highs(j - 1)
                            if m == 10:
                                eng.wait_ge(moe_t.sem, moe_t.at("spread", r))
                                done(eng, act(spread[:, :], bank[7][:, 0:T], ACT.Copy).then_inc(moe_a.sem, 1),
                                     moe_a, "spread", r)
                            if m == 6 * GATHER + 4:
                                fill_half(bank[7], 0, r, fill + 1, moe_t, "ga", (u + 1) % 2)
                            if m == 6 * GATHER + 10:
                                fill_half(bank[7], 1, r, fill + 1, moe_t, "gb", (u + 1) % 2)
                        act_highs(NJ - 1)
                eng.wait_ge(unit_used, used_at(expert(q, NE // PAIR, -1), UNITS - 1))
                y_highs(q * (NE + 1) + NE)

            def layer_constants():
                eng.wait_ge(pre_v.sem, pre_v.at("gd1"))
                done(eng, act(small[:, 5, 0:2 * CB], small[:, 4, 0:2 * CB], ACT.Exp).then_inc(pre_a.sem, 1),
                     pre_a, "gexp")
                done(eng, act(small[:, 6, 0:DEPTH * CB], small[:, 1, 0:DEPTH * CB], ACT.Exp, scale=-1.0).then_inc(pre_a.sem, 1),
                     pre_a, "lexp")
                done(eng, act(small[:, 7, 0:DEPTH * CB], small[:, 6, 0:DEPTH * CB], ACT.Ln, bias=1.0).then_inc(pre_a.sem, 1),
                     pre_a, "lln")

            eng.dma_start(c_row[:, :], a["c"].rearrange("o (k p) -> (o k) p", p=P)).then_inc(s_c, 16)
            eng.dma_start(x[:, :, :], a["x"][0].rearrange("(t p) d -> p t d", p=P)).then_inc(s_x, 16)
            eng.wait_ge(pre_t.sem, pre_t.at("c"))
            done(eng, act(c_act[:, :], bank[2][:, 0:KB], ACT.Silu).then_inc(pre_a.sem, 1), pre_a, "c")
            n = 0
            for first in ("sh1", "sh2"):
                r, k = ROWS["b_" + first][0], 2 * KB
                col = MOD_COL[first] * D
                eng.dma_start(prow[r:r + k, :, :], a["b_mod"][:, col:col + 2 * D].rearrange("l (r p) -> r l p", p=P))\
                   .then_inc(s_rows, 16)
                n += 1
            for name, src in (("norm_mix", a["norm_mix"]), ("norm_ffn", a["norm_ffn"]),
                              ("pool_scale", a["pool_scale"]), ("pool_out", a["pool_out_norm"]),
                              ("sgu_out", a["sgu_out_norm"]), ("conv_b", a["conv_b"]), ("lru_ba", a["lru_ba"]),
                              ("lru_bx", a["lru_bx"]), ("lambda", a["lru_lambda"]), ("lru_out", a["lru_out_norm"]),
                              ("hgrn_out", a["hgrn_out_norm"])):
                r, k = ROWS[name]
                eng.dma_start(prow[r:r + k, :, :], src.rearrange("l (r p) -> r l p", p=P)).then_inc(s_rows, 16)
                n += 1
            for l in range(DEPTH):
                r, k = ROWS["conv_w"]
                eng.dma_start(prow[r:r + k, l, :], a["conv_w"][l].rearrange("k (r p) -> (k r) p", p=P))\
                   .then_inc(s_rows, 16)
                r, k = ROWS["gamma"]
                eng.dma_start(prow[r:r + k, l, :], a["hgrn_gamma"].rearrange("l (r p) -> (l r) p", p=P))\
                   .then_inc(s_rows, 16)
                n += 2
            assert n == N_ROW_LOADS
            eng.wait_ge(s_const, FIRST_CONSTS)
            eng.wait_ge(s_x, 16)
            mean_square(norm_a, 0)
            eng.wait_ge(s_const, MIX_CONSTS)
            for l in range(DEPTH):
                norm(2 * l)
                if l == 0:
                    layer_constants()
                mixers(l)
                norm(2 * l + 1)
                if l == 0:
                    ffn()
            eng.wait_ge(route_v.sem, route_v.at("diff"))
            done(eng, act(route_c[:, 5, :, :], route_c[:, 3, :, :], ACT.Exp).then_inc(route_a.sem, 1), route_a, "exp")
            experts(0)
            eng.wait_ge(route_v.sem, route_v.at("most_i"))
            with eng.If(eng.value_load(most_i[0:1, 0:1], min_val=0, max_val=T) > SLOTS):
                experts(1)
            eng.wait_ge(res_v.sem, res_v.at("r7", 3))
            mean_square(end_a, 0)


_INS = ['x', 'c', 'w_mod', 'b_mod', 'norm_mix', 'norm_ffn', 'norm_final', 'w_in', 'w_out', 'pool_w', 'pool_scale',
        'pool_out_norm', 'sgu_ws', 'sgu_b', 'sgu_out_norm', 'conv_w', 'conv_b', 'lru_wa', 'lru_ba', 'lru_wx', 'lru_bx',
        'lru_lambda', 'lru_out_norm', 'hgrn_gamma', 'hgrn_out_norm', 'ffn_w1', 'ffn_w3', 'ffn_w2', 'router_w',
        'router_b', 'moe_w1', 'moe_w3', 'moe_w2']
_OUTS = [((1, T, D), 'float32')]


def kernel(**inputs):
    import numpy as _np
    import concourse.bacc as _bacc
    from concourse import mybir as _mybir
    from concourse.bass_utils import run_bass_kernel_spmd as _run

    nc = _bacc.Bacc("TRN2", target_bir_lowering=False, num_devices=1)
    arrays, args = {}, {}
    for name in _INS:
        v = _np.ascontiguousarray(inputs[name])
        arrays[f"in_{name}_dram"] = v
        args[name] = nc.dram_tensor(f"in_{name}_dram", v.shape, _mybir.dt.from_np(v.dtype), kind="ExternalInput").ap()
    out = nc.dram_tensor("out_0_dram", _OUTS[0][0], _mybir.dt.float32, kind="ExternalOutput").ap()
    hybrid_stream_block(nc, args, out)
    r = _run(nc, [arrays], core_ids=[0])
    return r.results[0]["out_0_dram"]
```
